# Optimizing a Trainium2 kernel written in Bass

```python
import jax, jax.numpy as jnp
from jax import lax
import numpy as np

D_MODEL = 1024
BATCH = 1
SEQ = 512
DEPTH = 4
DEC_BATCH = 8
DEC_SEQ = 8
PAST_LEN = 1024
PAGE_SIZE = 128

N_MIXERS = 3
N_A_LAYERS = (DEPTH + 2) // 3
N_B_LAYERS = (DEPTH + 1) // 3
N_C_LAYERS = DEPTH // 3
A_HEAD = 64
A_HEADS = D_MODEL // A_HEAD
A_DECAY_LORA = 64
A_ICLR_LORA = 64
A_GATE_LORA = 128
A_GN_EPS = 64e-5
A_N_MIX = 6
B_HEAD = 64
B_HEADS = D_MODEL // B_HEAD
Q_BLOCK = 128
C_WIDTH = 3
D_FF = 2816
FFN_WIDTH = 3
RMS_EPS = 1e-6
POOL_NUM = 5
POOL_DEN = 4

kernel_name = "hybrid_rwkv7_fox_shortconv_convffn_step"

def rmsnorm(x, g):
    xf = x.astype(jnp.float32)
    y = xf * lax.rsqrt(jnp.mean(xf * xf, axis=-1, keepdims=True) + RMS_EPS)
    return (y * g.astype(jnp.float32)).astype(x.dtype)

def causal_dwconv(u, buf, w):
    K = w.shape[0]
    T = u.shape[1]
    full = jnp.concatenate([buf.astype(u.dtype), u], axis=1)
    y = full[:, 0:T] * w[0]
    for j in range(1, K):
        y = y + full[:, j:j + T] * w[j]
    return y, full[:, full.shape[1] - (K - 1):]

def _wkv_step(S, inp):
    r, k, v, w, kk, b = inp
    sa = jnp.einsum('bhij,bhj->bhi', S, -kk)
    S = S * w[:, :, None, :] + sa[..., None] * b[:, :, None, :] + v[..., None] * k[:, :, None, :]
    return S, jnp.einsum('bhij,bhj->bhi', S, r)

def rwkv7_mix(xn, shift, S0, mu, w_rkv, w0, w1, w2, a0, a1, a2, g1, g2, k_k, k_a, r_k, lnx_g, lnx_b, w_out):
    f32 = jnp.float32
    Bn, T, D = xn.shape
    x_prev = jnp.concatenate([shift[:, None].astype(xn.dtype), xn[:, :-1]], axis=1)
    dx = x_prev - xn
    mix = lambda c: xn + dx * mu[c]
    r = mix(0) @ w_rkv[0]
    k = mix(2) @ w_rkv[1]
    v = mix(3) @ w_rkv[2]
    w_log = -jax.nn.softplus(-(w0 + jnp.tanh(mix(1) @ w1) @ w2).astype(f32)) - 0.5
    decay = jnp.exp(-jnp.exp(w_log))
    iclr = jax.nn.sigmoid((a0 + (mix(4) @ a1) @ a2).astype(f32))
    g = jax.nn.sigmoid(mix(5) @ g1) @ g2
    heads = lambda z: z.reshape(Bn, T, A_HEADS, A_HEAD)
    kk = heads((k * k_k).astype(f32))
    kk = kk / jnp.maximum(jnp.linalg.norm(kk, axis=-1, keepdims=True), 1e-12)
    k_h = heads(k.astype(f32) * (1.0 + (iclr - 1.0) * k_a.astype(f32)))
    r_h = heads(r.astype(f32))
    v_h = heads(v.astype(f32))
    b_h = kk * heads(iclr)
    xs = tuple(jnp.moveaxis(z, 1, 0) for z in (r_h, k_h, v_h, heads(decay), kk, b_h))
    S_T, o = lax.scan(_wkv_step, S0.astype(f32), xs)
    o = jnp.moveaxis(o, 0, 1)
    mean = jnp.mean(o, axis=-1, keepdims=True)
    var = jnp.mean(jnp.square(o - mean), axis=-1, keepdims=True)
    o = ((o - mean) * lax.rsqrt(var + A_GN_EPS)).reshape(Bn, T, D) * lnx_g.astype(f32) + lnx_b.astype(f32)
    bonus = jnp.sum(r_h * k_h * r_k.astype(f32), axis=-1, keepdims=True) * v_h
    o = (o + bonus.reshape(Bn, T, D)).astype(xn.dtype) * g
    return o @ w_out, xn[:, -1], S_T.astype(S0.dtype)

def fox_project(xn, w_in, f_bias, q_g, k_g):
    Bn, T, D = xn.shape
    proj = xn @ w_in
    q = rmsnorm(proj[..., 0:D].reshape(Bn, T, B_HEADS, B_HEAD), q_g)
    k = rmsnorm(proj[..., D:2 * D].reshape(Bn, T, B_HEADS, B_HEAD), k_g)
    v = proj[..., 2 * D:3 * D].reshape(Bn, T, B_HEADS, B_HEAD)
    g = proj[..., 3 * D:4 * D]
    logf = jax.nn.log_sigmoid(proj[..., 4 * D:].astype(jnp.float32) + f_bias.astype(jnp.float32))
    return q, k, v, g, logf

def fox_attend(q, k, v, Fq, Fk, q_pos, k_pos):
    Bn, Tq, H, HD = q.shape
    QB = min(Q_BLOCK, Tq)
    nb = Tq // QB
    qb = q.reshape(Bn, nb, QB, H, HD).transpose(1, 0, 2, 3, 4)
    Fqb = Fq.reshape(Bn, nb, QB, H).transpose(1, 0, 3, 2)
    pb = q_pos.reshape(nb, QB)
    Fk_t = Fk.transpose(0, 2, 1)[:, :, None, :]
    scale = HD ** -0.5

    def block(args):
        qi, Fi, pi = args
        s = jnp.einsum('bqhd,bkhd->bhqk', qi, k).astype(jnp.float32) * scale
        s = s + Fi[..., None] - Fk_t
        mask = k_pos[None, :] <= pi[:, None]
        s = jnp.where(mask, s, -jnp.inf)
        p = jax.nn.softmax(s, axis=-1).astype(v.dtype)
        return jnp.einsum('bhqk,bkhd->bqhd', p, v)

    o = lax.map(block, (qb, Fqb, pb))
    return o.transpose(1, 0, 2, 3, 4).reshape(Bn, Tq, H * HD)

def conv_mix(xn, buf, w_in, conv_w, w_out):
    D = xn.shape[-1]
    proj = xn @ w_in
    gb, gc, h = proj[..., 0:D], proj[..., D:2 * D], proj[..., 2 * D:3 * D]
    z, new_buf = causal_dwconv(gc * h, buf, conv_w)
    return (gb * z) @ w_out, new_buf

def conv_ffn(xn, buf, w_up, conv_w, conv_b, w_down):
    u = xn @ w_up
    gate, val = u[..., 0:D_FF], u[..., D_FF:]
    gate_c, new_buf = causal_dwconv(gate, buf, conv_w)
    h = jax.nn.silu(gate_c + conv_b) * val
    return h @ w_down, new_buf

def setup_inputs(seed: int = 0) -> dict:
    key = jax.random.key(seed)
    ks = iter(jax.random.split(key, 64))
    nrm = lambda shape, s=1.0: jax.random.normal(next(ks), shape, jnp.float32) * s
    n_pages = PAST_LEN // PAGE_SIZE
    n_pool = DEC_BATCH * n_pages * POOL_NUM // POOL_DEN
    D = D_MODEL
    inp = {}
    inp['x_prompt'] = nrm((BATCH, SEQ, D))
    inp['x_sample'] = nrm((DEC_BATCH, DEC_SEQ, D))
    inp['state_wkv'] = nrm((N_A_LAYERS, DEC_BATCH, A_HEADS, A_HEAD, A_HEAD), 0.5)
    inp['state_shift'] = nrm((N_A_LAYERS, DEC_BATCH, D))
    inp['cache_k'] = nrm((N_B_LAYERS, n_pool, PAGE_SIZE, B_HEADS, B_HEAD))
    inp['cache_v'] = nrm((N_B_LAYERS, n_pool, PAGE_SIZE, B_HEADS, B_HEAD))
    inp['cache_logf'] = jax.nn.log_sigmoid(3.0 + nrm((N_B_LAYERS, n_pool, PAGE_SIZE, B_HEADS)))
    inp['state_conv_mix'] = nrm((N_C_LAYERS, DEC_BATCH, C_WIDTH - 1, D))
    inp['state_conv_ffn'] = nrm((DEPTH, DEC_BATCH, FFN_WIDTH - 1, D_FF))
    perm = jax.random.permutation(next(ks), n_pool)[:DEC_BATCH * n_pages]
    inp['page_table'] = perm.reshape(DEC_BATCH, n_pages).astype(jnp.int32)
    inp['norm_mix_g'] = 1.0 + nrm((DEPTH, D), 0.01)
    inp['norm_ffn_g'] = 1.0 + nrm((DEPTH, D), 0.01)
    NA = N_A_LAYERS
    inp['a_mu'] = jax.random.uniform(next(ks), (NA, A_N_MIX, D), jnp.float32)
    inp['a_w_rkv'] = nrm((NA, 3, D, D), D ** -0.5)
    inp['a_w0'] = -1.0 + nrm((NA, D), 0.3)
    inp['a_w1'] = nrm((NA, D, A_DECAY_LORA), D ** -0.5)
    inp['a_w2'] = nrm((NA, A_DECAY_LORA, D), A_DECAY_LORA ** -0.5)
    inp['a_a0'] = nrm((NA, D), 0.1)
    inp['a_a1'] = nrm((NA, D, A_ICLR_LORA), D ** -0.5)
    inp['a_a2'] = nrm((NA, A_ICLR_LORA, D), A_ICLR_LORA ** -0.5)
    inp['a_g1'] = nrm((NA, D, A_GATE_LORA), D ** -0.5)
    inp['a_g2'] = nrm((NA, A_GATE_LORA, D), A_GATE_LORA ** -0.5)
    inp['a_k_k'] = 1.0 + nrm((NA, D), 0.1)
    inp['a_k_a'] = 1.0 + nrm((NA, D), 0.1)
    inp['a_r_k'] = nrm((NA, A_HEADS, A_HEAD), 0.1)
    inp['a_lnx_g'] = 1.0 + nrm((NA, D), 0.01)
    inp['a_lnx_b'] = nrm((NA, D), 0.01)
    inp['a_w_out'] = nrm((NA, D, D), D ** -0.5)
    NB = N_B_LAYERS
    inp['b_w_in'] = nrm((NB, D, 4 * D + B_HEADS), D ** -0.5)
    inp['b_f_bias'] = jnp.linspace(1.0, 5.0, B_HEADS, dtype=jnp.float32)[None] + nrm((NB, B_HEADS), 0.1)
    inp['b_q_norm_g'] = 1.0 + nrm((NB, B_HEAD), 0.01)
    inp['b_k_norm_g'] = 1.0 + nrm((NB, B_HEAD), 0.01)
    inp['b_w_out'] = nrm((NB, D, D), D ** -0.5)
    NC = N_C_LAYERS
    inp['c_w_in'] = nrm((NC, D, 3 * D), D ** -0.5)
    inp['c_conv_w'] = nrm((NC, C_WIDTH, D), C_WIDTH ** -0.5)
    inp['c_w_out'] = nrm((NC, D, D), D ** -0.5)
    inp['f_w_up'] = nrm((DEPTH, D, 2 * D_FF), D ** -0.5)
    inp['f_conv_w'] = nrm((DEPTH, FFN_WIDTH, D_FF), FFN_WIDTH ** -0.5)
    inp['f_conv_b'] = nrm((DEPTH, D_FF), 0.01)
    inp['f_w_down'] = nrm((DEPTH, D_FF, D), D_FF ** -0.5)
    return inp

def reference(x_prompt, x_sample, state_wkv, state_shift, cache_k, cache_v, cache_logf, state_conv_mix, state_conv_ffn, page_table,
              norm_mix_g, norm_ffn_g,
              a_mu, a_w_rkv, a_w0, a_w1, a_w2, a_a0, a_a1, a_a2, a_g1, a_g2, a_k_k, a_k_a, a_r_k, a_lnx_g, a_lnx_b, a_w_out,
              b_w_in, b_f_bias, b_q_norm_g, b_k_norm_g, b_w_out,
              c_w_in, c_conv_w, c_w_out,
              f_w_up, f_conv_w, f_conv_b, f_w_down):
    BP, TP, D = x_prompt.shape
    DB, TS, _ = x_sample.shape
    P = page_table.shape[1] * cache_k.shape[2]
    xp, xs = x_prompt, x_sample
    wkv_p, shift_p, wkv_s, shift_s = [], [], [], []
    k_p, v_p, lf_p, k_s, v_s, lf_s = [], [], [], [], [], []
    cm_p, cm_s, cf_p, cf_s = [], [], [], []
    for i in range(DEPTH):
        kind, j = i % N_MIXERS, i // N_MIXERS
        hp = rmsnorm(xp, norm_mix_g[i])
        hs = rmsnorm(xs, norm_mix_g[i])
        if kind == 0:
            pa = (a_mu[j], a_w_rkv[j], a_w0[j], a_w1[j], a_w2[j], a_a0[j], a_a1[j], a_a2[j], a_g1[j], a_g2[j],
                  a_k_k[j], a_k_a[j], a_r_k[j], a_lnx_g[j], a_lnx_b[j], a_w_out[j])
            zero_shift = jnp.zeros((BP, D), xp.dtype)
            zero_S = jnp.zeros((BP, A_HEADS, A_HEAD, A_HEAD), jnp.float32)
            yp, sh1, S1 = rwkv7_mix(hp, zero_shift, zero_S, *pa)
            ys, sh2, S2 = rwkv7_mix(hs, state_shift[j], state_wkv[j], *pa)
            wkv_p.append(S1); shift_p.append(sh1); wkv_s.append(S2); shift_s.append(sh2)
        elif kind == 1:
            pb = (b_w_in[j], b_f_bias[j], b_q_norm_g[j], b_k_norm_g[j])
            q, k, v, g, logf = fox_project(hp, *pb)
            F = jnp.cumsum(logf, axis=1)
            pos = jnp.arange(TP, dtype=jnp.int32)
            o = fox_attend(q, k, v, F, F, pos, pos)
            yp = (o * jax.nn.sigmoid(g)) @ b_w_out[j]
            k_p.append(k); v_p.append(v); lf_p.append(logf.astype(xp.dtype))
            q2, k2, v2, g2, logf2 = fox_project(hs, *pb)
            k_past = cache_k[j][page_table].reshape(DB, P, B_HEADS, B_HEAD).astype(k2.dtype)
            v_past = cache_v[j][page_table].reshape(DB, P, B_HEADS, B_HEAD).astype(v2.dtype)
            lf_past = cache_logf[j][page_table].reshape(DB, P, B_HEADS).astype(jnp.float32)
            F2 = jnp.cumsum(jnp.concatenate([lf_past, logf2], axis=1), axis=1)
            k_all = jnp.concatenate([k_past, k2], axis=1)
            v_all = jnp.concatenate([v_past, v2], axis=1)
            q_pos = P + jnp.arange(TS, dtype=jnp.int32)
            k_pos = jnp.arange(P + TS, dtype=jnp.int32)
            o2 = fox_attend(q2, k_all, v_all, F2[:, P:], F2, q_pos, k_pos)
            ys = (o2 * jax.nn.sigmoid(g2)) @ b_w_out[j]
            k_s.append(k2); v_s.append(v2); lf_s.append(logf2.astype(xs.dtype))
        else:
            zero_buf = jnp.zeros((BP, C_WIDTH - 1, D), xp.dtype)
            yp, b1 = conv_mix(hp, zero_buf, c_w_in[j], c_conv_w[j], c_w_out[j])
            ys, b2 = conv_mix(hs, state_conv_mix[j], c_w_in[j], c_conv_w[j], c_w_out[j])
            cm_p.append(b1); cm_s.append(b2)
        xp = xp + yp
        xs = xs + ys
        zero_fbuf = jnp.zeros((BP, FFN_WIDTH - 1, D_FF), xp.dtype)
        fp, fb1 = conv_ffn(rmsnorm(xp, norm_ffn_g[i]), zero_fbuf, f_w_up[i], f_conv_w[i], f_conv_b[i], f_w_down[i])
        fs, fb2 = conv_ffn(rmsnorm(xs, norm_ffn_g[i]), state_conv_ffn[i], f_w_up[i], f_conv_w[i], f_conv_b[i], f_w_down[i])
        xp = xp + fp
        xs = xs + fs
        cf_p.append(fb1); cf_s.append(fb2)
    return (xp, xs,
            jnp.stack(wkv_p), jnp.stack(shift_p), jnp.stack(wkv_s), jnp.stack(shift_s),
            jnp.stack(k_p), jnp.stack(v_p), jnp.stack(lf_p), jnp.stack(k_s), jnp.stack(v_s), jnp.stack(lf_s),
            jnp.stack(cm_p), jnp.stack(cm_s), jnp.stack(cf_p), jnp.stack(cf_s))


_drawn_inputs = setup_inputs


def setup_inputs(seed=0):
    import zlib

    import numpy as np

    out = dict(_drawn_inputs(seed))
    spreads = {}
    factors = {'norm_ffn_g': 3.414,
     'a_lnx_g': 5.689,
     'a_lnx_b': 6.006,
     'b_q_norm_g': 147.441,
     'b_k_norm_g': 156.968,
     'f_conv_b': 4.973,
     'cache_logf': 27.936}
    for name, (base, spread) in spreads.items():
        noise = np.random.default_rng([zlib.crc32(name.encode()), seed]).standard_normal(out[name].shape)
        drawn = base * np.exp(spread * noise) if base else spread * noise
        out[name] = __import__('jax').numpy.asarray(drawn.astype(out[name].dtype))
    for name, factor in factors.items():
        out[name] = (out[name] * factor).astype(out[name].dtype)
    return out
```

```python
from contextlib import ExitStack

import numpy as np

import concourse.bass as bass
from concourse import mybir

F32 = mybir.dt.float32
F32R = mybir.dt.float32r
I32 = mybir.dt.int32
ALU = mybir.AluOpType
ACT = mybir.ActivationFunctionType
AX = mybir.AxisListType

P = 128
D = 1024
KD = D // P
TP = 512
NS, TS = 8, 8
TSN = NS * TS
T = TP + TSN
HT = T // 2
FF = 2816
KF = FF // P
DEPTH = 4
RMS_EPS = 1e-6
CH = 8
RAWS, SPL = 4, 2
GW = 2 + TP + NS * (2 + TS)
GS = 2 + TP


def down_chunks():
    return [(k, min(CH, KF - k)) for k in range(0, KF, CH)]


KINDS = {"a": 27 + 8, "b": 33 + 8, "c": 24 + 8}
FFN_CHUNKS = 2 * KF + KD * len(down_chunks())
MIXERS = [("a", 0), ("b", 0), ("c", 0), ("a", 1)]


class Map:

    def __init__(self, at):
        self.at = at

    def take(self, n):
        at = self.at
        self.at += (n + 31) // 32 * 32
        return at


def params(depth=DEPTH):
    cols, at = {}, 0
    for n in range(depth):
        for name, w in (("gm", KD), ("gf", KD), ("fw", 3 * KF), ("fb", KF)):
            cols[name, n] = at
            at += w
    for n in range(2):
        for name, w in (("mu", 6 * KD), ("w0", KD), ("a0", KD), ("kk", KD), ("ka", KD), ("rk", KD), ("lg", KD),
                        ("lb", KD)):
            cols[name, n] = at
            at += w
    for name, w in (("qg", 1), ("kg", 1), ("fbias", 1), ("cw", 3 * KD)):
        cols[name, 0] = at
        at += w
    return cols, at


def const_columns():
    where, at = {}, 0
    for name, w in (("ones", P), ("ident", P), ("heads", P), ("tri", P), ("neg", P), ("hot", 16), ("m8", TSN),
                    ("seq", NS), ("negn", NS * TS), ("qm", TS)):
        where[name] = (at, w)
        at += w
    return where, at


CONS, NCON = const_columns()
NEG = -1e30
MIX = [("r", 0), ("k", 2), ("v", 3), ("g1", 5), ("w1", 1), ("a1", 4)]
CT = 64
SB = 16
NBAT = 2 * KD + 2
DECAY = float(np.exp(-0.5))
GN_EPS = 64e-5


def mask_columns():
    where, at = {}, 0
    for name, w in (("d0", P), ("dt0", P), ("et0", P), ("ak0", P), ("r0", CT), ("d1", P), ("dt1", P), ("et1", P),
                    ("ak1", P), ("r1", CT), ("ist", CT), ("seqm", NS), ("scan0", 4 * CT), ("scan1", 4 * CT)):
        where[name] = (at, w)
        at += w
    return where, at


MASKS, NMASK = mask_columns()


def build_program(nc, I, O, mixers=MIXERS):
    depth = len(mixers)
    PC, NPAR = params()
    ctx = ExitStack()
    with ctx:
        m = Map((nc.sbuf_base + 31) // 32 * 32)

        def at(name, shape, dt, offset):
            return nc.alloc_sbuf_tensor_at(name, [P] + list(shape), dt, offset=offset)

        def sb(name, shape, dt=F32):
            return at(name, shape, dt, m.take(4 * int(np.prod(shape))))

        def sem(name):
            return ctx.enter_context(nc.semaphore(name))

        x = sb("x", [KD, T])
        xh_at = m.at
        xh, xl = sb("xh", [KD, T], F32R), sb("xl", [KD, T], F32R)
        raw = sb("raw", [RAWS, CH, P])
        wh, wl = sb("wh", [SPL, CH, P], F32R), sb("wl", [SPL, CH, P], F32R)
        con = sb("con", [NCON])
        ones, ident, heads = (con[:, CONS[k][0]:CONS[k][0] + P] for k in ("ones", "ident", "heads"))
        par = sb("par", [NPAR])
        qg8 = sb("qg8", [1])
        gneps = sb("gneps", [1])
        eps, free = sb("eps", [1]), sb("free", [32])
        big = m.at
        f = Map(big)
        at_hh, at_hl = f.take(4 * KF * T), f.take(4 * KF * T)
        hh, hl = at("hh", [KF, T], F32R, at_hh), at("hl", [KF, T], F32R, at_hl)
        misc = f.at
        gate = at("gate", [2, GW], F32, f.take(8 * GW))
        conv = at("conv", [2, GW], F32, f.take(8 * GW))
        hf = at("hf", [T], F32, f.take(4 * T))
        sq = at("sq", [2, T], F32, f.take(8 * T))
        at_rstd = f.take(4 * T)
        rstd = at("rstd", [T], F32, at_rstd)
        co = at("co", [KF, 2 + 2 * NS], F32, f.take(4 * KF * (2 + 2 * NS)))
        cs = at("cs", [KF, 2 * NS], F32, f.take(4 * KF * 2 * NS))
        assert f.at <= nc.sbuf_usable_end, (f.at, nc.sbuf_usable_end)
        xt = at("xt", [2, T], F32, misc)

        b = Map(big)
        qk = at("qk", [2 * KD, T], F32, b.take(8 * KD * T))
        vg = at("vg", [2 * KD, T], F32, b.take(8 * KD * T))
        lf = at("lf", [T], F32, b.take(4 * T))
        lfc = at("lfc", [T], F32, b.take(4 * T))
        fq = at("fq", [4, 16], F32, b.take(4 * 64))
        col = at("col", [64], F32, b.take(256))
        b1 = Map(b.at)
        qs, ks, vs = (at(k, [TP], F32, b1.take(4 * TP)) for k in ("qs", "ks", "vs"))
        vts = at("vts", [4, P], F32, b1.take(4 * TP))
        fm, fk = at("fm", [2, TP], F32, b1.take(8 * TP)), at("fk", [2, TP], F32, b1.take(8 * TP))
        sc = at("sc", [2, 10 * P], F32, b1.take(80 * P))
        pt = at("pt", [2, 4, TP], F32, b1.take(32 * TP))
        og = at("og", [TP], F32, b1.take(4 * TP))
        qn, rn = at("qn", [2, T], F32, b.at), at("rn", [2, T], F32, b.at + 8 * T)
        KR = 4
        b2 = Map(b.at)
        kp, vp = at("kp", [KR, D], F32, b2.take(4 * KR * D)), at("vp", [KR, D], F32, b2.take(4 * KR * D))
        at_st = b2.take(36 * P)
        st, pm, tot = at("st", [9, P], F32, at_st), at("pm", [9, P], F32, at_st), at("tot", [NS, 8, 16], F32, at_st)
        pts = at("pts", [9, P], F32, b2.take(36 * P))
        qb = at("qb", [KD, 2, TS], F32, b2.take(8 * KD * TS))
        ogs = at("ogs", [KD, TSN], F32, b2.take(4 * KD * TSN))
        lfp = at("lfp", [NS, 8, 16], F32, b2.take(4096))
        vtn = at("vtn", [D], F32, b2.take(4 * D))
        fn = at("fn", [16], F32, b2.take(64))
        fw8 = at("fw8", [NS, 16], F32, b2.take(512))
        zn = at("zn", [16, TS], F32, b2.take(512))
        fqn = at("fqn", [NS], F32, b2.take(32))
        lfn = at("lfn", [16], F32, b2.take(64))
        pgs = at("pgs", [64], I32, b2.take(256))
        assert max(b1.at, b2.at) <= nc.sbuf_usable_end, (b1.at, b2.at, nc.sbuf_usable_end)

        a = Map(big)
        rkv = at("rkv", [3 * KD, T], F32, a.take(12 * KD * T))
        at_xn, at_dx = a.take(4 * KD * T), a.take(4 * KD * T)
        xn, dx = at("xn", [KD, T], F32, at_xn), at("dx", [KD, T], F32, at_dx)
        la = at("la", [T], F32, at_rstd)
        sg = at("sg", [T], F32, a.take(4 * T))
        sho = at("sho", [KD, 1 + NS], F32, a.take(4 * KD * (1 + NS)))
        shi = at("shi", [KD, NS], F32, a.take(4 * KD * NS))
        wkvo = at("wkvo", [KD, 64], F32, a.take(2048))
        w2s = at("w2s", [P], F32, a.take(512))
        NSCAN = 8 * CT
        scans = at("scans", [NSCAN], F32, a.take(4 * NSCAN))
        assert a.at <= misc
        a1 = Map(misc)
        zz = at("zz", [2, 4, CT], F32, a1.take(2048))
        csum, cprev, pinv, pprev, kraw, kn, kh, kst, bb, t3 = (
            at("a_" + k, [4, CT], F32, a1.take(1024)) for k in
            "csum cprev pinv pprev kraw kn kh kst bb t3".split())
        sst, sp_, xb, ust = (at("a_" + k, [64], F32, a1.take(256)) for k in ("sst", "sp", "xb", "ust"))
        sbd, ubd = at("sbd", [2, 64], F32, a1.take(512)), at("ubd", [2, 64], F32, a1.take(512))
        assert a1.at <= at_rstd, a1.at - misc
        a2 = Map(at_rstd + 4 * T)
        lora2 = at("lora2", [2 * D], F32, a2.take(8 * D))
        msk = at("msk", [NMASK - NSCAN], F32, a2.take(4 * (NMASK - NSCAN)))
        assert a2.at <= nc.sbuf_usable_end, (a2.at, nc.sbuf_usable_end)
        slots = []
        for s_, where in enumerate((None, at_xn)):
            w = Map(xh_at if s_ == 0 else where)
            sl = {}
            for k in ("bda", "bdb", "bdk", "bdv", "m1", "m2", "m3", "m4", "m5", "m6", "et", "aak", "ktok", "vtok"):
                sl[k] = at(f"{k}{s_}", [4, 2, CT], F32, w.take(2048))
            sl["ar"] = at(f"ar{s_}", [4, 2, CT], F32, w.take(2048))
            for k in ("bst", "p", "arb", "ark", "vst"):
                sl[k] = at(f"{k}{s_}", [4, CT], F32, w.take(1024))
            sl["btok"] = sl["m6"]
            assert w.at <= (xh_at if s_ == 0 else where) + 8 * KD * T, w.at
            slots.append(sl)
        q_ = Map(at_xn)
        ss = at("ss", [KD, NS, 64], F32, q_.take(4 * KD * NS * 64))
        sb8 = at("sb8", [NS, 2, 64], F32, q_.take(4096))
        uq, vq = at("uq", [NS, 64], F32, q_.take(2048)), at("vq", [NS, 64], F32, q_.take(2048))

        ps = ctx.enter_context(nc.psum_tensor("ps", [P, 8 * 512], F32))

        def tile_cols(b):
            return b * 1024 + 512 - HT

        def pst(b, lo=0, hi=T):
            return ps[:, tile_cols(b) + lo:tile_cols(b) + hi]

        STAT = 2

        s_const, s_xin = sem("s_const"), sem("s_xin")
        s_raw = [sem(f"s_raw{i}") for i in range(RAWS)]
        s_hi, s_lo = sem("s_hi"), sem("s_lo")
        s_mm = sem("s_mm")
        s_ev = [sem("s_ev0"), sem("s_ev1")]
        s_rs, s_rr = sem("s_rs"), sem("s_rr")
        s_xt, s_xh, s_xl = sem("s_xt"), sem("s_xh"), sem("s_xl")
        s_sq, s_squ = sem("s_sq"), sem("s_squ")
        s_pad, s_g, s_t0, s_cv1, s_cv = sem("s_pad"), sem("s_g"), sem("s_t0"), sem("s_cv1"), sem("s_cv")
        s_si, s_h, s_hh, s_hl, s_cap = sem("s_si"), sem("s_h"), sem("s_hh"), sem("s_hl"), sem("s_cap")
        s_cs, s_co, s_out = sem("s_cs"), sem("s_co"), sem("s_out")
        s_eps, s_seen = sem("s_eps"), sem("s_seen")

        b_kd, b_vd = ([sem(f"b_{k}d{i}") for i in range(KR)] for k in "kv")
        (b_hsq, b_hsm, b_hrt, b_hrc, b_hn, b_f, b_ft, b_fe, b_qs, b_vtp, b_vts, b_fm, b_fkm, b_fk, b_s, b_sc, b_mx,
         b_ex, b_rc, b_nm, b_tp, b_pt, b_pv, b_og, b_oxh, b_oxl, b_out, b_pg, b_lfp, b_pre, b_pr, b_pf, b_zn, b_fq,
         b_vn, b_vne, b_qb, b_ks, b_st, b_stp, b_nb, b_nb1, b_sex, b_src, b_pn, b_ptp, b_pts, b_vs, b_ogs) = (
            sem("b_" + k) for k in (
                "hsq hsm hrt hrc hn f ft fe qs vtp vts fm fkm fk s sc mx ex rc nm tp pt pv og oxh oxl out pg lfp pre "
                "pr pf zn fq vn vne qb ks st stp nb nb1 sex src pn ptp pts vs ogs").split())

        (a_ld, a_xn, a_dx, a_sh, a_w2, a_z, a_k1, a_k2, a_zz, a_kn, a_sg, a_cs, a_cm, a_kr, a_kv, a_kk, a_ex,
         a_kh, a_bb, a_ar, a_bk, a_bd, a_rk, a_bo, a_bon, a_p1, a_cx, a_xe, a_cu, a_ue, a_ub,
         a_cs2, a_sp, a_s, a_sb, a_co, a_oe, a_zh, a_out2, a_q, a_qa, a_qd, a_qp, a_g, a_ga, a_gd, a_ss, a_out) = (
            sem("a_" + k) for k in (
                "ld xn dx sh w2 z k1 k2 zz kn sg cs cm kr kv kk ex kh bb ar bk bd rk bo bon p1 cx xe cu "
                "ue ub cs2 sp s sb co oe zh out2 q qa qd qp g ga gd ss out").split())

        a_A, a_D, a_m, a_e, a_d = ([sem(f"a_{k}{s_}") for s_ in range(2)] for k in "ADmed")

        class Ph:
            pass

        plan, c, n = {}, 0, 0
        conv0, hist_of, rows, loads = {}, {}, 0, 0
        NRES = 0
        NCONST = 2
        for layer, (kind, idx) in enumerate(mixers):
            names = []
            if kind == "a":
                names += [("r", 8, 8), ("k", 8, 8), ("v", 8, 8), ("g1", 1, 1), ("w1", 1, 1), ("a1", 1, 1)]
            elif kind == "b":
                names += [("qk", 16, 16), ("vg", 16, 16), ("f", 1, 1)]
            elif kind == "c":
                names += [("in", 24, 24)]
            if kind != "n":
                names += [("out", 8, 8)]
            names += [("up", 44, 44), ("down", 24, 8)]
            for name, nch, ntile in names:
                ph = Ph()
                ph.c0, ph.nch, ph.n0, ph.ntile = c, nch, n, ntile
                ph.res = NRES
                if name in ("out", "down"):
                    NRES += 1
                if name == "up" or (kind, name) == ("c", "in"):
                    conv0[layer, name], hist_of[layer, name] = rows, loads
                    rows, loads = rows + (KF if name == "up" else KD), loads + 1
                plan[layer, name] = ph
                c, n = c + nch, n + ntile
        NCHUNK = c
        n_norm, row0 = {}, {}
        q = r0 = 0
        for layer, (kind, _) in enumerate(mixers):
            if kind != "n":
                n_norm[layer, "mix"], row0[layer, "mix"] = q, r0
                q, r0 = q + 1, r0 + (len(MIX) if kind == "a" else 1) * KD
            n_norm[layer, "ffn"], row0[layer, "ffn"] = q, r0
            q, r0 = q + 1, r0 + KD
        def sq0(r):
            return KD + r * (1 + KD)

        def squ0(r):
            return KD + r * (2 + KD)

        def turns(n):
            return n // 2 + 1

        block = ctx.enter_context(nc.Block())

        def weights_in(sp, first, last):
            def load(c, i=0):
                if not isinstance(i, int) or c >= RAWS:
                    sp.wait_ge(s_lo, i * RAWS + c - RAWS + 1)
                src = I["w"][c] if isinstance(i, int) else I["w"][bass.ds(i * RAWS + c, 1)].rearrange("o p c -> p (o c)")
                sp.dma_start(raw[:, c % RAWS], src.rearrange("p (k c) -> p k c", c=P)).then_inc(s_raw[c % RAWS], 16)

            c = first
            while c < min(RAWS, last):
                load(c)
                c += 1
            n = (last - c) // RAWS
            if n > 1:
                with sp.Fori(0, n) as i:
                    for s in range(RAWS):
                        load(c + s, i)
                c += n * RAWS
            while c < last:
                load(c)
                c += 1

        def split_hi(act, c, i=0, step=0):
            if isinstance(i, int) and c + i * step >= NCHUNK:
                return
            act.wait_ge(s_raw[c % RAWS], i * (step // RAWS * 16) + 16 * (c // RAWS + 1))
            if c >= SPL:
                act.wait_ge(s_mm, i * step + c - SPL + 1)
            act.activation(wh[:, c % SPL], raw[:, c % RAWS], ACT.Copy).then_inc(s_hi, 1)

        def split_lo(dve, c, i=0, step=0):
            if isinstance(i, int) and c + i * step >= NCHUNK:
                return
            dve.wait_ge(s_hi, i * step + c + 1)
            dve.tensor_tensor(wl[:, c % SPL], raw[:, c % RAWS], wh[:, c % SPL].bitcast(F32),
                              ALU.subtract).then_inc(s_lo, 1)

        def chunk_mm(pe, c, n, rh, rl, k0=0, nk=CH, first=True, last=True, i=0, cstep=0, nstep=0, row_ready=None):
            pe.wait_ge(s_lo, i * cstep + c + 1)
            if first:
                pe.wait_ge(s_ev[n % 2], i * (nstep // 2) + turns(n))
            for k in range(nk):
                if row_ready is not None:
                    pe.wait_ge(row_ready[0], row_ready[1] + k)
                for a in range(2):
                    out = pst(n % 2, a * HT, (a + 1) * HT)
                    rhs_h, rhs_l = rh[:, k0 + k, a * HT:(a + 1) * HT], rl[:, k0 + k, a * HT:(a + 1) * HT]
                    w_h, w_l = wh[:, c % SPL, k], wl[:, c % SPL, k]
                    pe.matmul(out, w_h, rhs_h, start=(first and k == 0), stop=False)
                    pe.matmul(out, w_h, rhs_l, start=False, stop=False)
                    mm = pe.matmul(out, w_l, rhs_h, start=False, stop=(last and k == nk - 1))
            mm.then_inc(s_mm, 1)

        def norm_dve(dve, q, r0, col):
            dve.wait_ge(s_rs, q + 1)
            dve.reciprocal(rstd[:], rstd[:]).then_inc(s_rr, 1)

            def lo(k):
                dve.wait_ge(s_xh, r0 + k + 1)
                dve.tensor_tensor(xl[:, k], xt[:, k % 2], xh[:, k].bitcast(F32), ALU.subtract).then_inc(s_xl, 1)

            dve.wait_ge(s_rr, q + 1)
            for k in range(KD):
                if k >= 2:
                    dve.wait_ge(s_xl, r0 + k - 1)
                dve.scalar_tensor_tensor(xt[:, k % 2], x[:, k], par[:, col + k:col + k + 1], rstd[:],
                                         ALU.mult, ALU.mult).then_inc(s_xt, 1)
                if k >= 1:
                    lo(k - 1)
            lo(KD - 1)

        def norm_act(act, q, r0):
            act.wait_ge(s_squ, KD + q * (2 + KD))
            act.activation(rstd[:], pst(STAT), ACT.Sqrt, bias=eps[:], scale=1.0 / D).then_inc(s_rs, 1)
            for k in range(KD):
                act.wait_ge(s_xt, r0 + k + 1)
                act.activation(xh[:, k], xt[:, k % 2], ACT.Copy).then_inc(s_xh, 1)

        def square(act, k, count):
            if count > 0:
                act.wait_ge(s_squ, count)
            act.activation(sq[:, k % 2], x[:, k], ACT.Square).then_inc(s_sq, 1)

        def add_squares(pe, b, ready, start=False, stop=False):
            pe.wait_ge(s_sq, ready)
            for a in range(2):
                mm = pe.matmul(pst(STAT, a * HT, (a + 1) * HT), ones, sq[:, b, a * HT:(a + 1) * HT],
                               start=start, stop=stop)
            mm.then_inc(s_squ, 1)

        def rounds(eng, n, ph):
            if ph.c0 + ph.nch == NCHUNK:
                yield from range(n)
            else:
                with eng.Fori(0, n) as i:
                    yield i

        def res_act(act, ph, per):
            r = ph.res
            act.wait_ge(s_squ, squ0(r))
            act.activation(sq[:, 1], x[:, 0], ACT.Copy, scale=0.0).then_inc(s_sq, 1)
            for i in rounds(act, 2, ph):
                for j in range(4):
                    for e in range(per):
                        split_hi(act, ph.c0 + per * j + e + 2, i, 4 * per)
                    n = ph.n0 + j
                    act.wait_ge(s_ev[n % 2], i * 2 + turns(n) + 1)
                    act.wait_ge(s_squ, i * 4 + squ0(r) + j + 1)
                    act.activation(sq[:, j % 2:j % 2 + 1], x[:, bass.ds(i * 4 + j, 1)], ACT.Square)\
                        .then_inc(s_sq, 1)

        def res_dve(dve, ph, per):
            for i in rounds(dve, 2, ph):
                for j in range(4):
                    for e in range(per):
                        split_lo(dve, ph.c0 + per * j + e + 2, i, 4 * per)
                    n = ph.n0 + j
                    dve.wait_ge(s_mm, i * 4 * per + ph.c0 + per * (j + 1))
                    row = x[:, bass.ds(i * 4 + j, 1)]
                    dve.tensor_tensor(row, row, pst(n % 2).rearrange("p (o t) -> p o t", o=1), ALU.add)\
                        .then_inc(s_ev[n % 2], 1)

        def res_pe(pe, ph, per, rh, rl, ready, ready_step=0):
            r = ph.res
            parts = down_chunks() if per > 1 else [(0, CH)]
            add_squares(pe, 1, sq0(r) + 1, start=True)
            ready(pe)
            for i in rounds(pe, 2, ph):
                for j in range(4):
                    for e, (k0, nk) in enumerate(parts):
                        chunk_mm(pe, ph.c0 + per * j + e, ph.n0 + j, rh, rl, k0, nk, e == 0, e == per - 1,
                                 i, 4 * per, 4)
                    pe.wait_ge(s_sq, i * 4 + sq0(r) + 1 + j)
                    for a in range(2):
                        mm = pe.matmul(pst(STAT, a * HT, (a + 1) * HT), ones,
                                       sq[:, (j + 1) % 2, a * HT:(a + 1) * HT], start=False, stop=False)
                    mm.then_inc(s_squ, 1)
            add_squares(pe, 1, sq0(r) + 1 + KD, stop=True)

        def tok(ap, part):
            return ap[:, 0:TP] if part == 0 else ap[:, TP:T].rearrange("p (s t) -> p s t", t=TS)

        def hist(ap, part, back=0):
            if part == 0:
                return ap[:, 2 - back:2 - back + TP]
            return ap[:, GS:GW].rearrange("p (s t) -> p s t", t=2 + TS)[:, :, 2 - back:2 - back + TS]

        def one(ap):
            return ap.rearrange("p (o t) -> p o t", o=1)

        def up_act(act, layer):
            ph = plan[layer, "up"]
            fb, fw, up = PC["fb", layer], PC["fw", layer], conv0[layer, "up"]
            with act.Fori(0, KF // 2) as i:
                for u in range(2):
                    c, n, p = ph.c0 + 2 * u, ph.n0 + 2 * u, up + u
                    split_hi(act, c + 2, i, 4)
                    act.wait_ge(s_mm, i * 4 + c + 1)
                    act.wait_ge(s_pad, i * 2 + p + 1)
                    act.activation(gate[:, u, 2:GS], tok(pst(n % 2), 0), ACT.Copy)
                    act.activation(hist(gate[:, u], 1), tok(pst(n % 2), 1), ACT.Copy).then_inc(s_ev[n % 2], 1)
                    act.wait_ge(s_ev[n % 2], i * 2 + turns(n) + 1)
                    act.activation(conv[:, u, 2:GW], gate[:, u, 0:GW - 2], ACT.Identity,
                                   bias=par[:, bass.ds(i * 2 + fb + u, 1)],
                                   scale=par[:, bass.ds(i * 2 + fw + u, 1)]).then_inc(s_t0, 1)
                    act.wait_ge(s_cv, i * 2 + p + 3)
                    act.activation(conv[:, u, 2:GW], conv[:, u, 2:GW], ACT.Silu).then_inc(s_si, 1)
                    split_hi(act, c + 3, i, 4)
                    act.wait_ge(s_ev[(n + 1) % 2], i * 2 + turns(n + 1) + 1)
                    act.activation(hh[:, bass.ds(i * 2 + u, 1)], one(hf[:]), ACT.Copy).then_inc(s_hh, 1)

        def up_dve(dve, layer):
            ph = plan[layer, "up"]
            fw, up = PC["fw", layer], conv0[layer, "up"]
            with dve.Fori(0, KF // 2) as i:
                for u in range(2):
                    c, n, p = ph.c0 + 2 * u, ph.n0 + 2 * u, up + u
                    split_lo(dve, c + 2, i, 4)
                    dve.wait_ge(s_t0, i * 2 + p + 1)
                    dve.scalar_tensor_tensor(conv[:, u, 2:GW], gate[:, u, 1:GW - 1],
                                             par[:, bass.ds(i * 2 + fw + KF + u, 1)], conv[:, u, 2:GW],
                                             ALU.mult, ALU.add).then_inc(s_cv1, 1)
                    dve.wait_ge(s_cv1, i * 2 + p + 1)
                    dve.scalar_tensor_tensor(conv[:, u, 2:GW], gate[:, u, 2:GW],
                                             par[:, bass.ds(i * 2 + fw + 2 * KF + u, 1)], conv[:, u, 2:GW],
                                             ALU.mult, ALU.add).then_inc(s_cv, 1)
                    dve.wait_ge(s_mm, i * 4 + c + 2)
                    dve.wait_ge(s_si, i * 2 + layer * KF + u + 1)
                    dve.tensor_tensor(tok(hf[:], 0), hist(conv[:, u], 0), tok(pst((n + 1) % 2), 0), ALU.mult)
                    dve.tensor_tensor(tok(hf[:], 1), hist(conv[:, u], 1), tok(pst((n + 1) % 2), 1),
                                      ALU.mult).then_inc(s_ev[(n + 1) % 2], 1)
                    split_lo(dve, c + 3, i, 4)
                    dve.wait_ge(s_hh, i * 2 + p + 1)
                    dve.tensor_tensor(hl[:, bass.ds(i * 2 + u, 1)], one(hf[:]),
                                      hh[:, bass.ds(i * 2 + u, 1)].bitcast(F32),
                                      ALU.subtract).then_inc(s_hl, 1)

        def conv_pool(pool, layer, name, normed):
            ph, r0, load = plan[layer, name], conv0[layer, name], hist_of[layer, name]
            per = 2 if name == "up" else 3
            pool.wait_ge(s_xl, normed + KD)
            pool.wait_ge(s_cs, 16 * (load + 1))
            if load:
                pool.wait_ge(s_co, 16 * load)
            with pool.Fori(0, (KF if name == "up" else KD) // 2) as i:
                for u in range(2):
                    n, r = ph.n0 + per * u + per - 2, r0 + u
                    g = gate[:, u, GS:GW].rearrange("p (s t) -> p s t", t=2 + TS)
                    pool.wait_ge(s_cv, i * 2 + r + 1)
                    pool.sem_inc(s_seen, 1)
                    pool.memset(gate[:, u, 0:2], 0.0)
                    pool.tensor_copy(g[:, :, 0:2], cs[:, bass.ds(i * 2 + u, 1)]
                                     .rearrange("p o (s t) -> p (o s) t", t=2)).then_inc(s_pad, 1)
                    pool.wait_ge(s_ev[n % 2], i * per + turns(n) + 1)
                    pool.sem_inc(s_seen, 1)
                    pool.tensor_copy(co[:, bass.ds(i * 2 + u, 1), 0:2], one(gate[:, u, GS - 2:GS]))
                    pool.tensor_copy(co[:, bass.ds(i * 2 + u, 1), 2:].rearrange("p o (s t) -> p (o s) t", t=2),
                                     g[:, :, TS:TS + 2]).then_inc(s_cap, 1)

        def convmix_act(act, layer):
            ph, fw, r0 = plan[layer, "in"], PC["cw", 0], conv0[layer, "in"]
            with act.Fori(0, 2) as i:
                for j in range(4):
                    c, n, r, u = ph.c0 + 3 * j, ph.n0 + 3 * j, r0 + j, j % 2
                    split_hi(act, c + 2, i, 12)
                    act.wait_ge(s_mm, i * 12 + c + 1)
                    act.activation(sq[:, u], pst(n % 2), ACT.Copy).then_inc(s_ev[n % 2], 1)
                    split_hi(act, c + 3, i, 12)
                    act.wait_ge(s_ev[(n + 1) % 2], i * 6 + turns(n + 1) + 1)
                    act.activation(conv[:, u, 2:GW], gate[:, u, 0:GW - 2], ACT.Copy,
                                   scale=par[:, bass.ds(i * 4 + fw + j, 1)]).then_inc(s_t0, 1)
                    split_hi(act, c + 4, i, 12)
                    act.wait_ge(s_ev[(n + 2) % 2], i * 6 + turns(n + 2) + 1)
                    act.activation(hh[:, bass.ds(i * 4 + j, 1)], one(hf[:]), ACT.Copy).then_inc(s_hh, 1)

        def convmix_dve(dve, layer):
            ph, fw, r0 = plan[layer, "in"], PC["cw", 0], conv0[layer, "in"]
            with dve.Fori(0, 2) as i:
                for j in range(4):
                    c, n, r, u = ph.c0 + 3 * j, ph.n0 + 3 * j, r0 + j, j % 2
                    split_lo(dve, c + 2, i, 12)
                    dve.wait_ge(s_mm, i * 12 + c + 2)
                    dve.wait_ge(s_pad, i * 4 + r + 1)
                    dve.wait_ge(s_ev[n % 2], i * 6 + turns(n) + 1)
                    for part in range(2):
                        mul = dve.tensor_tensor(hist(gate[:, u], part), tok(sq[:, u], part),
                                                tok(pst((n + 1) % 2), part), ALU.mult)
                    mul.then_inc(s_ev[(n + 1) % 2], 1)
                    split_lo(dve, c + 3, i, 12)
                    dve.wait_ge(s_t0, i * 4 + r + 1)
                    dve.scalar_tensor_tensor(conv[:, u, 2:GW], gate[:, u, 1:GW - 1],
                                             par[:, bass.ds(i * 4 + fw + KD + j, 1)], conv[:, u, 2:GW],
                                             ALU.mult, ALU.add).then_inc(s_cv1, 1)
                    dve.wait_ge(s_cv1, i * 4 + r + 1)
                    dve.scalar_tensor_tensor(conv[:, u, 2:GW], gate[:, u, 2:GW],
                                             par[:, bass.ds(i * 4 + fw + 2 * KD + j, 1)], conv[:, u, 2:GW],
                                             ALU.mult, ALU.add).then_inc(s_cv, 1)
                    dve.wait_ge(s_mm, i * 12 + c + 3)
                    dve.wait_ge(s_cv, i * 4 + r + 3)
                    for part in range(2):
                        mul = dve.tensor_tensor(tok(hf[:], part), hist(conv[:, u], part),
                                                tok(pst((n + 2) % 2), part), ALU.mult)
                    mul.then_inc(s_ev[(n + 2) % 2], 1)
                    split_lo(dve, c + 4, i, 12)
                    dve.wait_ge(s_hh, i * 4 + r + 1)
                    dve.tensor_tensor(hl[:, bass.ds(i * 4 + j, 1)], one(hf[:]),
                                      hh[:, bass.ds(i * 4 + j, 1)].bitcast(F32), ALU.subtract).then_inc(s_hl, 1)

        def rows_pe(pe, ph, r0, per):
            with pe.Fori(0, ph.nch // per) as i:
                for e in range(per):
                    chunk_mm(pe, ph.c0 + e, ph.n0 + e, xh, xl, i=i, cstep=per, nstep=per,
                             row_ready=(s_xl, r0 + 1) if e == 0 else None)

        def bank(n, w=512):
            return ps[:, n * 512:n * 512 + w]

        def mview(name, n=None):
            at_, w = MASKS[name if n is None else f"{name}{n}"]
            return scans[:, at_ - NMASK + NSCAN:at_ - NMASK + NSCAN + w] if name == "scan" else msk[:, at_:at_ + w]

        def a_norm_act(act, layer, j):
            q = n_norm[layer, "mix"]
            act.wait_ge(s_squ, KD + q * (2 + KD))
            act.activation(rstd[:], pst(STAT), ACT.Sqrt, bias=eps[:], scale=1.0 / D).then_inc(s_rs, 1)
            if hist_done(layer):
                act.wait_ge(s_pad, rows_done(layer))
            act.dma_start(msk[:], I["masks"][:, 0:NMASK - NSCAN]).then_inc(a_ld, 16)
            act.dma_start(scans[:], I["masks"][:, NMASK - NSCAN:]).then_inc(a_ld, 16)
            act.dma_start(lora2[:], I["lora2"][j]).then_inc(a_ld, 16)
            act.dma_start(shi[:], I["shift"][j]).then_inc(a_ld, 16)

        def hist_done(layer):
            return sum(1 for (l, _) in hist_of if l < layer)

        def rows_done(layer):
            return sum((KF if name == "up" else KD) for (l, name) in hist_of if l < layer)

        def a_norm_dve(dve, layer, j):
            q, col_ = n_norm[layer, "mix"], PC["gm", layer]
            dve.wait_ge(s_rs, q + 1)
            dve.reciprocal(rstd[:], rstd[:]).then_inc(s_rr, 1)
            dve.wait_ge(s_rr, q + 1)
            for k in range(KD):
                dve.scalar_tensor_tensor(xn[:, k], x[:, k], par[:, col_ + k:col_ + k + 1], rstd[:],
                                         ALU.mult, ALU.mult).then_inc(a_xn, 1)
            for k in range(KD):
                dve.wait_ge(a_xn, KD * j + k + 1)
                dve.tensor_tensor(dx[:, k, 1:T], xn[:, k, 0:T - 1], xn[:, k, 1:T], ALU.subtract).then_inc(a_dx, 1)
            dve.wait_ge(a_dx, (KD + 2) * j + KD)
            dve.tensor_scalar(dx[:, :, 0], xn[:, :, 0], -1.0, None, ALU.mult).then_inc(a_dx, 1)
            dve.wait_ge(a_ld, 64 * (j + 1))
            starts = xn[:, :, TP:T].rearrange("p k (s t) -> p k s t", t=TS)
            dve.tensor_tensor(dx[:, :, TP:T].rearrange("p k (s t) -> p k s t", t=TS)[:, :, :, 0], shi[:],
                              starts[:, :, :, 0], ALU.subtract).then_inc(a_dx, 1)
            dve.tensor_copy(sho[:, :, 0:1], xn[:, :, TP - 1:TP]).then_inc(a_sh, 1)
            dve.tensor_copy(sho[:, :, 1:], starts[:, :, :, TS - 1]).then_inc(a_sh, 1)
            dve.wait_ge(a_dx, (KD + 2) * (j + 1))

        def mix_dve(dve, layer, j, n):
            name, c = MIX[n]
            r0 = row0[layer, "mix"] + n * KD
            if n:
                before = plan[layer, MIX[n - 1][0]]
                dve.wait_ge(s_mm, before.c0 + before.nch)

            def lo(k):
                dve.wait_ge(s_xh, r0 + k + 1)
                dve.tensor_tensor(xl[:, k], xt[:, k % 2], xh[:, k].bitcast(F32), ALU.subtract).then_inc(s_xl, 1)

            for k in range(KD):
                if k >= 2:
                    dve.wait_ge(s_xl, r0 + k - 1)
                mu = PC["mu", j] + c * KD + k
                dve.scalar_tensor_tensor(xt[:, k % 2], dx[:, k], par[:, mu:mu + 1], xn[:, k],
                                         ALU.mult, ALU.add).then_inc(s_xt, 1)
                if k >= 1:
                    lo(k - 1)
            lo(KD - 1)
            ph = plan[layer, name]
            for k in range(ph.nch):
                split_lo(dve, ph.c0 + k + 2)

        def mix_act(act, layer, j, n):
            name, c = MIX[n]
            r0 = row0[layer, "mix"] + n * KD
            if n:
                before = plan[layer, MIX[n - 1][0]]
                act.wait_ge(s_mm, before.c0 + before.nch)
            for k in range(KD):
                act.wait_ge(s_xt, r0 + k + 1)
                act.activation(xh[:, k], xt[:, k % 2], ACT.Copy).then_inc(s_xh, 1)
            ph = plan[layer, name]
            for k in range(ph.nch):
                m_ = ph.n0 + k
                split_hi(act, ph.c0 + k + 2)
                act.wait_ge(s_mm, ph.c0 + k + 1)
                if name == "g1":
                    op = act.activation(sg[:], pst(m_ % 2), ACT.Sigmoid)
                elif name == "w1":
                    op = act.activation(la[0:64], pst(m_ % 2)[0:64], ACT.Tanh)
                elif name == "a1":
                    op = act.activation(la[64:P], pst(m_ % 2)[64:P], ACT.Copy)
                else:
                    op = act.activation(rkv[:, n * KD + k], pst(m_ % 2), ACT.Copy)
                op.then_inc(s_ev[m_ % 2], 1)

        def mix_pe(pe, layer, n):
            ph = plan[layer, MIX[n][0]]
            r0 = row0[layer, "mix"] + n * KD
            for k in range(ph.nch):
                chunk_mm(pe, ph.c0 + k, ph.n0 + k, xh, xl, row_ready=(s_xl, r0 + 1) if k == 0 else None)

        class Bat:
            def __init__(self, j, s, i=None):
                self.j, self.s, self.i, self.prompt = j, (s if i is not None else 0), i, i is not None
                self.const = NBAT * j + (s if self.prompt else 2 * KD + s)
                self.b = s

            def cnt(self, n, k, back=0):
                v = n * (self.const - back) + k
                return self.i * (2 * n) + v if self.prompt else v

            def own(self, n, k):
                if self.prompt:
                    return self.i * n + n * (KD if self.s else KD + 2) * self.j + k
                return n * ((KD + 2) * self.j + KD + self.b) + k

            def row(self, t, first):
                if self.prompt:
                    lo = self.s * 4 * CT
                    return t[:, bass.ds(self.i + first, 1), lo:lo + 4 * CT].rearrange("p o (c t) -> p (o c) t", t=CT)
                return t[:, first + 4 * self.b:first + 4 * self.b + 4, TP:T]

            def per(self, c0):
                if self.prompt:
                    return par[:, bass.ds(self.i + c0, 1)].to_broadcast([P, 4 * CT])\
                        .rearrange("p (c t) -> p c t", t=CT)
                return par[:, c0 + 4 * self.b:c0 + 4 * self.b + 4].unsqueeze(2).to_broadcast([P, 4, CT])

        def flat(t):
            return t.rearrange("p a b -> p (a b)")

        two_heads = heads.rearrange("p (h t) -> p h t", h=2)

        def prep_pe(pe, B):
            pe.wait_ge(a_bon, B.cnt(1, 1))
            if B.prompt:
                pe.wait_ge(a_w2, B.i + KD * B.j + 1)
                for h in range(2):
                    mm = pe.matmul(bank(7)[:, h * 256:h * 256 + 256], w2s[64 * h:64 * h + 64],
                                   la[64 * h:64 * h + 64, B.s * 256:B.s * 256 + 256], start=True, stop=True)
                    if h == 0:
                        mm.then_inc(a_zh, 1)
                        pe.wait_ge(a_zh, B.cnt(1, 1))
            else:
                for h in range(2):
                    for p in range(4):
                        w0 = (4 * B.b + p) * P
                        mm = pe.matmul(bank(7)[:, h * 256 + p * CT:h * 256 + (p + 1) * CT],
                                       lora2[64 * h:64 * h + 64, w0:w0 + P], la[64 * h:64 * h + 64, TP:T],
                                       start=True, stop=True)
                    if h == 0:
                        mm.then_inc(a_zh, 1)
                        pe.wait_ge(a_zh, B.cnt(1, 1))
            mm.then_inc(a_z, 1)
            pe.wait_ge(a_zz, B.cnt(1, 1))
            pe.wait_ge(a_k2, B.cnt(1, 1))
            pe.matmul(bank(7, 256), heads, flat(kn[:]), start=True, stop=True).then_inc(a_kn, 1)
            pe.wait_ge(a_kr, B.cnt(1, 1))
            pe.wait_ge(a_rk, B.cnt(2, 2))
            pe.matmul(bank(7, 256), heads, flat(t3[:]), start=True, stop=True).then_inc(a_bo, 1)

        def prep_dve(dve, B, j):
            sl = slots[B.s]
            dve.wait_ge(a_bd, B.cnt(1, 1))
            dve.wait_ge(a_co, B.cnt(4, 1 if B.prompt else 5))
            dve.tensor_tensor(kraw[:], B.row(rkv, KD), B.per(PC["kk", j]), ALU.mult).then_inc(a_k1, 1)
            dve.wait_ge(a_z, B.cnt(1, 2))
            z = bank(7).rearrange("p (h c t) -> p h c t", h=2, t=CT)
            dve.tensor_tensor(zz[:, 0], z[:, 0], B.per(PC["w0", j]), ALU.add)
            dve.tensor_tensor(zz[:, 1], z[:, 1], B.per(PC["a0", j]), ALU.add).then_inc(a_zz, 1)
            dve.wait_ge(a_sg, B.cnt(1, 1))
            dve.tensor_tensor_scan(flat(csum[:]), mview("scan", 0 if B.prompt else 1), flat(zz[:, 0]), 0.0,
                                   ALU.mult, ALU.add).then_inc(a_cs, 1)
            dve.wait_ge(a_kr, B.cnt(1, 1))
            dve.tensor_scalar(kn[:], kn[:], 1e-12, None, ALU.max).then_inc(a_kv, 1)
            dve.wait_ge(a_kv, B.cnt(2, 1))
            dve.reciprocal(kn[:], kn[:]).then_inc(a_kv, 1)
            dve.scalar_tensor_tensor(t3[:], zz[:, 1], -1.0, B.per(PC["ka", j]), ALU.add, ALU.mult).then_inc(a_kh, 1)
            dve.wait_ge(a_kv, B.cnt(2, 2))
            dve.tensor_tensor(kraw[:], kraw[:], kn[:], ALU.mult).then_inc(a_kk, 1)
            dve.wait_ge(a_kh, B.cnt(2, 1))
            dve.scalar_tensor_tensor(kh[:], t3[:], 1.0, B.row(rkv, KD), ALU.add, ALU.mult).then_inc(a_kh, 1)
            dve.wait_ge(a_kk, B.cnt(1, 1))
            dve.wait_ge(a_ex, B.cnt(3, 3))
            dve.tensor_tensor(sl["ar"][:, :, 1], B.row(rkv, 0), sl["p"][:], ALU.mult)
            dve.scalar_tensor_tensor(sl["ar"][:, :, 0], kraw[:], -1.0, pprev[:], ALU.mult, ALU.mult)\
                .then_inc(a_ar, 1)
            dve.wait_ge(a_kh, B.cnt(2, 2))
            dve.tensor_tensor(t3[:], B.row(rkv, 0), kh[:], ALU.mult).then_inc(a_rk, 1)
            dve.tensor_tensor(kst[:], kh[:], pinv[:], ALU.mult).then_inc(a_bk, 1)
            dve.wait_ge(a_rk, B.cnt(2, 1))
            dve.tensor_tensor(t3[:], t3[:], B.per(PC["rk", j]), ALU.mult).then_inc(a_rk, 1)
            dve.wait_ge(a_bb, B.cnt(1, 1))
            dve.tensor_tensor(sl["bst"][:], bb[:], pinv[:], ALU.mult).then_inc(a_bk, 1)
            dve.wait_ge(a_bo, B.cnt(1, 1))
            dve.tensor_tensor(B.row(rkv, KD), bank(7, 256).rearrange("p (c t) -> p c t", t=CT), B.row(rkv, 2 * KD),
                              ALU.mult).then_inc(a_bon, 1)

        def prep_act(act, B):
            sl = slots[B.s]
            act.wait_ge(a_k1, B.cnt(1, 1))
            act.activation(kn[:], kraw[:], ACT.Square).then_inc(a_k2, 1)
            act.wait_ge(a_zz, B.cnt(1, 1))
            act.activation(zz[:], zz[:], ACT.Sigmoid).then_inc(a_sg, 1)
            act.wait_ge(a_kn, B.cnt(1, 1))
            act.activation(flat(kn[:]), bank(7, 256), ACT.Sqrt).then_inc(a_kr, 1)
            act.wait_ge(a_cs, B.cnt(1, 1))
            act.wait_ge(a_co, B.cnt(4, 1 if B.prompt else 5))
            if not B.prompt:
                act.wait_ge(a_qd, 6 * tile_no(B, 0) + 1)
            act.activation(sl["p"][:], csum[:], ACT.Exp, scale=-DECAY).then_inc(a_ex, 1)
            act.activation(pinv[:], csum[:], ACT.Exp, scale=DECAY).then_inc(a_ex, 1)
            act.wait_ge(a_cm, B.cnt(1, 1))
            act.activation(pprev[:], cprev[:], ACT.Exp, scale=-DECAY).then_inc(a_ex, 1)

        def prep_pool(pool, B):
            sl = slots[B.s]

            def seen(*waits):
                for s, v in waits:
                    pool.wait_ge(s, v)
                    pool.sem_inc(s_seen, 1)

            seen((a_cs, B.cnt(1, 1)))
            pool.tensor_tensor(cprev[:], csum[:], zz[:, 0], ALU.subtract).then_inc(a_cm, 1)
            seen((a_kk, B.cnt(1, 1)))
            pool.tensor_tensor(bb[:], kraw[:], zz[:, 1], ALU.mult).then_inc(a_bb, 1)
            def apart(to, src):
                return pool.tensor_tensor(sl[to][:], src.unsqueeze(2).to_broadcast([P, 4, 2, CT]),
                                          two_heads.unsqueeze(1).to_broadcast([P, 4, 2, CT]), ALU.mult)

            seen((a_ar, B.cnt(1, 1)))
            apart("bda", sl["ar"][:, :, 0])
            apart("bdv", B.row(rkv, 2 * KD))
            seen((a_bk, B.cnt(2, 1)))
            apart("bdk", kst[:])
            seen((a_bk, B.cnt(2, 2)))
            apart("bdb", sl["bst"][:]).then_inc(a_bd, 1)

        def sq_(sl, k, p):
            return sl[k][:, p].rearrange("p a b -> p (a b)")

        INV = [("m2", "m1", 0), ("m1", "m2", 1), ("m4", "m5", 2), ("m4", "m3", 0), ("m3", "m4", 1), ("m2", "m6", 2),
               ("m1", "m2", 0), ("m4", "m5", 1), ("et", "m6", 0), ("m6", None, 2), ("m1", "m2", 1), ("m1", "m5", 0),
               ("m1", "m3", 1)]
        COPY = {1: "m3", 2: "m4", 4: "m1", 5: "m2", 7: "m4", 9: "m1", 10: "m2"}
        ADD = {3: ("m5", "m6"), 6: ("m6", "m5"), 8: ("m5", "m6"), 11: ("m2", "m5"), 12: ("m2", "m3"), 13: ("m2", "m5")}
        NEED = {3: (2, 0), 4: (2, 0), 5: (2, 0), 6: (4, 1), 7: (4, 1), 8: (5, 2), 9: (5, 3), 10: (5, 3),
                11: (7, 3), 12: (7, 4), 13: (7, 5)}
        NC, NA = len(COPY) + 4, len(ADD)

        def inv_pe(pe, B, k):
            sl, b0 = slots[B.s], 3 * B.s
            if k == 0:
                pe.wait_ge(a_bd, B.cnt(1, 2))
                pe.wait_ge(a_oe, B.cnt(1, 1 if B.prompt else 2))
                pe.wait_ge(a_ar, B.cnt(1, 1))
                for n, (l_, r_) in enumerate((("bda", "bst"), ("bdb", "ar"), ("bdk", "ar"))):
                    w = CT if n == 0 else P
                    for p in range(4):
                        rhs = sl["bst"][:, p] if n == 0 else sq_(sl, "ar", p)
                        mm = pe.matmul(bank(b0 + n)[:, p * w:(p + 1) * w], sq_(sl, l_, p), rhs, start=True, stop=True)
                    mm.then_inc(a_A[B.s], 1)
                return
            if k <= 13:
                if k == 1:
                    pe.wait_ge(a_D[B.s], B.own(6, 2))
                elif k == 2:
                    pe.wait_ge(a_D[B.s], B.own(6, 4))
                else:
                    c, d = NEED[k]
                    pe.wait_ge(a_e[B.s], B.own(NC, c))
                    if d:
                        pe.wait_ge(a_d[B.s], B.own(NA, d))
                    if k == 3:
                        pe.wait_ge(a_p1, B.cnt(1, 1))
                        pe.wait_ge(a_D[B.s], B.own(6, 6))
                l_, r_, bk = INV[k - 1]
                for p in range(4):
                    out = bank(b0 + bk)[:, p * P:(p + 1) * P]
                    if r_ is None:
                        mm = pe.transpose(out, sq_(sl, l_, p), ident)
                    else:
                        mm = pe.matmul(out, sq_(sl, l_, p), sq_(sl, r_, p), start=True, stop=True)
                mm.then_inc(a_m[B.s], 1)
                return
            name, bk, copies, adds = {14: ("bdb", 0, 7, 5), 15: ("bdk", 2, 7, 5), 16: ("bdv", 1, 8, 6),
                                      17: ("bdv", 0, 8, 6)}[k]
            pe.wait_ge(a_e[B.s], B.own(NC, copies))
            pe.wait_ge(a_d[B.s], B.own(NA, adds))
            for p in range(4):
                if k < 17:
                    mm = pe.transpose(bank(b0 + bk)[:, p * P:(p + 1) * P], sq_(sl, name, p), ident)
                else:
                    mm = pe.matmul(bank(b0 + bk)[:, p * CT:(p + 1) * CT], sq_(sl, name, p), mview("ist"),
                                   start=True, stop=True)
            mm.then_inc(a_m[B.s], 1)

        def inv_act(act, B, k):
            sl, b0 = slots[B.s], 3 * B.s
            if k in COPY:
                dst, bk = COPY[k], INV[k - 1][2]
            elif k >= 14:
                dst, bk = {14: ("btok", 0), 15: ("ktok", 2), 16: ("vtok", 1), 17: ("vst", 0)}[k]
            else:
                return
            act.wait_ge(a_m[B.s], B.own(17, k))
            if k == 4:
                act.wait_ge(a_p1, B.cnt(1, 1))
            src = bank(b0 + bk, 4 * CT if k == 17 else 4 * P)
            out = flat(sl[dst][:]) if k == 17 else sl[dst][:].rearrange("p a b c -> p (a b c)")
            act.activation(out, src, ACT.Copy).then_inc(a_e[B.s], 1)

        def inv_dve(dve, B, k):
            sl, b0, n = slots[B.s], 3 * B.s, 0 if B.prompt else 1
            if k == 0:
                def spread(name):
                    return mview(name, n).rearrange("p (h t) -> p h t", h=2).unsqueeze(1).to_broadcast([P, 4, 2, CT])

                def twice(src):
                    return src.unsqueeze(2).to_broadcast([P, 4, 2, CT])

                left = bank(b0, 4 * CT).rearrange("p (c t) -> p c t", t=CT)
                rb, rk_ = (bank(b0 + q).rearrange("p (c w t) -> p c w t", w=2, t=CT) for q in (1, 2))
                mr = mview("r", n).unsqueeze(1).to_broadcast([P, 4, CT])
                for need, out, src, mask in ((1, "m1", twice(left), spread("d")),
                                             (2, "m2", twice(rb[:, :, 0]), spread("dt")),
                                             (2, "et", twice(rb[:, :, 0]), spread("et")),
                                             (2, "arb", rb[:, :, 1], mr),
                                             (3, "aak", twice(rk_[:, :, 0]), spread("ak")),
                                             (3, "ark", rk_[:, :, 1], mr)):
                    dve.wait_ge(a_A[B.s], B.own(3, need))
                    dve.tensor_tensor(sl[out][:], src, mask, ALU.mult).then_inc(a_D[B.s], 1)
            elif k in ADD:
                what, to = ADD[k]
                dve.wait_ge(a_m[B.s], B.own(17, k))
                dve.tensor_tensor(sl[to][:].rearrange("p a b c -> p (a b c)"), bank(b0 + INV[k - 1][2]),
                                  sl[what][:].rearrange("p a b c -> p (a b c)"), ALU.add).then_inc(a_d[B.s], 1)

        def inv_pool(pool, B):
            sl = slots[B.s]
            pool.wait_ge(a_D[B.s], B.own(6, 1))
            pool.sem_inc(s_seen, 1)
            pool.tensor_tensor(sl["m5"][:].rearrange("p a b c -> p a (b c)"), sl["m1"][:].rearrange("p a b c -> p a (b c)"),
                               ident.unsqueeze(1).to_broadcast([P, 4, P]), ALU.add).then_inc(a_p1, 1)


        def chain_pe(pe, B, g):
            sl, p, cx = slots[B.s], g % 4, chunk_no(B, g)
            if p == 0:
                pe.wait_ge(a_e[B.s], B.own(NC, NC))
                pe.wait_ge(a_d[B.s], B.own(NA, NA))
            pe.wait_ge(a_s, state_cnt(B, g))
            pe.matmul(bank(6, 64), sq_(sl, "bda", p), sst[:], start=True, stop=False)
            pe.matmul(bank(6, 64), sq_(sl, "aak", p), sl["vst"][:, p], start=False, stop=True).then_inc(a_cx, 1)
            pe.wait_ge(a_xe, cx)
            pe.matmul(bank(6, 64), sq_(sl, "m5", p), xb[:], start=True, stop=True).then_inc(a_cu, 1)
            pe.wait_ge(a_ue, cx)
            pe.matmul(bank(6, 64), sq_(sl, "btok", p), ust[:], start=True, stop=False)
            pe.matmul(bank(6, 64), sq_(sl, "ktok", p), sl["vst"][:, p], start=False, stop=True).then_inc(a_cs2, 1)
            out = bank(3 * B.s + 2)[:, p * CT:(p + 1) * CT]
            pe.wait_ge(a_sb, state_cnt(B, g))
            pe.matmul(out, sbd[:].rearrange("p a b -> p (a b)"), sl["ar"][:, p, 1], start=True, stop=False)
            pe.wait_ge(a_ub, cx)
            pe.matmul(out, ubd[:].rearrange("p a b -> p (a b)"), sl["arb"][:, p], start=False, stop=False)
            pe.matmul(out, sq_(sl, "vtok", p), sl["ark"][:, p], start=False, stop=True).then_inc(a_co, 1)

        def state_cnt(B, g):
            return B.i * 9 + 9 * KD * B.j + g + 1

        def chunk_no(B, g):
            return B.i * 8 + 8 * KD * B.j + g + 1

        def chain_dve(dve, B, g):
            sl, p, cx = slots[B.s], g % 4, chunk_no(B, g)
            if g == 0:
                dve.wait_ge(a_co, B.cnt(4, 5))
                dve.memset(sst[:], 0.0).then_inc(a_s, 1)
                dve.memset(sbd[:], 0.0).then_inc(a_sb, 1)
            dve.wait_ge(a_cx, cx)
            dve.tensor_copy(xb[:], bank(6, 64)).then_inc(a_xe, 1)
            dve.wait_ge(a_cs2, cx)
            dve.wait_ge(a_sp, cx)
            dve.wait_ge(a_sb, state_cnt(B, g))
            last = sl["p"][:, p, CT - 1:CT]
            dve.scalar_tensor_tensor(sst[:], bank(6, 64), last, sp_[:], ALU.mult, ALU.add).then_inc(a_s, 1)
            if g == 7:
                dve.wait_ge(a_s, state_cnt(B, 8))
                dve.tensor_copy(wkvo[:, bass.ds(B.i, 1)], sst[:].unsqueeze(1)).then_inc(a_ss, 1)

        def chain_act(act, B, g):
            sl, p, cx = slots[B.s], g % 4, chunk_no(B, g)
            act.wait_ge(a_s, state_cnt(B, g))
            act.activation(sp_[:], sst[:], ACT.Copy, scale=sl["p"][:, p, CT - 1:CT]).then_inc(a_sp, 1)
            act.wait_ge(a_cu, cx)
            act.activation(ust[:], bank(6, 64), ACT.Copy).then_inc(a_ue, 1)
            if p == 3:
                act.wait_ge(a_co, B.cnt(4, 9))
                act.sem_inc(s_seen, 1)
                act.activation(B.row(rkv, 0), bank(3 * B.s + 2, 256).rearrange("p (c t) -> p c t", t=CT), ACT.Copy)\
                    .then_inc(a_oe, 1)

        def chain_pool(pool, B, g):
            p, cx = g % 4, chunk_no(B, g)
            for s, v in ((a_ue, cx),):
                pool.wait_ge(s, v)
                pool.sem_inc(s_seen, 1)
            pool.tensor_tensor(ubd[:], ust[:].unsqueeze(1).to_broadcast([P, 2, 64]), two_heads, ALU.mult)\
                .then_inc(a_ub, 1)
            if g < 7:
                for s, v in ((a_s, state_cnt(B, g + 1)), (a_co, B.cnt(4, p + 6))):
                    pool.wait_ge(s, v)
                    pool.sem_inc(s_seen, 1)
                pool.tensor_tensor(sbd[:], sst[:].unsqueeze(1).to_broadcast([P, 2, 64]), two_heads, ALU.mult)\
                    .then_inc(a_sb, 1)
            else:
                pool.wait_ge(a_co, B.cnt(4, p + 6))
                pool.sem_inc(a_sb, 1)

        def tile_no(B, p):
            return KD * B.j + 4 * B.b + p

        def seq_pe(pe, j, B):
            sl = slots[0]
            pe.wait_ge(a_e[B.s], B.own(NC, NC))
            pe.wait_ge(a_d[B.s], B.own(NA, NA))
            pe.wait_ge(a_out, 16 * (1 + 3 * j))
            for p in range(4):
                t, n = tile_no(B, p), 4 * B.b + p
                pe.wait_ge(a_qd, 6 * t + 1)
                pe.matmul(bank(3), sq_(sl, "bda", p), ss[:, n].rearrange("p a b -> p (a b)"), start=True, stop=True)\
                    .then_inc(a_q, 1)
                pe.matmul(bank(6, 64), sq_(sl, "aak", p), sl["vst"][:, p], start=True, stop=True).then_inc(a_q, 1)
                pe.wait_ge(a_qd, 6 * t + 4)
                pe.matmul(bank(6, 64), sq_(sl, "m5", p), xb[:], start=True, stop=True).then_inc(a_q, 1)
                out = bank(2)[:, p * CT:(p + 1) * CT]
                pe.wait_ge(a_qp, 2 * t + 1)
                for q in range(NS):
                    pe.matmul(out[:, q * TS:(q + 1) * TS], sb8[:, q].rearrange("p a b -> p (a b)"),
                              sl["ar"][:, p, 1, q * TS:(q + 1) * TS], start=(q == 0), stop=False,
                              skip_group_check=True)
                pe.wait_ge(a_qp, 2 * t + 2)
                pe.matmul(out, ubd[:].rearrange("p a b -> p (a b)"), sl["arb"][:, p], start=False, stop=False,
                          skip_group_check=True)
                pe.matmul(out, sq_(sl, "vtok", p), sl["ark"][:, p], start=False, stop=True,
                          skip_group_check=True).then_inc(a_co, 1)
                pe.wait_ge(a_qd, 6 * t + 5)
                pe.matmul(bank(4), sq_(sl, "btok", p), uq[:].rearrange("p a b -> p (a b)"), start=True, stop=False)
                pe.matmul(bank(4), sq_(sl, "ktok", p), vq[:].rearrange("p a b -> p (a b)"), start=False, stop=True)\
                    .then_inc(a_q, 1)

        def seq_dve(dve, j, B):
            sl = slots[0]
            seqm = mview("seqm").unsqueeze(2).to_broadcast([P, NS, 64])
            for p in range(4):
                t, n = tile_no(B, p), 4 * B.b + p
                dve.wait_ge(a_q, 4 * t + 1)
                dve.tensor_tensor(uq[:], bank(3).rearrange("p (q i) -> p q i", i=64), seqm, ALU.mult).then_inc(a_qd, 1)
                dve.wait_ge(a_qd, 6 * t + 2)
                dve.tensor_reduce(xb[:], uq[:].rearrange("p q i -> p i q"), AX.X, ALU.add).then_inc(a_qd, 1)
                dve.wait_ge(a_q, 4 * t + 2)
                dve.wait_ge(a_qd, 6 * t + 3)
                dve.tensor_tensor(xb[:], xb[:], bank(6, 64), ALU.add).then_inc(a_qd, 1)
                dve.wait_ge(a_qa, t + 1)
                dve.tensor_tensor(uq[:], ust[:].unsqueeze(1).to_broadcast([P, NS, 64]), seqm, ALU.mult)
                dve.tensor_tensor(vq[:], sl["vst"][:, p].unsqueeze(1).to_broadcast([P, NS, 64]), seqm, ALU.mult)\
                    .then_inc(a_qd, 1)
                dve.wait_ge(a_q, 4 * t + 4)
                dve.tensor_tensor(ss[:, n], ss[:, n], bank(4).rearrange("p (q i) -> p q i", i=64), ALU.add)\
                    .then_inc(a_qd, 1)
                dve.wait_ge(a_qd, 6 * t + 6)
                ends = sl["p"][:, p].rearrange("p (q t) -> p q t", t=TS)[:, :, TS - 1:TS].to_broadcast([P, NS, 64])
                dve.tensor_tensor(ss[:, n], ss[:, n], ends, ALU.mult).then_inc(a_qd, 1)

        def seq_act(act, j, B):
            for p in range(4):
                t = tile_no(B, p)
                act.wait_ge(a_q, 4 * t + 3)
                act.activation(ust[:], bank(6, 64), ACT.Copy).then_inc(a_qa, 1)
            act.wait_ge(a_co, B.cnt(4, 9))
            act.activation(B.row(rkv, 0), bank(2, 256).rearrange("p (c t) -> p c t", t=CT), ACT.Copy).then_inc(a_oe, 1)

        def seq_pool(pool, j, B):
            for p in range(4):
                t, n = tile_no(B, p), 4 * B.b + p
                pool.wait_ge(a_out, 16 * (1 + 3 * j))
                if t:
                    pool.wait_ge(a_q, 4 * t)
                pool.tensor_tensor(sb8[:], ss[:, n].unsqueeze(2).to_broadcast([P, NS, 2, 64]),
                                   two_heads.unsqueeze(1).to_broadcast([P, NS, 2, 64]), ALU.mult).then_inc(a_qp, 1)
                pool.wait_ge(a_qa, t + 1)
                pool.tensor_tensor(ubd[:], ust[:].unsqueeze(1).to_broadcast([P, 2, 64]), two_heads, ALU.mult)\
                    .then_inc(a_qp, 1)

        def gn_pe(pe, j):
            for n in range(KD):
                g = KD * j + n
                pe.wait_ge(a_oe, NBAT * (j + 1) + 2)
                pe.wait_ge(a_bon, NBAT * (j + 1) + 1)
                if g:
                    pe.wait_ge(a_gd, 6 * g)
                for a_ in range(2):
                    mm = pe.matmul(pst(0, a_ * HT, (a_ + 1) * HT), heads, rkv[:, n, a_ * HT:(a_ + 1) * HT],
                                   start=True, stop=True)
                mm.then_inc(a_g, 1)
                pe.wait_ge(a_ga, 3 * g + 1)
                for a_ in range(2):
                    mm = pe.matmul(pst(1, a_ * HT, (a_ + 1) * HT), heads, sq[:, 0, a_ * HT:(a_ + 1) * HT],
                                   start=True, stop=True)
                mm.then_inc(a_g, 1)
                for a_ in range(2):
                    mm = pe.matmul(pst(2, a_ * HT, (a_ + 1) * HT), lora2[:, D + n * P:D + (n + 1) * P],
                                   sg[:, a_ * HT:(a_ + 1) * HT], start=True, stop=True)
                mm.then_inc(a_g, 1)

        def gn_act(act, j):
            for n in range(KD):
                g = KD * j + n
                act.wait_ge(a_gd, 6 * g + 1)
                act.activation(sq[:, 0], rkv[:, n], ACT.Square).then_inc(a_ga, 1)
                act.wait_ge(a_g, 3 * g + 2)
                act.activation(sq[:, 1], pst(1), ACT.Sqrt, bias=gneps[:], scale=1.0 / 64).then_inc(a_ga, 1)
                act.wait_ge(a_gd, 6 * g + 5)
                act.activation(xh[:, n], rkv[:, n], ACT.Copy).then_inc(a_ga, 1)

        def gn_dve(dve, j):
            for n in range(KD):
                g, lg, lb = KD * j + n, PC["lg", j] + n, PC["lb", j] + n
                row = rkv[:, n]

                def step(k):
                    dve.wait_ge(a_gd, 6 * g + k)

                dve.wait_ge(a_g, 3 * g + 1)
                dve.scalar_tensor_tensor(row, pst(0), -1.0 / 64, row, ALU.mult, ALU.add).then_inc(a_gd, 1)
                dve.wait_ge(a_ga, 3 * g + 2)
                dve.reciprocal(sq[:, 1], sq[:, 1]).then_inc(a_gd, 1)
                step(2)
                dve.scalar_tensor_tensor(row, row, par[:, lg:lg + 1], sq[:, 1], ALU.mult, ALU.mult).then_inc(a_gd, 1)
                step(3)
                dve.scalar_tensor_tensor(row, row, par[:, lb:lb + 1], rkv[:, KD + n], ALU.add, ALU.add)\
                    .then_inc(a_gd, 1)
                dve.wait_ge(a_g, 3 * g + 3)
                step(4)
                dve.tensor_tensor(row, row, pst(2), ALU.mult).then_inc(a_gd, 1)
                dve.wait_ge(a_ga, 3 * g + 3)
                dve.tensor_tensor(xl[:, n], row, xh[:, n].bitcast(F32), ALU.subtract).then_inc(a_gd, 1)

        def a_pe(pe, layer, j):
            for n in range(len(MIX)):
                mix_pe(pe, layer, n)
            for n in range(2):
                last = plan[layer, MIX[-1][0]].n0 - n
                pe.wait_ge(s_ev[last % 2], turns(last) + 1)
            with pe.Fori(0, KD) as i:
                bats = [Bat(j, s, i) for s in range(2)]
                for B in bats:
                    prep_pe(pe, B)
                for k in range(18):
                    for B in bats:
                        inv_pe(pe, B, k)
                for g in range(8):
                    chain_pe(pe, bats[g // 4], g)
            for b_ in range(2):
                B = Bat(j, b_)
                prep_pe(pe, B)
                for k in range(18):
                    inv_pe(pe, B, k)
                seq_pe(pe, j, B)
            gn_pe(pe, j)
            res_pe(pe, plan[layer, "out"], 1, xh, xl, lambda e: e.wait_ge(a_gd, 6 * KD * (j + 1)))

        def a_act(act, layer, j):
            a_norm_act(act, layer, j)
            for n in range(len(MIX)):
                mix_act(act, layer, j, n)
            with act.Fori(0, KD) as i:
                bats = [Bat(j, s, i) for s in range(2)]
                for B in bats:
                    prep_act(act, B)
                for k in range(1, 18):
                    for B in bats:
                        inv_act(act, B, k)
                for g in range(8):
                    chain_act(act, bats[g // 4], g)
            act.wait_ge(a_ss, KD * (j + 1))
            act.wait_ge(a_co, 4 * (NBAT * j + 2 * KD) + 5)
            act.dma_start(ss[:], I["wkv"][j]).then_inc(a_out, 16)
            for b_ in range(2):
                B = Bat(j, b_)
                prep_act(act, B)
                for k in range(1, 18):
                    inv_act(act, B, k)
                seq_act(act, j, B)
            act.dma_start(O["wkvp"][j], wkvo[:]).then_inc(a_out2, 16)
            act.wait_ge(a_qd, 6 * KD * (j + 1) + 1)
            act.dma_start(O["wkvs"][j], ss[:]).then_inc(a_out, 16)
            act.wait_ge(a_sh, 2 * (j + 1))
            act.dma_start(O["shift"][j], sho[:]).then_inc(a_out, 16)
            gn_act(act, j)
            act.wait_ge(a_out, 48 * (j + 1))
            act.wait_ge(a_out2, 16 * (j + 1))
            res_act(act, plan[layer, "out"], 1)

        def a_dve(dve, layer, j):
            a_norm_dve(dve, layer, j)
            for n in range(len(MIX)):
                mix_dve(dve, layer, j, n)
            dve.wait_ge(s_mm, plan[layer, MIX[-1][0]].c0 + 1)
            with dve.Fori(0, KD) as i:
                bats = [Bat(j, s, i) for s in range(2)]
                for B in bats:
                    prep_dve(dve, B, j)
                for k in range(14):
                    for B in bats:
                        inv_dve(dve, B, k)
                for g in range(8):
                    chain_dve(dve, bats[g // 4], g)
            for b_ in range(2):
                B = Bat(j, b_)
                prep_dve(dve, B, j)
                for k in range(14):
                    inv_dve(dve, B, k)
                seq_dve(dve, j, B)
            gn_dve(dve, j)
            res_dve(dve, plan[layer, "out"], 1)

        def a_pool(pool, layer, j):
            pool.wait_ge(s_mm, plan[layer, MIX[-1][0]].c0 + 1)
            pool.wait_ge(a_ld, 64 * (j + 1))
            with pool.Fori(0, KD) as i:
                bats = [Bat(j, s, i) for s in range(2)]
                pool.wait_ge(a_z, bats[0].cnt(1, 1))
                pool.sem_inc(s_seen, 1)
                pool.tensor_copy(w2s[:].unsqueeze(1), lora2[:, 0:D].rearrange("p (k c) -> p k c", c=P)[:, bass.ds(i, 1)])\
                    .then_inc(a_w2, 1)
                for B in bats:
                    prep_pool(pool, B)
                for B in bats:
                    inv_pool(pool, B)
                for g in range(8):
                    chain_pool(pool, bats[g // 4], g)
            for b_ in range(2):
                B = Bat(j, b_)
                prep_pool(pool, B)
                inv_pool(pool, B)
                seq_pool(pool, j, B)

        def store_act(act, ph, t0, n, dst, k0, func=ACT.Copy):
            with act.Fori(0, n // 4) as i:
                for j in range(4):
                    c, m = ph.c0 + t0 + j, ph.n0 + t0 + j
                    split_hi(act, c + 2, i, 4)
                    act.wait_ge(s_mm, i * 4 + c + 1)
                    act.activation(dst[:, bass.ds(i * 4 + k0 + j, 1)], one(pst(m % 2)), func)\
                        .then_inc(s_ev[m % 2], 1)

        def plain_dve(dve, ph, t0, n):
            with dve.Fori(0, n // 4) as i:
                for j in range(4):
                    split_lo(dve, ph.c0 + t0 + j + 2, i, 4)

        def qk_act(act, layer):
            ph = plan[layer, "qk"]
            for half in range(2):
                with act.Fori(0, 2) as i:
                    def root(j):
                        r = 8 * half + j
                        act.wait_ge(b_hsm, i * 4 + r + 1)
                        act.activation(rn[:, j % 2], pst(3), ACT.Sqrt, bias=eps[:], scale=1.0 / 64)\
                            .then_inc(b_hrt, 1)

                    for j in range(4):
                        r = 8 * half + j
                        c, m = ph.c0 + r, ph.n0 + r
                        split_hi(act, c + 2, i, 4)
                        act.wait_ge(s_mm, i * 4 + c + 1)
                        act.activation(qk[:, bass.ds(i * 4 + r, 1)], one(pst(m % 2)), ACT.Copy)\
                            .then_inc(s_ev[m % 2], 1)
                        act.wait_ge(b_hn, i * 4 + r + 1)
                        act.wait_ge(s_ev[m % 2], i * 2 + turns(m) + 1)
                        act.sem_inc(s_seen, 1)
                        act.activation(one(qn[:, j % 2]), qk[:, bass.ds(i * 4 + r, 1)], ACT.Square)\
                            .then_inc(b_hsq, 1)
                        if j:
                            root(j - 1)
                    root(3)

        def qk_dve(dve, layer):
            ph = plan[layer, "qk"]
            for half in range(2):
                g = qg8[:] if half == 0 else par[:, PC["kg", 0]:PC["kg", 0] + 1]
                with dve.Fori(0, 2) as i:
                    def norm(j):
                        r = 8 * half + j
                        dve.wait_ge(b_hrt, i * 4 + r + 2)
                        dve.reciprocal(rn[:, j % 2], rn[:, j % 2]).then_inc(b_hrc, 1)
                        dve.wait_ge(b_hrc, i * 4 + r + 1)
                        row = qk[:, bass.ds(i * 4 + r, 1)]
                        dve.scalar_tensor_tensor(row, row, g, one(rn[:, j % 2]), ALU.mult, ALU.mult)\
                            .then_inc(b_hn, 1)

                    for j in range(4):
                        split_lo(dve, ph.c0 + 8 * half + j + 2, i, 4)
                        if j:
                            norm(j - 1)
                    norm(3)

        def qk_pe(pe, layer, r0):
            ph = plan[layer, "qk"]
            with pe.Fori(0, 4) as i:
                def heads_sum(j):
                    pe.wait_ge(b_hsq, i * 4 + j + 1)
                    pe.wait_ge(b_hrt, i * 4 + j + 1)
                    for a in range(2):
                        mm = pe.matmul(pst(3, a * HT, (a + 1) * HT), heads, qn[:, j % 2, a * HT:(a + 1) * HT],
                                       start=True, stop=True)
                    mm.then_inc(b_hsm, 1)

                for j in range(4):
                    chunk_mm(pe, ph.c0 + j, ph.n0 + j, xh, xl, i=i, cstep=4, nstep=4,
                             row_ready=(s_xl, r0 + 1) if j == 0 else None)
                    if j:
                        heads_sum(j - 1)
                heads_sum(3)

        def forget_act(act, layer):
            ph = plan[layer, "f"]
            split_hi(act, ph.c0 + 2)
            act.wait_ge(s_mm, ph.c0 + 1)
            t = qn[0:16, 0]
            act.activation(lf[0:16], pst(ph.n0 % 2)[0:16], ACT.Identity,
                           bias=par[0:16, PC["fbias", 0]:PC["fbias", 0] + 1]).then_inc(s_ev[ph.n0 % 2], 1)
            act.wait_ge(s_ev[ph.n0 % 2], turns(ph.n0) + 1)
            act.activation(t, lf[0:16], ACT.Abs).then_inc(b_f, 1)
            act.wait_ge(b_f, 1)
            act.activation(t, t, ACT.Exp, scale=-1.0).then_inc(b_f, 1)
            act.wait_ge(b_f, 2)
            act.activation(t, t, ACT.Ln, bias=1.0).then_inc(b_f, 1)
            act.wait_ge(b_ft, 5)
            act.activation(fq[:].rearrange("p a b -> p (a b)"), ps[:, 2048:2048 + 64], ACT.Copy).then_inc(b_fe, 1)
            act.dma_start(O["logf"], lf[0:16]).then_inc(b_out, 16)
            act.dma_start(O["k"], qk[:, KD:]).then_inc(b_out, 16)
            act.dma_start(O["v"], vg[:, 0:KD]).then_inc(b_out, 16)

        def forget_dve(dve, layer):
            split_lo(dve, plan[layer, "f"].c0 + 2)
            dve.memset(rn[0:16, 0], 1.0).then_inc(b_pr, 1)
            dve.wait_ge(b_f, 3)
            dve.scalar_tensor_tensor(lf[0:16], lf[0:16], 0.0, qn[0:16, 0], ALU.min, ALU.subtract).then_inc(b_pr, 1)
            dve.wait_ge(b_pr, 2)
            dve.tensor_tensor_scan(lfc[0:16, 0:TP], rn[0:16, 0, 0:TP], lf[0:16, 0:TP], 0.0, ALU.mult, ALU.add)\
                .then_inc(b_pr, 1)
            dve.wait_ge(b_ft, 5)
            dve.tensor_copy(col[0:TSN, 32:48], ps[0:TSN, 2560:2576]).then_inc(b_fe, 1)

        def forget_pe(pe, layer):
            ph = plan[layer, "f"]
            chunk_mm(pe, ph.c0, ph.n0, xh, xl)
            pe.wait_ge(b_pr, 3)
            for n in range(4):
                pe.transpose(ps[:, 2048 + 16 * n:2048 + 16 * n + 16], lfc[0:16, n * P:(n + 1) * P],
                             ident[0:16, 0:16]).then_inc(b_ft, 1)
            pe.transpose(ps[0:TSN, 2560:2576], lf[0:16, TP:T], ident[0:16, 0:16]).then_inc(b_ft, 1)

        OFF = [0, 1, 3, 6]

        def prompt_pool(pool):
            pool.wait_ge(b_fe, 2)
            with pool.Fori(0, KD) as i:
                pool.wait_ge(b_sc, i * 8 + 4)
                pool.sem_inc(s_seen, 1)
                pool.tensor_copy(one(qs[:]), qk[:, bass.ds(i, 1), 0:TP])
                pool.tensor_copy(one(ks[:]), qk[:, bass.ds(i + KD, 1), 0:TP])
                pool.wait_ge(b_vts, i + 1)
                pool.sem_inc(s_seen, 1)
                pool.tensor_copy(one(vs[:]), vg[:, bass.ds(i, 1), 0:TP]).then_inc(b_qs, 1)

        def prompt_pe(pe):
            with pe.Fori(0, KD) as i:
                pe.wait_ge(b_qs, i + 1)
                pe.wait_ge(b_vts, i + 1)
                for n in range(4):
                    mm = pe.transpose(bank(4)[:, n * P:(n + 1) * P], vs[:, n * P:(n + 1) * P], ident)
                mm.then_inc(b_vtp, 1)
                pe.wait_ge(b_fm, i + 1)
                pe.wait_ge(b_pt, i * 8 + 2)
                for h in range(2):
                    pe.matmul(bank(5 + 2 * h), ones[0:16], fm[0:16, h], start=True, stop=True).then_inc(b_fkm, 1)
                for h in range(2):
                    for n in range(4):
                        pe.wait_ge(b_sc, i * 8 + 4 * h + n + 1)
                        nk = (n + 1) * P
                        pe.matmul(bank(n, nk), qs[64 * h:64 * h + 64, n * P:nk],
                                  ks[64 * h:64 * h + 64, 0:nk], start=True, stop=False)
                        pe.matmul(bank(n)[:, nk - P:nk], ident, con[:, CONS["neg"][0]:CONS["neg"][0] + P],
                                  start=False, stop=True).then_inc(b_s, 1)
                for h in range(2):
                    for n in range(4):
                        k = 4 * h + n
                        pe.wait_ge(b_nm, i * 8 + k + 1)
                        pe.wait_ge(b_pt, i * 8 + k + 1)
                        for m in range(n + 1):
                            at = (OFF[n] + m) * P
                            mm = pe.transpose(bank(5 + 2 * (k % 2))[:, m * P:(m + 1) * P], sc[:, h, at:at + P], ident)
                        mm.then_inc(b_tp, 1)
                    pe.wait_ge(b_pt, i * 8 + 4 * h + 6)
                    pe.wait_ge(b_vts, i + 2)
                    if h == 0:
                        pe.wait_ge(b_og, i + 1)
                    for n in range(4):
                        mm = pe.matmul(bank(6)[64 * h:64 * h + 64, n * P:], vts[:, n, 64 * h:64 * h + 64],
                                       pt[:, h, n, n * P:], start=(n == 0), stop=(n == 3), skip_group_check=True)
                    mm.then_inc(b_pv, 1)

        def prompt_act(act):
            with act.Fori(0, KD) as i:
                act.wait_ge(b_vtp, i + 1)
                act.wait_ge(b_pv, i * 2 + 2)
                act.activation(vts[:].rearrange("p a b -> p (a b)"), bank(4), ACT.Copy).then_inc(b_vts, 1)
                for h in range(2):
                    act.wait_ge(b_fkm, i * 2 + h + 1)
                    act.wait_ge(b_sc, i * 8 + 4)
                    act.activation(fk[:, h], bank(5 + 2 * h), ACT.Copy).then_inc(b_fk, 1)

                def exp(h, n):
                    k = 4 * h + n
                    act.wait_ge(b_mx, i * 8 + k + 1)
                    row = sc[:, h, OFF[n] * P:(OFF[n] + n + 1) * P]
                    act.activation(row, row, ACT.Exp, bias=col[:, k:k + 1], accum_out=col[:, 8 + k:9 + k])\
                        .then_inc(b_ex, 1)

                def turn(h, n):
                    k = 4 * h + n
                    act.wait_ge(b_tp, i * 8 + k + 9)
                    act.wait_ge(b_pv, i * 2 + h + 1)
                    act.activation(pt[:, h, 0:n + 1, n * P:(n + 1) * P],
                                   bank(5 + 2 * (k % 2), (n + 1) * P).rearrange("p (a b) -> p a b", b=P),
                                   ACT.Copy).then_inc(b_pt, 1)

                for h in range(2):
                    for n in range(4):
                        exp(h, n)
                for h in range(2):
                    for n in range(4):
                        turn(h, n)
                act.wait_ge(b_og, i + 2)
                act.activation(xh[:, bass.ds(i, 1), 0:TP], one(og[:]), ACT.Copy).then_inc(b_oxh, 1)

        def prompt_dve(dve):
            with dve.Fori(0, KD) as i:
                dve.wait_ge(b_fk, i * 2 + 2)
                for h in range(2):
                    op = dve.tensor_scalar(fm[0:16, h], lfc[0:16, 0:TP],
                                           con[0:16, bass.ds(i * 2 + CONS["hot"][0] + h, 1)], None, ALU.mult)
                op.then_inc(b_fm, 1)
                for h in range(2):
                    for n in range(4):
                        k = 4 * h + n
                        row = sc[:, h, OFF[n] * P:(OFF[n] + n + 1) * P]
                        dve.wait_ge(b_s, i * 8 + k + 1)
                        dve.wait_ge(b_fk, i * 2 + h + 3)
                        dve.wait_ge(b_tp, i * 8 + k + 1)
                        dve.scalar_tensor_tensor(row, bank(n, (n + 1) * P), fq[:, n, bass.ds(i * 2 + h, 1)],
                                                 fk[:, h, 0:(n + 1) * P], ALU.add, ALU.subtract).then_inc(b_sc, 1)
                        dve.wait_ge(b_sc, i * 8 + k + 5)
                        dve.tensor_reduce(col[:, k:k + 1], row, AX.X, ALU.max, negate=True).then_inc(b_mx, 1)
                for h in range(2):
                    for n in range(4):
                        k = 4 * h + n
                        row = sc[:, h, OFF[n] * P:(OFF[n] + n + 1) * P]
                        dve.wait_ge(b_ex, i * 8 + k + 1)
                        dve.reciprocal(col[:, 8 + k:9 + k], col[:, 8 + k:9 + k]).then_inc(b_rc, 1)
                        dve.wait_ge(b_rc, i * 8 + k + 1)
                        dve.tensor_scalar(row, row, col[:, 8 + k:9 + k], None, ALU.mult).then_inc(b_nm, 1)
                dve.wait_ge(b_pv, i * 2 + 4)
                dve.tensor_tensor(one(og[:]), one(bank(6)), vg[:, bass.ds(i + KD, 1), 0:TP], ALU.mult)\
                    .then_inc(b_og, 1)
                dve.wait_ge(b_oxh, i + 1)
                dve.tensor_tensor(xl[:, bass.ds(i, 1), 0:TP], one(og[:]), xh[:, bass.ds(i, 1), 0:TP].bitcast(F32),
                                  ALU.subtract).then_inc(b_oxl, 1)

        def attend_sp(sp):
            sp.wait_ge(b_oxl, KD)
            sp.dma_start(pgs[0:1], I["pages"]).then_inc(b_pg, 16)
            sp.wait_ge(b_pg, 16)
            with sp.Fori(0, NS) as i:
                for p in range(8):
                    page = sp.value_load(pgs[0:1, bass.ds(i * 8 + p, 1)], min_val=0, max_val=I["cache_v"].shape[0] - 1)
                    sp.dma_start(lfp[:, bass.ds(i, 1), p], I["cache_logf"][bass.ds(page, 1)]
                                 .rearrange("o r h -> r o h")).then_inc(b_lfp, 16)
            with sp.Fori(0, NS) as i:
                for dst, src, sems, used in ((kp, I["cache_k"].rearrange("g p k r -> g p (k r)"), b_kd, b_ks),
                                             (vp, I["cache_v"], b_vd, b_vs)):
                    for p in range(8):
                        page = sp.value_load(pgs[0:1, bass.ds(i * 8 + p, 1)], min_val=0,
                                             max_val=src.shape[0] - 1)
                        sp.wait_ge(used, i * 9 + (9 + p - KR + 1 if p >= KR else 9 + p - KR))
                        sp.dma_start(dst[:, bass.ds(p % KR, 1)], src[bass.ds(page, 1)].rearrange("o p d -> p o d"))\
                            .then_inc(sems[p % KR], 16)

        def samples_pe(pe):
            tri, m8 = (con[:, CONS[k][0]:CONS[k][0] + CONS[k][1]] for k in ("tri", "m8"))
            pe.wait_ge(b_lfp, 16 * 64)
            pe.wait_ge(b_oxl, KD)
            flat = lfp[:].rearrange("p a b c -> p (a b c)")
            for n in range(2):
                pe.matmul(bank(n), tri, flat[:, n * 512:(n + 1) * 512], start=True, stop=True)
            for n in range(2):
                pe.matmul(bank(2 + n), ones, flat[:, n * 512:(n + 1) * 512], start=True, stop=True)
            pe.matmul(bank(4, 16)[0:TSN], m8[0:TSN], col[0:TSN, 32:48], start=True, stop=True).then_inc(b_pre, 1)
            for n in range(KD):
                mm = pe.transpose(ps[0:TSN, 6 * 512 + n * P:6 * 512 + (n + 1) * P], vg[:, n, TP:T], ident)
            mm.then_inc(b_vn, 1)
            pe.wait_ge(b_zn, 2)
            pe.matmul(bank(5, NS), zn[0:TSN].rearrange("p a b -> p (a b)"),
                      con[0:TSN, CONS["seq"][0]:CONS["seq"][0] + NS], start=True, stop=True).then_inc(b_fq, 1)
            pe.wait_ge(b_pf, 2)
            pe.wait_ge(b_vne, 1)
            with pe.Fori(0, NS) as i:
                pe.wait_ge(b_qb, i + 1)
                pe.wait_ge(b_pts, i * 3 + 3)
                for p in range(9):
                    if p < 8:
                        pe.wait_ge(b_kd[p % KR], i * (16 * 8 // KR) + 16 * (p // KR + 1))
                    for n in range(KD):
                        if p < 8:
                            k, out = kp[:, p % KR, n * P:(n + 1) * P], bank(p // 4)[:, p % 4 * P + n * 16:p % 4 * P + n * 16 + 16]
                        else:
                            k, out = qk[:, KD + n, TP:T], bank(2)[0:TSN, n * 16:n * 16 + 16]
                        mm = pe.matmul(out, k, qb[:, n].rearrange("p a b -> p (a b)"), start=True, stop=True)
                    mm.then_inc(b_ks, 1)
                pe.wait_ge(b_sex, i + 1)
                for p in range(9):
                    pe.wait_ge(b_st, i * 3 + p // 4 + 1)
                    if p < 8:
                        mm = pe.transpose(bank(3 + p // 4)[:, p % 4 * P:(p % 4 + 1) * P], st[:, p], ident)
                    else:
                        pe.sem_inc(s_seen, 1)
                        mm = pe.transpose(bank(5, TSN), st[0:TSN, p], ident[0:TSN, 0:TSN])
                mm.then_inc(b_stp, 1)
                pe.wait_ge(b_pn, i + 1)
                for p in range(9):
                    if p < 8:
                        mm = pe.transpose(bank(p // 4)[:, p % 4 * P:(p % 4 + 1) * P], pm[:, p], ident)
                    else:
                        mm = pe.transpose(bank(2)[0:TSN, 0:P], pm[:, p, 0:TSN], ident)
                mm.then_inc(b_ptp, 1)
                pe.wait_ge(b_pts, i * 3 + 6)
                pe.wait_ge(b_ogs, i + 1)
                for p in range(9):
                    if p < 8:
                        pe.wait_ge(b_vd[p % KR], i * (16 * 8 // KR) + 16 * (p // KR + 1))
                    for n in range(KD):
                        r, v = (P, vp[:, p % KR, n * P:(n + 1) * P]) if p < 8 else (TSN, vtn[0:TSN, n * P:(n + 1) * P])
                        mm = pe.matmul(bank(6)[:, n * 16:n * 16 + 16], v, pts[0:r, p, n * 16:n * 16 + 16],
                                       start=(p == 0 and n == 0), stop=(p == 8), skip_group_check=True)
                    mm.then_inc(b_vs, 1)

        def samples_act(act):
            act.wait_ge(b_vn, 1)
            act.activation(vtn[0:TSN], ps[0:TSN, 6 * 512:6 * 512 + D], ACT.Copy).then_inc(b_vne, 1)
            with act.Fori(0, NS) as i:
                act.wait_ge(b_nb, i + 1)
                act.activation(pm[:].rearrange("p a b -> p (a b)")[:, 0:8 * P + TSN], ps[:, 3 * 512:3 * 512 + 8 * P + TSN],
                               ACT.Exp, bias=col[:, 49:50], accum_out=col[:, 50:51]).then_inc(b_sex, 1)
                act.wait_ge(b_ptp, i + 1)
                act.wait_ge(b_vs, i * 9 + 9)
                for n in range(2):
                    act.activation(pts[:, 4 * n:4 * n + 4].rearrange("p a b -> p (a b)"), bank(n), ACT.Copy)\
                        .then_inc(b_pts, 1)
                act.activation(pts[0:TSN, 8], bank(2, P)[0:TSN], ACT.Copy).then_inc(b_pts, 1)
            act.wait_ge(b_ogs, NS + 1)
            act.activation(xh[:, :, TP:T], ogs[:], ACT.Copy).then_inc(b_oxh, 1)

        def samples_dve(dve):
            def cview(k):
                return con[:, CONS[k][0]:CONS[k][0] + CONS[k][1]]

            dve.wait_ge(b_pre, 1)
            dve.memset(tot[:, :, 0], 0.0).then_inc(b_pr, 1)
            sums = ps[:, 1024:2048].rearrange("p (s g h) -> p s g h", g=8, h=16)
            for g in range(8):
                dve.wait_ge(b_pr, 4 + g)
                dst = tot[:, :, g + 1] if g < 7 else fw8[:]
                dve.tensor_tensor(dst, tot[:, :, g], sums[:, :, g], ALU.add).then_inc(b_pr, 1)
            dve.wait_ge(b_pr, 12)
            for n in range(2):
                dve.tensor_tensor(lfp[:].rearrange("p a b c -> p (a b c)")[:, n * 512:(n + 1) * 512], bank(n),
                                  tot[:].rearrange("p a b c -> p (a b c)")[:, n * 512:(n + 1) * 512],
                                  ALU.add).then_inc(b_pf, 1)
            pick = pts[0:TSN, 0].rearrange("p (h s) -> p h s", s=NS)
            dve.tensor_tensor(pick, fw8[0:TSN].rearrange("p s h -> p h s"),
                              cview("seq")[0:TSN].unsqueeze(1).to_broadcast([TSN, 16, NS]), ALU.mult)\
                .then_inc(b_pr, 1)
            dve.wait_ge(b_pr, 13)
            dve.tensor_reduce(fn[0:TSN], pick, AX.X, ALU.add).then_inc(b_pr, 1)
            dve.wait_ge(b_pr, 14)
            dve.tensor_tensor(fn[0:TSN], fn[0:TSN], bank(4, 16)[0:TSN], ALU.add).then_inc(b_zn, 1)
            dve.wait_ge(b_zn, 1)
            dve.tensor_tensor(zn[0:TSN], fn[0:TSN].unsqueeze(2).to_broadcast([TSN, 16, TS]),
                              cview("qm")[0:TSN].unsqueeze(1).to_broadcast([TSN, 16, TS]), ALU.mult)\
                .then_inc(b_zn, 1)
            dve.memset(qb[:], 0.0).then_inc(b_pr, 1)
            dve.wait_ge(b_fq, 1)
            dve.tensor_copy(fqn[:], bank(5, NS)).then_inc(b_pr, 1)
            dve.wait_ge(b_pr, 16)
            dve.wait_ge(b_pf, 2)
            with dve.Fori(0, NS) as i:
                dve.wait_ge(b_ks, i * 9 + 9)
                for h in range(2):
                    rows_ = slice(64 * h, 64 * h + 64)
                    op = dve.tensor_copy(qb[rows_, :, h], qk[rows_, 0:KD, bass.ds(i * TS + TP, TS)])
                op.then_inc(b_qb, 1)
                for n in range(2):
                    dve.wait_ge(b_ks, i * 9 + 9 + 4 * n + 4)
                    dve.tensor_tensor(
                        st[:, 4 * n:4 * n + 4].rearrange("p a (h q) -> p (a h) q", q=TS),
                        bank(n).rearrange("p (a q) -> p a q", q=TS),
                        lfp[:, bass.ds(i, 1), 4 * n:4 * n + 4].rearrange("p o a h -> p (o a h)")
                        .unsqueeze(2).to_broadcast([P, 64, TS]), ALU.subtract).then_inc(b_st, 1)
                dve.wait_ge(b_ks, i * 9 + 18)
                new = st[0:TSN, 8].rearrange("p (h q) -> p h q", q=TS)
                dve.tensor_tensor(new, bank(2, P)[0:TSN].rearrange("p (h q) -> p h q", q=TS),
                                  fn[0:TSN].unsqueeze(2).to_broadcast([TSN, 16, TS]), ALU.subtract).then_inc(b_nb1, 1)
                dve.wait_ge(b_nb1, i * 2 + 1)
                dve.tensor_tensor(new, new, con[0:TSN, bass.ds(i * TS + CONS["negn"][0], TS)]
                                  .unsqueeze(1).to_broadcast([TSN, 16, TS]), ALU.add).then_inc(b_st, 1)
                dve.wait_ge(b_stp, i + 1)
                dve.tensor_reduce(col[:, 48:49], ps[:, 3 * 512:3 * 512 + 8 * P + TSN], AX.X, ALU.max, negate=True)\
                    .then_inc(b_nb1, 1)
                dve.wait_ge(b_nb1, i * 2 + 2)
                dve.tensor_tensor(col[:, 48:49], col[:, 48:49], fqn[:, bass.ds(i, 1)], ALU.subtract)\
                    .then_inc(b_src, 1)
                dve.wait_ge(b_src, i * 2 + 1)
                dve.tensor_tensor(col[:, 49:50], col[:, 48:49], fqn[:, bass.ds(i, 1)], ALU.add).then_inc(b_nb, 1)
                dve.wait_ge(b_sex, i + 2)
                dve.reciprocal(col[:, 50:51], col[:, 50:51]).then_inc(b_src, 1)
                dve.wait_ge(b_src, i * 2 + 2)
                row = pm[:].rearrange("p a b -> p (a b)")[:, 0:8 * P + TSN]
                dve.tensor_scalar(row, row, col[:, 50:51], None, ALU.mult).then_inc(b_pn, 1)
                dve.wait_ge(b_vs, i * 9 + 18)
                out = bank(6, P).rearrange("p (n h q) -> p n h q", h=2, q=TS)
                for h in range(2):
                    rows_ = slice(64 * h, 64 * h + 64)
                    op = dve.tensor_tensor(ogs[rows_, :, bass.ds(i * TS, TS)], out[rows_, :, h],
                                           vg[rows_, KD:, bass.ds(i * TS + TP, TS)], ALU.mult)
                op.then_inc(b_ogs, 1)
            dve.wait_ge(b_oxh, KD + 1)
            dve.tensor_tensor(xl[:, :, TP:T], ogs[:], xh[:, :, TP:T].bitcast(F32), ALU.subtract).then_inc(b_oxl, 1)

        @block.sync
        def _(sp):
            done = 0
            for layer, (kind, idx) in enumerate(mixers):
                if kind == "b":
                    weights_in(sp, done, plan[layer, "out"].c0 + SPL + RAWS)
                    done = plan[layer, "out"].c0 + SPL + RAWS
                    attend_sp(sp)
            weights_in(sp, done, NCHUNK)

        @block.tensor
        def _(pe):
            pe.wait_ge(s_const, 16 * NCONST)
            for k in range(KD):
                add_squares(pe, k % 2, k + 1, start=(k == 0), stop=(k == KD - 1))
            for layer, (kind, idx) in enumerate(mixers):
                if kind == "a":
                    a_pe(pe, layer, idx)
                if kind == "b":
                    qk_pe(pe, layer, row0[layer, "mix"])
                    rows_pe(pe, plan[layer, "vg"], row0[layer, "mix"], 4)
                    forget_pe(pe, layer)
                    prompt_pe(pe)
                    samples_pe(pe)
                    res_pe(pe, plan[layer, "out"], 1, xh, xl, lambda e: e.wait_ge(b_oxl, KD + 1))
                if kind == "c":
                    rows_pe(pe, plan[layer, "in"], row0[layer, "mix"], 12)
                    res_pe(pe, plan[layer, "out"], 1, hh, hl,
                           lambda e: e.wait_ge(s_hl, conv0[layer, "in"] + KD))
                rows_pe(pe, plan[layer, "up"], row0[layer, "ffn"], 4)
                res_pe(pe, plan[layer, "down"], len(down_chunks()), hh, hl,
                       lambda e: e.wait_ge(s_hl, conv0[layer, "up"] + KF))

        def history_in(act, layer, name, src):
            if conv0[layer, name]:
                act.wait_ge(s_pad, conv0[layer, name])
            act.dma_start(cs[:, 0:src.shape[1]], src).then_inc(s_cs, 16)

        def history_out(act, layer, name, dst):
            act.wait_ge(s_cap, conv0[layer, name] + dst.shape[1])
            act.dma_start(dst, co[:, 0:dst.shape[1]]).then_inc(s_co, 16)

        @block.scalar
        def _(act):
            act.dma_start(con[:], I["consts"]).then_inc(s_const, 16)
            act.dma_start(par[:], I["params"]).then_inc(s_const, 16)
            act.dma_start(x[:], I["x"]).then_inc(s_xin, 16)
            act.wait_ge(s_xin, 16)
            split_hi(act, 0)
            split_hi(act, 1)
            for k in range(KD):
                square(act, k, k - 1)
            act.wait_ge(s_eps, 1)
            act.wait_ge(s_const, 16 * NCONST)
            for layer, (kind, idx) in enumerate(mixers):
                if kind in "ab" and hist_done(layer):
                    act.wait_ge(s_co, 16 * hist_done(layer))
                if kind == "a":
                    a_act(act, layer, idx)
                if kind == "b":
                    norm_act(act, n_norm[layer, "mix"], row0[layer, "mix"])
                    qk_act(act, layer)
                    store_act(act, plan[layer, "vg"], 0, 8, vg, 0)
                    store_act(act, plan[layer, "vg"], 8, 8, vg, 8, ACT.Sigmoid)
                    forget_act(act, layer)
                    prompt_act(act)
                    samples_act(act)
                    res_act(act, plan[layer, "out"], 1)
                if kind == "c":
                    history_in(act, layer, "in", I["conv_mix"])
                    norm_act(act, n_norm[layer, "mix"], row0[layer, "mix"])
                    convmix_act(act, layer)
                    history_out(act, layer, "in", O["conv_mix"])
                    res_act(act, plan[layer, "out"], 1)
                history_in(act, layer, "up", I["conv_ffn"][layer])
                norm_act(act, n_norm[layer, "ffn"], row0[layer, "ffn"])
                up_act(act, layer)
                history_out(act, layer, "up", O["conv_ffn"][layer])
                res_act(act, plan[layer, "down"], len(down_chunks()))
            last = plan[depth - 1, "down"]
            for n in range(last.n0 + KD - 2, last.n0 + KD):
                act.wait_ge(s_ev[n % 2], turns(n) + 1)
            act.dma_start(O["x"], x[:]).then_inc(s_out, 16)
            act.wait_ge(s_out, 16)
            act.wait_ge(s_co, 16 * len(hist_of))
            if ("b", 0) in mixers:
                act.wait_ge(b_out, 48)

        @block.vector
        def _(dve):
            dve.memset(gneps[:], GN_EPS)
            dve.memset(eps[:], RMS_EPS).then_inc(s_eps, 1)
            for b in range(2):
                dve.memset(free[:, 2 * b:2 * b + 1], 0.0).then_inc(s_ev[b], 1)
                dve.memset(free[:, 2 * b + 1:2 * b + 2], 0.0).then_inc(s_cv, 1)
            for n, (s, by) in enumerate(((b_hn, 2), (b_hrt, 1), (b_sc, 4), (b_vts, 1), (b_fk, 2), (b_tp, 8), (b_pt, 2),
                                         (b_pv, 2), (b_og, 1), (b_ks, 9), (b_pts, 3), (b_sex, 1), (b_vs, 9),
                                         (b_ogs, 1), (a_bon, 1), (a_bd, 1), (a_co, 5), (a_oe, 2), (a_z, 1),
                                         (a_qd, 1))):
                dve.memset(free[:, 4 + n:5 + n], 0.0).then_inc(s, by)
            dve.wait_ge(s_const, 16 * NCONST)
            dve.tensor_scalar(qg8[:], par[:, PC["qg", 0]:PC["qg", 0] + 1], 64.0 ** -0.5, None, ALU.mult)
            split_lo(dve, 0)
            split_lo(dve, 1)
            for layer, (kind, idx) in enumerate(mixers):
                if kind == "a":
                    a_dve(dve, layer, idx)
                if kind == "b":
                    norm_dve(dve, n_norm[layer, "mix"], row0[layer, "mix"], PC["gm", layer])
                    qk_dve(dve, layer)
                    plain_dve(dve, plan[layer, "vg"], 0, 16)
                    forget_dve(dve, layer)
                    prompt_dve(dve)
                    samples_dve(dve)
                    res_dve(dve, plan[layer, "out"], 1)
                if kind == "c":
                    norm_dve(dve, n_norm[layer, "mix"], row0[layer, "mix"], PC["gm", layer])
                    convmix_dve(dve, layer)
                    res_dve(dve, plan[layer, "out"], 1)
                norm_dve(dve, n_norm[layer, "ffn"], row0[layer, "ffn"], PC["gf", layer])
                up_dve(dve, layer)
                res_dve(dve, plan[layer, "down"], len(down_chunks()))

        @block.gpsimd
        def _(pool):
            for layer, (kind, idx) in enumerate(mixers):
                if kind == "a":
                    a_pool(pool, layer, idx)
                if kind == "b":
                    prompt_pool(pool)
                if kind == "c":
                    conv_pool(pool, layer, "in", row0[layer, "mix"])
                conv_pool(pool, layer, "up", row0[layer, "ffn"])


def rows(a):
    a = np.asarray(a)
    return np.ascontiguousarray(a.T.reshape(-1, P, a.shape[0]).transpose(1, 0, 2))


def unrows(a):
    return np.ascontiguousarray(a.transpose(1, 0, 2).reshape(-1, a.shape[2]).T)


def cols(v):
    return np.asarray(v).reshape(-1, P).T


def tiles(w):
    k, m = w.shape
    return np.asarray(w).reshape(k // P, P, m // P, P).transpose(2, 1, 0, 3)


def pack(a):
    w = np.zeros((sum(KINDS[k] + FFN_CHUNKS for k, _ in MIXERS), P, CH, P), np.float32)
    at = 0

    def put(*chunks):
        nonlocal at
        for c in chunks:
            w[at, :, 0:c.shape[1]] = c
            at += 1

    for layer, (kind, j) in enumerate(MIXERS):
        if kind == "a":
            for n in range(3):
                put(*tiles(a["a_w_rkv"][j, n]))
            put(*tiles(a["a_g1"][j]))
            lora = tiles(np.concatenate([a["a_w1"][j], a["a_a1"][j]], 1))
            put(*lora, *lora)
            put(*tiles(a["a_w_out"][j]))
        elif kind == "b":
            put(*tiles(a["b_w_in"][j, :, 0:4 * D]))
            put(*tiles(np.concatenate([a["b_w_in"][j, :, 4 * D:], np.zeros((D, P - 16), np.float32)], 1)))
            put(*tiles(a["b_w_out"][j]))
        else:
            t = tiles(a["c_w_in"][j])
            for n in range(KD):
                put(t[KD + n], t[2 * KD + n], t[n])
            put(*tiles(a["c_w_out"][j]))
        t = tiles(a["f_w_up"][layer])
        for n in range(KF):
            put(t[n], t[KF + n])
        t = tiles(a["f_w_down"][layer])
        for n in range(KD):
            put(*[t[n][:, k:k + nk] for k, nk in down_chunks()])
    where, npar = params()
    par = np.zeros((P, npar), np.float32)

    def put_par(name, n, v):
        v = cols(v)
        par[:, where[name, n]:where[name, n] + v.shape[1]] = v

    for layer in range(DEPTH):
        put_par("gm", layer, a["norm_mix_g"][layer])
        put_par("gf", layer, a["norm_ffn_g"][layer])
        put_par("fw", layer, a["f_conv_w"][layer])
        put_par("fb", layer, a["f_conv_b"][layer])
    for j in range(2):
        for name, v in (("mu", "a_mu"), ("w0", "a_w0"), ("a0", "a_a0"), ("kk", "a_k_k"), ("ka", "a_k_a"),
                        ("rk", "a_r_k"), ("lg", "a_lnx_g"), ("lb", "a_lnx_b")):
            put_par(name, j, a[v][j])
    put_par("cw", 0, a["c_conv_w"][0])
    for name, v in (("qg", "b_q_norm_g"), ("kg", "b_k_norm_g")):
        put_par(name, 0, np.tile(a[v][0], 2))
    par[0:16, where["fbias", 0]] = np.asarray(a["b_f_bias"][0])
    x = np.concatenate([a["x_prompt"].reshape(TP, D), a["x_sample"].reshape(TSN, D)])
    return dict(
        masks=masks(),
        lora2=np.stack([np.concatenate([np.concatenate([a["a_w2"][j], a["a_a2"][j]]), a["a_g2"][j]], 1)
                        for j in range(2)]),
        shift=np.stack([rows(v) for v in np.asarray(a["state_shift"])]),
        wkv=np.ascontiguousarray(np.asarray(a["state_wkv"]).reshape(2, NS, KD, 2, 64, 64)
                                 .transpose(0, 3, 5, 2, 1, 4).reshape(2, P, KD, NS, 64)),
        pages=np.asarray(a["page_table"]).reshape(1, -1),
        cache_k=np.ascontiguousarray(np.asarray(a["cache_k"][0]).reshape(-1, P, KD, P).transpose(0, 3, 2, 1)),
        cache_v=np.asarray(a["cache_v"][0]).reshape(-1, P, D), cache_logf=np.asarray(a["cache_logf"][0]),
        x=rows(x), w=w.reshape(-1, P, CH * P), params=par, consts=constants(),
        conv_ffn=np.stack([rows(c.reshape(2 * NS, FF)) for c in np.asarray(a["state_conv_ffn"])]),
        conv_mix=rows(np.asarray(a["state_conv_mix"]).reshape(2 * NS, D)),
    )


def constants():
    c = np.zeros((P, NCON), np.float32)
    p, f = np.arange(P)[:, None], np.arange(P)[None, :]
    tok, tok2, q = np.arange(P)[:, None], np.arange(TSN)[None, :], np.arange(TS)[None, :]
    values = dict(
        ones=np.ones((P, P)), ident=p == f,
        heads=p // 64 == f // 64,
        tri=p <= f,
        neg=np.where(f > p, NEG, 0),
        hot=p == f[:, 0:16],
        m8=(p // TS == tok2 // TS) & (p <= tok2),
        seq=p // TS == f[:, 0:NS],
        negn=np.where((p // TS == tok2 // TS) & (p % TS <= tok2 % TS), 0, NEG),
        qm=p % TS == q,
    )
    for name, v in values.items():
        at, w = CONS[name]
        c[:, at:at + w] = v
    return c


def masks():
    c = np.zeros((P, NMASK), np.float32)
    h, t = np.divmod(np.arange(P), CT)
    same, before = h[:, None] == h[None, :], t[:, None] > t[None, :]
    u = np.arange(CT)[None, :]
    values = dict(ist=t[:, None] == u, seqm=t[:, None] // TS == np.arange(NS)[None, :])
    for n, block, chunk in ((0, SB, CT), (1, TS, TS)):
        near = t[:, None] // block == t[None, :] // block
        within = t[:, None] // chunk == t[None, :] // chunk
        d = same & before & near
        low = same & before & within
        values |= {f"d{n}": d, f"dt{n}": d.T, f"et{n}": (low & ~near).T, f"ak{n}": low.T,
                   f"r{n}": (t[:, None] <= u) & (t[:, None] // chunk == u // chunk),
                   f"scan{n}": np.broadcast_to(np.tile(np.arange(CT) % chunk != 0, 4), (P, 4 * CT))}
    for name, v in values.items():
        at, w = MASKS[name]
        c[:, at:at + w] = v
    return c


def outputs():
    return dict(x=((P, KD, T), "float32"), conv_ffn=((DEPTH, P, KF, 2 + 2 * NS), "float32"),
                conv_mix=((P, KD, 2 + 2 * NS), "float32"), k=((P, KD, T), "float32"), v=((P, KD, T), "float32"),
                logf=((16, T), "float32"), shift=((2, P, KD, 1 + NS), "float32"), wkvp=((2, P, KD, 64), "float32"),
                wkvs=((2, P, KD, NS, 64), "float32"))


def split_groups(a):
    return a[None, 0:TP], a[TP:T].reshape(NS, TS, -1)


def split_history(a):
    h = unrows(a)
    return h[None, 0:2], h[2:].reshape(NS, 2, -1)


def kernel(**inputs):
    import concourse.bacc as bacc
    from concourse.bass_utils import run_bass_kernel_spmd

    nc = bacc.Bacc("TRN2", target_bir_lowering=False, num_devices=1, dynamic_dma_scratch_size=1024)
    arrays = pack({k: np.asarray(v) for k, v in inputs.items()})
    ins = {k: nc.dram_tensor(f"in_{k}", a.shape, mybir.dt.from_np(a.dtype), kind="ExternalInput").ap()
           for k, a in arrays.items()}
    outs = {k: nc.dram_tensor(f"out_{k}", shape, mybir.dt.from_np(np.dtype(dt)), kind="ExternalOutput").ap()
            for k, (shape, dt) in outputs().items()}
    build_program(nc, ins, outs)
    results = run_bass_kernel_spmd(nc, [{f"in_{k}": a for k, a in arrays.items()}], core_ids=[0]).results[0]
    r = {k: results[f"out_{k}"] for k in outs}
    xp, xs = split_groups(unrows(r["x"]))
    kp, ks = split_groups(unrows(r["k"]))
    vp, vs = split_groups(unrows(r["v"]))
    fp, fs = split_groups(r["logf"].T)
    mp, ms = split_history(r["conv_mix"])
    cp, cs = zip(*(split_history(c) for c in r["conv_ffn"]))
    shift = np.stack([unrows(s) for s in r["shift"]])
    wkvp = r["wkvp"].reshape(2, 2, 64, KD, 64).transpose(0, 3, 1, 4, 2).reshape(2, 1, 2 * KD, 64, 64)
    wkvs = r["wkvs"].reshape(2, 2, 64, KD, NS, 64).transpose(0, 4, 3, 1, 5, 2).reshape(2, NS, 2 * KD, 64, 64)

    def heads(a):
        return np.ascontiguousarray(a.reshape(a.shape[:-1] + (16, 64))[None])

    return tuple(np.ascontiguousarray(o) for o in (
        xp, xs, wkvp, shift[:, 0:1], wkvs, shift[:, 1:], heads(kp), heads(vp), fp[None], heads(ks), heads(vs),
        fs[None], mp[None], ms[None], np.stack(cp), np.stack(cs)))
```

```python
from contextlib import ExitStack

import numpy as np

import concourse.bass as bass
from concourse import mybir

F32 = mybir.dt.float32
F32R = mybir.dt.float32r
I32 = mybir.dt.int32
ALU = mybir.AluOpType
ACT = mybir.ActivationFunctionType
AX = mybir.AxisListType

P = 128
D = 1024
KD = D // P
TP = 512
NS, TS = 8, 8
TSN = NS * TS
T = TP + TSN
HT = T // 2
FF = 2816
KF = FF // P
DEPTH = 4
RMS_EPS = 1e-6
CH = 8
RAWS, SPL = 4, 2
GW = 2 + TP + NS * (2 + TS)
GS = 2 + TP


def down_chunks():
    return [(k, min(CH, KF - k)) for k in range(0, KF, CH)]


KINDS = {"a": 27 + 8, "b": 33 + 8, "c": 24 + 8}
FFN_CHUNKS = 2 * KF + KD * len(down_chunks())
MIXERS = [("a", 0), ("b", 0), ("c", 0), ("a", 1)]


class Map:

    def __init__(self, at):
        self.at = at

    def take(self, n):
        at = self.at
        self.at += (n + 31) // 32 * 32
        return at


def params(depth=DEPTH):
    cols, at = {}, 0
    for n in range(depth):
        for name, w in (("gm", KD), ("gf", KD), ("fw", 3 * KF), ("fb", KF)):
            cols[name, n] = at
            at += w
    for n in range(2):
        for name, w in (("mu", 6 * KD), ("w0", KD), ("a0", KD), ("kk", KD), ("ka", KD), ("rk", KD), ("lg", KD),
                        ("lb", KD)):
            cols[name, n] = at
            at += w
    for name, w in (("qg", 1), ("kg", 1), ("fbias", 1), ("cw", 3 * KD)):
        cols[name, 0] = at
        at += w
    return cols, at


def const_columns():
    where, at = {}, 0
    for name, w in (("ones", P), ("ident", P), ("heads", P), ("tri", P), ("neg", P), ("hot", 18), ("m8", TSN),
                    ("seq", NS), ("negn", NS * TS), ("qm", TS), ("hs", 30),
                    ("hq", 16)):
        where[name] = (at, w)
        at += w
    return where, at


CONS, NCON = const_columns()
NEG = -1e30
MIX = [("r", 0), ("k", 2), ("v", 3), ("g1", 5), ("w1", 1), ("a1", 4)]
CT = 64
SB = 16
NBAT = 2 * KD + 2
DECAY = float(np.exp(-0.5))
GN_EPS = 64e-5


def mask_columns():
    where, at = {}, 0
    for name, w in (("d0", P), ("dt0", P), ("et0", P), ("ak0", P), ("r0", CT), ("d1", P), ("dt1", P), ("et1", P),
                    ("ak1", P), ("r1", CT), ("ist", CT), ("seqm", NS), ("scan0", 4 * CT), ("scan1", 4 * CT)):
        where[name] = (at, w)
        at += w
    return where, at


MASKS, NMASK = mask_columns()


def build_program(nc, I, O, mixers=MIXERS):
    depth = len(mixers)
    PC, NPAR = params()
    ctx = ExitStack()
    with ctx:
        m = Map((nc.sbuf_base + 31) // 32 * 32)

        def at(name, shape, dt, offset):
            return nc.alloc_sbuf_tensor_at(name, [P] + list(shape), dt, offset=offset)

        def sb(name, shape, dt=F32):
            return at(name, shape, dt, m.take(4 * int(np.prod(shape))))

        def sem(name):
            return ctx.enter_context(nc.semaphore(name))

        x = sb("x", [KD, T])
        xh_at = m.at
        xh, xl = sb("xh", [KD, T], F32R), sb("xl", [KD, T], F32R)
        raw = sb("raw", [RAWS, CH, P])
        wh, wl = sb("wh", [SPL, CH, P], F32R), sb("wl", [SPL, CH, P], F32R)
        con = sb("con", [NCON])
        ones, ident, heads = (con[:, CONS[k][0]:CONS[k][0] + P] for k in ("ones", "ident", "heads"))
        par = sb("par", [NPAR])
        qg8 = sb("qg8", [1])
        gneps = sb("gneps", [1])
        eps, warm, free = sb("eps", [1]), sb("warm", [1]), sb("free", [32])
        big = m.at
        f = Map(big)
        at_hh, at_hl = f.take(4 * KF * T), f.take(4 * KF * T)
        hh, hl = at("hh", [KF, T], F32R, at_hh), at("hl", [KF, T], F32R, at_hl)
        misc = f.at
        gate = at("gate", [2, GW], F32, f.take(8 * GW))
        conv = at("conv", [2, GW], F32, f.take(8 * GW))
        hf = at("hf", [T], F32, f.take(4 * T))
        sq = at("sq", [2, T], F32, f.take(8 * T))
        at_rstd = f.take(4 * T)
        rstd = at("rstd", [T], F32, at_rstd)
        co = at("co", [KF, 2 + 2 * NS], F32, f.take(4 * KF * (2 + 2 * NS)))
        cs = at("cs", [KF, 2 * NS], F32, f.take(4 * KF * 2 * NS))
        assert f.at <= nc.sbuf_usable_end, (f.at, nc.sbuf_usable_end)
        xt = at("xt", [2, T], F32, misc)

        b = Map(big)
        qk = at("qk", [2 * KD, T], F32, b.take(8 * KD * T))
        vg = at("vg", [2 * KD, T], F32, b.take(8 * KD * T))
        lf = at("lf", [T], F32, b.take(4 * T))
        lfc = at("lfc", [T], F32, b.take(4 * T))
        fq = at("fq", [4, 16], F32, b.take(4 * 64))
        col = at("col", [64], F32, b.take(256))
        pgs = at("pgs", [64], I32, b.take(256))
        KR = 4
        kv_ = Map(xh_at)
        kp, vp = at("kp", [KR, D], F32, kv_.take(4 * KR * D)), at("vp", [KR, D], F32, kv_.take(4 * KR * D))
        lfp = at("lfp", [NS, 8, 16], F32, kv_.take(4096))
        assert kv_.at <= xh_at + 8 * KD * T
        b1 = Map(b.at)
        qs, ks, vs = (at(k, [TP], F32, b1.take(4 * TP)) for k in ("qs", "ks", "vs"))
        vts = at("vts", [4, P], F32, b1.take(4 * TP))
        fm = at("fm", [2, TP], F32, b1.take(8 * TP))
        sc = at("sc", [2, 10 * P], F32, b1.take(80 * P))
        pt = at("pt", [2, 4, TP], F32, b1.take(32 * TP))
        qn, rn = at("qn", [2, T], F32, b.at), at("rn", [2, T], F32, b.at + 8 * T)
        b2 = Map(b.at)
        at_pm = b2.take(36 * P)
        pm, tot = at("pm", [9, P], F32, at_pm), at("tot", [NS, 8, 16], F32, at_pm)
        pts = at("pts", [9, P], F32, b2.take(36 * P))
        QD = P + 2 * TS
        qz = at("qz", [KD * QD], F32, b2.take(4 * KD * QD))
        nf = at("nf", [8, 16, TS], F32, b2.take(4 * 8 * P))
        nfn = at("nfn", [16, TS], F32, b2.take(4 * P))
        om = at("om", [16, 64], F32, b2.take(4 * D))
        vtn = at("vtn", [D], F32, b2.take(4 * D))
        fn = at("fn", [16], F32, b2.take(64))
        fw8 = at("fw8", [NS, 16], F32, b2.take(512))
        zn = at("zn", [16, TS], F32, b2.take(512))
        fqn = at("fqn", [NS], F32, b2.take(32))
        assert max(b1.at, b2.at) <= nc.sbuf_usable_end, (b1.at, b2.at, nc.sbuf_usable_end)

        a = Map(big)
        rkv = at("rkv", [3 * KD, T], F32, a.take(12 * KD * T))
        at_xn, at_dx = a.take(4 * KD * T), a.take(4 * KD * T)
        xn, dx = at("xn", [KD, T], F32, at_xn), at("dx", [KD, T], F32, at_dx)
        la = at("la", [T], F32, at_rstd)
        sg = at("sg", [T], F32, a.take(4 * T))
        sho = at("sho", [KD, 1 + NS], F32, a.take(4 * KD * (1 + NS)))
        shi = at("shi", [KD, NS], F32, a.take(4 * KD * NS))
        wkvo = at("wkvo", [KD, 64], F32, a.take(2048))
        w2s = at("w2s", [P], F32, a.take(512))
        NSCAN = 8 * CT
        scans = at("scans", [NSCAN], F32, a.take(4 * NSCAN))
        assert a.at <= misc
        a1 = Map(misc)
        zz = at("zz", [2, 4, CT], F32, a1.take(2048))
        spread16 = at("spread16", [16, 64], F32, a1.at)
        csum, cprev, pinv, pprev, kraw, kn, kh, kst, bb, t3 = (
            at("a_" + k, [4, CT], F32, a1.take(1024)) for k in
            "csum cprev pinv pprev kraw kn kh kst bb t3".split())
        sst, sp_, xb, ust = (at("a_" + k, [64], F32, a1.take(256)) for k in ("sst", "sp", "xb", "ust"))
        sbd, ubd = at("sbd", [2, 64], F32, a1.take(512)), at("ubd", [2, 64], F32, a1.take(512))
        assert a1.at <= at_rstd, a1.at - misc
        a2 = Map(at_rstd + 4 * T)
        lora2 = at("lora2", [2 * D], F32, a2.take(8 * D))
        msk = at("msk", [NMASK - NSCAN], F32, a2.take(4 * (NMASK - NSCAN)))
        assert a2.at <= nc.sbuf_usable_end, (a2.at, nc.sbuf_usable_end)
        slots = []
        for s_, where in enumerate((None, at_xn)):
            w = Map(xh_at if s_ == 0 else where)
            sl = {}
            for k in ("bda", "bdb", "bdk", "bdv", "m1", "m2", "m3", "m4", "m5", "m6", "et", "aak", "ktok", "vtok"):
                sl[k] = at(f"{k}{s_}", [4, 2, CT], F32, w.take(2048))
            sl["ar"] = at(f"ar{s_}", [4, 2, CT], F32, w.take(2048))
            for k in ("bst", "p", "arb", "ark", "vst"):
                sl[k] = at(f"{k}{s_}", [4, CT], F32, w.take(1024))
            sl["btok"] = sl["m6"]
            assert w.at <= (xh_at if s_ == 0 else where) + 8 * KD * T, w.at
            slots.append(sl)
        q_ = Map(at_xn)
        ss = at("ss", [KD, NS, 64], F32, q_.take(4 * KD * NS * 64))
        sb8 = at("sb8", [2, NS, 2, 64], F32, q_.take(8192))
        xq = at("xq", [NS, 64], F32, q_.take(2048))
        uq, vq = at("uq", [NS, 64], F32, q_.take(2048)), at("vq", [NS, 64], F32, q_.take(2048))

        ps = ctx.enter_context(nc.psum_tensor("ps", [P, 8 * 512], F32))

        def tile_cols(b):
            return b * 1024 + 512 - HT

        def pst(b, lo=0, hi=T):
            return ps[:, tile_cols(b) + lo:tile_cols(b) + hi]

        STAT = 2

        s_const, s_xin = sem("s_const"), sem("s_xin")
        s_raw = [sem(f"s_raw{i}") for i in range(RAWS)]
        s_hi, s_lo = sem("s_hi"), sem("s_lo")
        s_mm = sem("s_mm")
        s_ev = [sem("s_ev0"), sem("s_ev1")]
        s_rs, s_rr = sem("s_rs"), sem("s_rr")
        s_xt, s_xh, s_xl = sem("s_xt"), sem("s_xh"), sem("s_xl")
        s_sq, s_squ = sem("s_sq"), sem("s_squ")
        s_pad, s_t0, s_cv1, s_cv = sem("s_pad"), sem("s_t0"), sem("s_cv1"), sem("s_cv")
        s_si, s_hh, s_hl, s_cap = sem("s_si"), sem("s_hh"), sem("s_hl"), sem("s_cap")
        s_cs, s_co, s_out = sem("s_cs"), sem("s_co"), sem("s_out")
        s_seen = sem("s_seen")

        b_kd, b_vd = ([sem(f"b_{k}d{i}") for i in range(KR)] for k in "kv")
        (b_hsq, b_hsm, b_hrt, b_hrc, b_hn, b_f, b_ft, b_fe, b_qs, b_vtp, b_vts, b_fm, b_s, b_sc, b_mx,
         b_ex, b_rc, b_nm, b_tp, b_pt, b_pv, b_og, b_oxh, b_oxl, b_out, b_pg, b_lfp, b_pre, b_pr, b_pf, b_zn,
         b_qb, b_ks, b_st, b_stp, b_nb, b_nb1, b_sex, b_src, b_pn, b_ptp, b_pts, b_vs, b_ogs) = (
            sem("b_" + k) for k in (
                "hsq hsm hrt hrc hn f ft fe qs vtp vts fm s sc mx ex rc nm tp pt pv og oxh oxl out pg lfp pre "
                "pr pf zn qb ks st stp nb nb1 sex src pn ptp pts vs ogs").split())

        (a_ld, a_xn, a_dx, a_sh, a_w2, a_z, a_k1, a_k2, a_zz, a_kn, a_sg, a_cs, a_cm, a_kr, a_kv, a_kk, a_ex,
         a_kh, a_bb, a_ar, a_bk, a_bd, a_rk, a_bo, a_bon, a_p1, a_cx, a_xe, a_cu, a_ue, a_ub,
         a_cs2, a_sp, a_s, a_sb, a_co, a_oe, a_zh, a_sst, a_q, a_qa, a_qd, a_qp, a_qu, a_qs, a_qv, a_qe,
         a_g, a_gd, a_gm, a_gb, a_gc, a_gs, a_gq, a_gi, a_gr, a_gx, a_gl, a_ge, a_row, a_ss, a_out) = (
            sem("a_" + k) for k in (
                "ld xn dx sh w2 z k1 k2 zz kn sg cs cm kr kv kk ex kh bb ar bk bd rk bo bon p1 cx xe cu "
                "ue ub cs2 sp s sb co oe zh sst q qa qd qp qu qs qv qe "
                "g gd gm gb gc gs gq gi gr gx gl ge row ss out").split())

        a_A, a_D, a_m, a_e, a_d = ([sem(f"a_{k}{s_}") for s_ in range(2)] for k in "ADmed")

        class Ph:
            pass

        plan, c, n = {}, 0, 0
        conv0, hist_of, rows, loads = {}, {}, 0, 0
        NRES = 0
        NCONST = 2
        for layer, (kind, idx) in enumerate(mixers):
            names = []
            if kind == "a":
                names += [("r", 8, 8), ("k", 8, 8), ("v", 8, 8), ("g1", 1, 1), ("w1", 1, 1), ("a1", 1, 1)]
            elif kind == "b":
                names += [("qk", 16, 16), ("vg", 16, 16), ("f", 1, 1)]
            elif kind == "c":
                names += [("in", 24, 24)]
            if kind != "n":
                names += [("out", 8, 8)]
            names += [("up", 44, 44), ("down", 24, 8)]
            for name, nch, ntile in names:
                ph = Ph()
                ph.c0, ph.nch, ph.n0, ph.ntile = c, nch, n, ntile
                ph.res = NRES
                if name in ("out", "down"):
                    NRES += 1
                if name == "up" or (kind, name) == ("c", "in"):
                    conv0[layer, name], hist_of[layer, name] = rows, loads
                    rows, loads = rows + (KF if name == "up" else KD), loads + 1
                plan[layer, name] = ph
                c, n = c + nch, n + ntile
        NCHUNK = c
        n_norm, row0 = {}, {}
        q = r0 = 0
        for layer, (kind, _) in enumerate(mixers):
            if kind != "n":
                n_norm[layer, "mix"], row0[layer, "mix"] = q, r0
                q, r0 = q + 1, r0 + (len(MIX) if kind == "a" else 1) * KD
            n_norm[layer, "ffn"], row0[layer, "ffn"] = q, r0
            q, r0 = q + 1, r0 + KD
        def sq0(r):
            return KD + r * (1 + KD)

        def squ0(r):
            return KD + r * (2 + KD)

        def turns(n):
            return n // 2 + 1

        block = ctx.enter_context(nc.Block())

        def weights_in(sp, first, last):
            def load(c, i=0):
                if not isinstance(i, int) or c >= RAWS:
                    sp.wait_ge(s_lo, i * RAWS + c - RAWS + 1)
                src = I["w"][c] if isinstance(i, int) else I["w"][bass.ds(i * RAWS + c, 1)].rearrange("o p c -> p (o c)")
                sp.dma_start(raw[:, c % RAWS], src.rearrange("p (k c) -> p k c", c=P)).then_inc(s_raw[c % RAWS], 16)

            c = first
            while c < min(RAWS, last):
                load(c)
                c += 1
            n = (last - c) // RAWS
            if n > 1:
                with sp.Fori(0, n) as i:
                    for s in range(RAWS):
                        load(c + s, i)
                c += n * RAWS
            while c < last:
                load(c)
                c += 1

        def split_hi(act, c, i=0, step=0):
            if isinstance(i, int) and c + i * step >= NCHUNK:
                return
            act.wait_ge(s_raw[c % RAWS], i * (step // RAWS * 16) + 16 * (c // RAWS + 1))
            if c >= SPL:
                act.wait_ge(s_mm, i * step + c - SPL + 1)
            act.activation(wh[:, c % SPL], raw[:, c % RAWS], ACT.Copy).then_inc(s_hi, 1)

        def split_lo(dve, c, i=0, step=0):
            if isinstance(i, int) and c + i * step >= NCHUNK:
                return
            dve.wait_ge(s_hi, i * step + c + 1)
            dve.tensor_tensor(wl[:, c % SPL], raw[:, c % RAWS], wh[:, c % SPL].bitcast(F32),
                              ALU.subtract).then_inc(s_lo, 1)

        def chunk_mm(pe, c, n, rh, rl, k0=0, nk=CH, first=True, last=True, i=0, cstep=0, nstep=0, row_ready=None,
                     row_used=None):
            pe.wait_ge(s_lo, i * cstep + c + 1)
            if first:
                pe.wait_ge(s_ev[n % 2], i * (nstep // 2) + turns(n))
            for k in range(nk):
                if row_ready is not None:
                    pe.wait_ge(row_ready[0], row_ready[1] + k)
                for a in range(2):
                    out = pst(n % 2, a * HT, (a + 1) * HT)
                    rhs_h, rhs_l = rh[:, k0 + k, a * HT:(a + 1) * HT], rl[:, k0 + k, a * HT:(a + 1) * HT]
                    w_h, w_l = wh[:, c % SPL, k], wl[:, c % SPL, k]
                    pe.matmul(out, w_h, rhs_h, start=(first and k == 0), stop=False)
                    pe.matmul(out, w_h, rhs_l, start=False, stop=False)
                    mm = pe.matmul(out, w_l, rhs_h, start=False, stop=(last and k == nk - 1))
                if row_used is not None and k < nk - 1:
                    mm.then_inc(row_used, 1)
            mm.then_inc(s_mm, 1)

        def norm_dve(dve, q, r0, col):
            dve.wait_ge(s_rs, q + 1)
            dve.reciprocal(rstd[:], rstd[:]).then_inc(s_rr, 1)

            def lo(k):
                dve.wait_ge(s_xh, r0 + k + 1)
                dve.tensor_tensor(xl[:, k], xt[:, k % 2], xh[:, k].bitcast(F32), ALU.subtract).then_inc(s_xl, 1)

            dve.wait_ge(s_rr, q + 1)
            for k in range(KD):
                if k >= 2:
                    dve.wait_ge(s_xl, r0 + k - 1)
                dve.scalar_tensor_tensor(xt[:, k % 2], x[:, k], par[:, col + k:col + k + 1], rstd[:],
                                         ALU.mult, ALU.mult).then_inc(s_xt, 1)
                if k >= 1:
                    lo(k - 1)
            lo(KD - 1)

        def norm_act(act, q, r0):
            act.activation(warm[:], eps[:], ACT.Sqrt)
            act.wait_ge(s_squ, KD + q * (2 + KD))
            act.activation(rstd[:], pst(STAT), ACT.Sqrt, bias=eps[:], scale=1.0 / D).then_inc(s_rs, 1)
            for k in range(KD):
                act.wait_ge(s_xt, r0 + k + 1)
                act.activation(xh[:, k], xt[:, k % 2], ACT.Copy).then_inc(s_xh, 1)

        def square(act, k, count):
            if count > 0:
                act.wait_ge(s_squ, count)
            act.activation(sq[:, k % 2], x[:, k], ACT.Square).then_inc(s_sq, 1)

        def add_squares(pe, b, ready, start=False, stop=False):
            pe.wait_ge(s_sq, ready)
            for a in range(2):
                mm = pe.matmul(pst(STAT, a * HT, (a + 1) * HT), ones, sq[:, b, a * HT:(a + 1) * HT],
                               start=start, stop=stop)
            mm.then_inc(s_squ, 1)

        def rounds(eng, n, ph):
            if ph.c0 + ph.nch == NCHUNK:
                yield from range(n)
            else:
                with eng.Fori(0, n) as i:
                    yield i

        def res_act(act, ph, per):
            r = ph.res
            act.wait_ge(s_squ, squ0(r))
            act.activation(sq[:, 1], x[:, 0], ACT.Copy, scale=0.0).then_inc(s_sq, 1)
            for i in rounds(act, 2, ph):
                for j in range(4):
                    for e in range(per):
                        split_hi(act, ph.c0 + per * j + e + 2, i, 4 * per)
                    n = ph.n0 + j
                    act.wait_ge(s_ev[n % 2], i * 2 + turns(n) + 1)
                    act.wait_ge(s_squ, i * 4 + squ0(r) + j + 1)
                    act.activation(sq[:, j % 2:j % 2 + 1], x[:, bass.ds(i * 4 + j, 1)], ACT.Square)\
                        .then_inc(s_sq, 1)

        def res_dve(dve, ph, per):
            for i in rounds(dve, 2, ph):
                for j in range(4):
                    for e in range(per):
                        split_lo(dve, ph.c0 + per * j + e + 2, i, 4 * per)
                    n = ph.n0 + j
                    dve.wait_ge(s_mm, i * 4 * per + ph.c0 + per * (j + 1))
                    row = x[:, bass.ds(i * 4 + j, 1)]
                    dve.tensor_tensor(row, row, pst(n % 2).rearrange("p (o t) -> p o t", o=1), ALU.add)\
                        .then_inc(s_ev[n % 2], 1)

        def res_pe(pe, ph, per, rh, rl, ready, row_ready=None):
            r = ph.res
            parts = down_chunks() if per > 1 else [(0, CH)]
            add_squares(pe, 1, sq0(r) + 1, start=True)
            if ready:
                pe.wait_ge(*ready)
            for i in rounds(pe, 2, ph):
                for j in range(4):
                    for e, (k0, nk) in enumerate(parts):
                        chunk_mm(pe, ph.c0 + per * j + e, ph.n0 + j, rh, rl, k0, nk, e == 0, e == per - 1,
                                 i, 4 * per, 4, row_ready if j == 0 else None)
                    pe.wait_ge(s_sq, i * 4 + sq0(r) + 1 + j)
                    for a in range(2):
                        mm = pe.matmul(pst(STAT, a * HT, (a + 1) * HT), ones,
                                       sq[:, (j + 1) % 2, a * HT:(a + 1) * HT], start=False, stop=False)
                    mm.then_inc(s_squ, 1)
            add_squares(pe, 1, sq0(r) + 1 + KD, stop=True)

        def tok(ap, part):
            return ap[:, 0:TP] if part == 0 else ap[:, TP:T].rearrange("p (s t) -> p s t", t=TS)

        def hist(ap, part, back=0):
            if part == 0:
                return ap[:, 2 - back:2 - back + TP]
            return ap[:, GS:GW].rearrange("p (s t) -> p s t", t=2 + TS)[:, :, 2 - back:2 - back + TS]

        def one(ap):
            return ap.rearrange("p (o t) -> p o t", o=1)

        def up_act(act, layer):
            ph = plan[layer, "up"]
            fb, fw, up = PC["fb", layer], PC["fw", layer], conv0[layer, "up"]
            with act.Fori(0, KF // 2) as i:
                for u in range(2):
                    c, n, p = ph.c0 + 2 * u, ph.n0 + 2 * u, up + u
                    split_hi(act, c + 2, i, 4)
                    act.wait_ge(s_mm, i * 4 + c + 1)
                    act.wait_ge(s_pad, i * 2 + p + 1)
                    act.activation(gate[:, u, 2:GS], tok(pst(n % 2), 0), ACT.Copy)
                    act.activation(hist(gate[:, u], 1), tok(pst(n % 2), 1), ACT.Copy).then_inc(s_ev[n % 2], 1)
                    act.wait_ge(s_ev[n % 2], i * 2 + turns(n) + 1)
                    act.activation(conv[:, u, 2:GW], gate[:, u, 0:GW - 2], ACT.Identity,
                                   bias=par[:, bass.ds(i * 2 + fb + u, 1)],
                                   scale=par[:, bass.ds(i * 2 + fw + u, 1)]).then_inc(s_t0, 1)
                    act.wait_ge(s_cv, i * 2 + p + 3)
                    act.activation(conv[:, u, 2:GW], conv[:, u, 2:GW], ACT.Silu).then_inc(s_si, 1)
                    split_hi(act, c + 3, i, 4)
                    act.wait_ge(s_ev[(n + 1) % 2], i * 2 + turns(n + 1) + 1)
                    act.activation(hh[:, bass.ds(i * 2 + u, 1)], one(hf[:]), ACT.Copy).then_inc(s_hh, 1)

        def up_dve(dve, layer):
            ph = plan[layer, "up"]
            fw, up = PC["fw", layer], conv0[layer, "up"]
            with dve.Fori(0, KF // 2) as i:
                for u in range(2):
                    c, n, p = ph.c0 + 2 * u, ph.n0 + 2 * u, up + u
                    split_lo(dve, c + 2, i, 4)
                    dve.wait_ge(s_t0, i * 2 + p + 1)
                    dve.scalar_tensor_tensor(conv[:, u, 2:GW], gate[:, u, 1:GW - 1],
                                             par[:, bass.ds(i * 2 + fw + KF + u, 1)], conv[:, u, 2:GW],
                                             ALU.mult, ALU.add).then_inc(s_cv1, 1)
                    dve.wait_ge(s_cv1, i * 2 + p + 1)
                    dve.scalar_tensor_tensor(conv[:, u, 2:GW], gate[:, u, 2:GW],
                                             par[:, bass.ds(i * 2 + fw + 2 * KF + u, 1)], conv[:, u, 2:GW],
                                             ALU.mult, ALU.add).then_inc(s_cv, 1)
                    dve.wait_ge(s_mm, i * 4 + c + 2)
                    dve.wait_ge(s_si, i * 2 + layer * KF + u + 1)
                    dve.tensor_tensor(tok(hf[:], 0), hist(conv[:, u], 0), tok(pst((n + 1) % 2), 0), ALU.mult)
                    dve.tensor_tensor(tok(hf[:], 1), hist(conv[:, u], 1), tok(pst((n + 1) % 2), 1),
                                      ALU.mult).then_inc(s_ev[(n + 1) % 2], 1)
                    split_lo(dve, c + 3, i, 4)
                    dve.wait_ge(s_hh, i * 2 + p + 1)
                    dve.tensor_tensor(hl[:, bass.ds(i * 2 + u, 1)], one(hf[:]),
                                      hh[:, bass.ds(i * 2 + u, 1)].bitcast(F32),
                                      ALU.subtract).then_inc(s_hl, 1)

        def conv_pool(pool, layer, name, normed):
            ph, r0, load = plan[layer, name], conv0[layer, name], hist_of[layer, name]
            per = 2 if name == "up" else 3
            pool.wait_ge(s_xl, normed + KD)
            pool.wait_ge(s_cs, 16 * (load + 1))
            if load:
                pool.wait_ge(s_co, 16 * load)
            with pool.Fori(0, (KF if name == "up" else KD) // 2) as i:
                for u in range(2):
                    n, r = ph.n0 + per * u + per - 2, r0 + u
                    g = gate[:, u, GS:GW].rearrange("p (s t) -> p s t", t=2 + TS)
                    pool.wait_ge(s_cv, i * 2 + r + 1)
                    pool.sem_inc(s_seen, 1)
                    pool.memset(gate[:, u, 0:2], 0.0)
                    pool.tensor_copy(g[:, :, 0:2], cs[:, bass.ds(i * 2 + u, 1)]
                                     .rearrange("p o (s t) -> p (o s) t", t=2)).then_inc(s_pad, 1)
                    pool.wait_ge(s_ev[n % 2], i * per + turns(n) + 1)
                    pool.sem_inc(s_seen, 1)
                    pool.tensor_copy(co[:, bass.ds(i * 2 + u, 1), 0:2], one(gate[:, u, GS - 2:GS]))
                    pool.tensor_copy(co[:, bass.ds(i * 2 + u, 1), 2:].rearrange("p o (s t) -> p (o s) t", t=2),
                                     g[:, :, TS:TS + 2]).then_inc(s_cap, 1)

        def convmix_act(act, layer):
            ph, fw, r0 = plan[layer, "in"], PC["cw", 0], conv0[layer, "in"]
            with act.Fori(0, 2) as i:
                for j in range(4):
                    c, n, r, u = ph.c0 + 3 * j, ph.n0 + 3 * j, r0 + j, j % 2
                    split_hi(act, c + 2, i, 12)
                    act.wait_ge(s_mm, i * 12 + c + 1)
                    act.activation(sq[:, u], pst(n % 2), ACT.Copy).then_inc(s_ev[n % 2], 1)
                    split_hi(act, c + 3, i, 12)
                    act.wait_ge(s_ev[(n + 1) % 2], i * 6 + turns(n + 1) + 1)
                    act.activation(conv[:, u, 2:GW], gate[:, u, 0:GW - 2], ACT.Copy,
                                   scale=par[:, bass.ds(i * 4 + fw + j, 1)]).then_inc(s_t0, 1)
                    split_hi(act, c + 4, i, 12)
                    act.wait_ge(s_ev[(n + 2) % 2], i * 6 + turns(n + 2) + 1)
                    act.activation(hh[:, bass.ds(i * 4 + j, 1)], one(hf[:]), ACT.Copy).then_inc(s_hh, 1)

        def convmix_dve(dve, layer):
            ph, fw, r0 = plan[layer, "in"], PC["cw", 0], conv0[layer, "in"]
            with dve.Fori(0, 2) as i:
                for j in range(4):
                    c, n, r, u = ph.c0 + 3 * j, ph.n0 + 3 * j, r0 + j, j % 2
                    split_lo(dve, c + 2, i, 12)
                    dve.wait_ge(s_mm, i * 12 + c + 2)
                    dve.wait_ge(s_pad, i * 4 + r + 1)
                    dve.wait_ge(s_ev[n % 2], i * 6 + turns(n) + 1)
                    for part in range(2):
                        mul = dve.tensor_tensor(hist(gate[:, u], part), tok(sq[:, u], part),
                                                tok(pst((n + 1) % 2), part), ALU.mult)
                    mul.then_inc(s_ev[(n + 1) % 2], 1)
                    split_lo(dve, c + 3, i, 12)
                    dve.wait_ge(s_t0, i * 4 + r + 1)
                    dve.scalar_tensor_tensor(conv[:, u, 2:GW], gate[:, u, 1:GW - 1],
                                             par[:, bass.ds(i * 4 + fw + KD + j, 1)], conv[:, u, 2:GW],
                                             ALU.mult, ALU.add).then_inc(s_cv1, 1)
                    dve.wait_ge(s_cv1, i * 4 + r + 1)
                    dve.scalar_tensor_tensor(conv[:, u, 2:GW], gate[:, u, 2:GW],
                                             par[:, bass.ds(i * 4 + fw + 2 * KD + j, 1)], conv[:, u, 2:GW],
                                             ALU.mult, ALU.add).then_inc(s_cv, 1)
                    dve.wait_ge(s_mm, i * 12 + c + 3)
                    dve.wait_ge(s_cv, i * 4 + r + 3)
                    for part in range(2):
                        mul = dve.tensor_tensor(tok(hf[:], part), hist(conv[:, u], part),
                                                tok(pst((n + 2) % 2), part), ALU.mult)
                    mul.then_inc(s_ev[(n + 2) % 2], 1)
                    split_lo(dve, c + 4, i, 12)
                    dve.wait_ge(s_hh, i * 4 + r + 1)
                    dve.tensor_tensor(hl[:, bass.ds(i * 4 + j, 1)], one(hf[:]),
                                      hh[:, bass.ds(i * 4 + j, 1)].bitcast(F32), ALU.subtract).then_inc(s_hl, 1)

        def rows_pe(pe, ph, r0, per):
            with pe.Fori(0, ph.nch // per) as i:
                for e in range(per):
                    chunk_mm(pe, ph.c0 + e, ph.n0 + e, xh, xl, i=i, cstep=per, nstep=per,
                             row_ready=(s_xl, r0 + 1) if e == 0 else None)

        def bank(n, w=512):
            return ps[:, n * 512:n * 512 + w]

        def mview(name, n=None):
            at_, w = MASKS[name if n is None else f"{name}{n}"]
            return scans[:, at_ - NMASK + NSCAN:at_ - NMASK + NSCAN + w] if name == "scan" else msk[:, at_:at_ + w]

        def a_norm_act(act, layer, j):
            q = n_norm[layer, "mix"]
            act.activation(warm[:], eps[:], ACT.Sqrt)
            act.wait_ge(s_squ, KD + q * (2 + KD))
            act.activation(rstd[:], pst(STAT), ACT.Sqrt, bias=eps[:], scale=1.0 / D).then_inc(s_rs, 1)
            if hist_done(layer):
                act.wait_ge(s_pad, rows_done(layer))
            act.dma_start(msk[:], I["masks"][:, 0:NMASK - NSCAN]).then_inc(a_ld, 16)
            act.dma_start(scans[:], I["masks"][:, NMASK - NSCAN:]).then_inc(a_ld, 16)
            act.dma_start(lora2[:], I["lora2"][j]).then_inc(a_ld, 16)
            act.dma_start(shi[:], I["shift"][j]).then_inc(a_ld, 16)

        def hist_done(layer):
            return sum(1 for (l, _) in hist_of if l < layer)

        def rows_done(layer):
            return sum((KF if name == "up" else KD) for (l, name) in hist_of if l < layer)

        def a_norm_dve(dve, layer, j):
            q, col_ = n_norm[layer, "mix"], PC["gm", layer]
            dve.wait_ge(s_rs, q + 1)
            dve.reciprocal(rstd[:], rstd[:]).then_inc(s_rr, 1)
            dve.wait_ge(s_rr, q + 1)
            for k in range(KD):
                dve.scalar_tensor_tensor(xn[:, k], x[:, k], par[:, col_ + k:col_ + k + 1], rstd[:],
                                         ALU.mult, ALU.mult).then_inc(a_xn, 1)
            for k in range(KD):
                dve.wait_ge(a_xn, KD * j + k + 1)
                dve.tensor_tensor(dx[:, k, 1:T], xn[:, k, 0:T - 1], xn[:, k, 1:T], ALU.subtract).then_inc(a_dx, 1)
            dve.wait_ge(a_dx, (KD + 2) * j + KD)
            dve.tensor_scalar(dx[:, :, 0], xn[:, :, 0], -1.0, None, ALU.mult).then_inc(a_dx, 1)
            dve.wait_ge(a_ld, 64 * (j + 1))
            starts = xn[:, :, TP:T].rearrange("p k (s t) -> p k s t", t=TS)
            dve.tensor_tensor(dx[:, :, TP:T].rearrange("p k (s t) -> p k s t", t=TS)[:, :, :, 0], shi[:],
                              starts[:, :, :, 0], ALU.subtract).then_inc(a_dx, 1)
            dve.tensor_copy(sho[:, :, 0:1], xn[:, :, TP - 1:TP]).then_inc(a_sh, 1)
            dve.tensor_copy(sho[:, :, 1:], starts[:, :, :, TS - 1]).then_inc(a_sh, 1)
            dve.wait_ge(a_dx, (KD + 2) * (j + 1))

        def mix_rows_dve(dve, layer, j, n):
            r0 = row0[layer, "mix"] + n * KD

            def lo(k):
                dve.wait_ge(s_xh, r0 + k + 1)
                dve.tensor_tensor(xl[:, k], xt[:, k % 2], xh[:, k].bitcast(F32), ALU.subtract).then_inc(s_xl, 1)

            for k in range(KD):
                if k >= 2 or n:
                    dve.wait_ge(s_xl, r0 + k - 1)
                mu = PC["mu", j] + MIX[n][1] * KD + k
                dve.scalar_tensor_tensor(xt[:, k % 2], dx[:, k], par[:, mu:mu + 1], xn[:, k],
                                         ALU.mult, ALU.add).then_inc(s_xt, 1)
                if k >= 1:
                    lo(k - 1)
            lo(KD - 1)

        def mix_rows_act(act, layer, j, n):
            r0 = row0[layer, "mix"] + n * KD
            for k in range(KD):
                act.wait_ge(s_xt, r0 + k + 1)
                if n and k < KD - 1:
                    act.wait_ge(a_row, ((len(MIX) - 1) * j + n - 1) * (KD - 1) + k + 1)
                elif n:
                    before = plan[layer, MIX[n - 1][0]]
                    act.wait_ge(s_mm, before.c0 + before.nch)
                act.activation(xh[:, k], xt[:, k % 2], ACT.Copy).then_inc(s_xh, 1)

        def mixes(eng, layer, j, mix_rows, chunk):
            mix_rows(eng, layer, j, 0)
            for n, (name, _) in enumerate(MIX):
                ph = plan[layer, name]
                for k in range(ph.nch):
                    if k == ph.nch - 1 and n + 1 < len(MIX):
                        mix_rows(eng, layer, j, n + 1)
                    chunk(eng, ph, n, name, k)

        def mix_chunk_dve(dve, ph, n, name, k):
            split_lo(dve, ph.c0 + k + 2)

        def mix_chunk_act(act, ph, n, name, k):
            m_ = ph.n0 + k
            split_hi(act, ph.c0 + k + 2)
            act.wait_ge(s_mm, ph.c0 + k + 1)
            if name == "g1":
                op = act.activation(sg[:], pst(m_ % 2), ACT.Sigmoid)
            elif name == "w1":
                op = act.activation(la[0:64], pst(m_ % 2)[0:64], ACT.Tanh)
            elif name == "a1":
                op = act.activation(la[64:P], pst(m_ % 2)[64:P], ACT.Copy)
            else:
                op = act.activation(rkv[:, n * KD + k], pst(m_ % 2), ACT.Copy)
            op.then_inc(s_ev[m_ % 2], 1)

        def mix_pe(pe, layer, n):
            ph = plan[layer, MIX[n][0]]
            r0 = row0[layer, "mix"] + n * KD
            for k in range(ph.nch):
                chunk_mm(pe, ph.c0 + k, ph.n0 + k, xh, xl, row_ready=(s_xl, r0 + 1) if k == 0 else None,
                         row_used=a_row if k == ph.nch - 1 and n + 1 < len(MIX) else None)

        class Bat:
            def __init__(self, j, s, i=None, off=0):
                self.j, self.b, self.i, self.off, self.prompt = j, s, i, off, i is not None
                self.s = s if self.prompt else 0
                self.const = NBAT * j + (2 * off + s if self.prompt else 2 * KD + s)
                self.last = 2 if self.prompt or s == 0 else 1

            def cnt(self, n, k):
                return self.i * (2 * n) + n * self.const + k if self.prompt else n * self.const + k

            def own(self, which, k):
                n, ns = COUNTS[which]
                a_layer = KD * n + 2 * ns if self.s == 0 else KD * n
                if self.prompt:
                    return self.i * n + a_layer * self.j + n * self.off + k
                return a_layer * self.j + KD * n + ns * self.b + k

            def tile(self, n, k):
                return self.i * n + n * (KD * self.j + self.off) + k

            def row(self, t, first):
                if self.prompt:
                    lo = self.s * 4 * CT
                    return t[:, bass.ds(self.i + (self.off + first), 1), lo:lo + 4 * CT].rearrange("p o (c t) -> p (o c) t", t=CT)
                return t[:, first + 4 * self.b:first + 4 * self.b + 4, TP:T]

            def per(self, c0):
                if self.prompt:
                    return par[:, bass.ds(self.i + (self.off + c0), 1)].to_broadcast([P, 4 * CT])\
                        .rearrange("p (c t) -> p c t", t=CT)
                return par[:, c0 + 4 * self.b:c0 + 4 * self.b + 4].unsqueeze(2).to_broadcast([P, 4, CT])

        def flat(t):
            return t.rearrange("p a b -> p (a b)")

        two_heads = heads.rearrange("p (h t) -> p h t", h=2)

        PIECES = 10

        def apart(eng, to, src):
            return eng.tensor_tensor(to[:], src.unsqueeze(2).to_broadcast([P, 4, 2, CT]),
                                     two_heads.unsqueeze(1).to_broadcast([P, 4, 2, CT]), ALU.mult)

        def prep_pe(pe, B, piece):
            if piece == 0:
                pe.wait_ge(a_bon, B.cnt(1, 1))
                if B.prompt:
                    pe.wait_ge(a_w2, B.tile(1, 1))
                for h in range(2):
                    rows_ = slice(64 * h, 64 * h + 64)
                    if B.prompt:
                        mm = pe.matmul(bank(7)[:, h * 256:h * 256 + 256], w2s[rows_],
                                       la[rows_, B.s * 256:B.s * 256 + 256], start=True, stop=True)
                    else:
                        for p in range(4):
                            w0 = (4 * B.b + p) * P
                            mm = pe.matmul(bank(7)[:, h * 256 + p * CT:h * 256 + (p + 1) * CT],
                                           lora2[rows_, w0:w0 + P], la[rows_, TP:T], start=True, stop=True)
                    if h == 0:
                        mm.then_inc(a_zh, 1)
                        pe.wait_ge(a_zh, B.cnt(1, 1))
                mm.then_inc(a_z, 1)
            if piece == 2:
                pe.wait_ge(a_zz, B.cnt(1, 1))
                pe.wait_ge(a_k2, B.cnt(1, 1))
                pe.matmul(bank(7, 256), heads, flat(kn[:]), start=True, stop=True).then_inc(a_kn, 1)
            if piece == 7:
                pe.wait_ge(a_kr, B.cnt(1, 1))
                pe.wait_ge(a_rk, B.cnt(2, 2))
                pe.matmul(bank(7, 256), heads, flat(t3[:]), start=True, stop=True).then_inc(a_bo, 1)

        def prep_dve(dve, B, piece):
            sl, j = slots[B.s], B.j
            if piece == 0:
                dve.wait_ge(a_bd, B.cnt(1, 1))
                dve.tensor_tensor(kraw[:], B.row(rkv, KD), B.per(PC["kk", j]), ALU.mult).then_inc(a_k1, 1)
            if piece == 1:
                dve.wait_ge(a_z, B.cnt(1, 2))
                z = bank(7).rearrange("p (h c t) -> p h c t", h=2, t=CT)
                dve.tensor_tensor(zz[:, 0], z[:, 0], B.per(PC["w0", j]), ALU.add)
                dve.tensor_tensor(zz[:, 1], z[:, 1], B.per(PC["a0", j]), ALU.add).then_inc(a_zz, 1)
            if piece == 3:
                dve.wait_ge(a_sg, B.cnt(1, 1))
                dve.tensor_tensor_scan(flat(csum[:]), mview("scan", 0 if B.prompt else 1), flat(zz[:, 0]), 0.0,
                                       ALU.mult, ALU.add).then_inc(a_cs, 1)
            if piece == 4:
                dve.wait_ge(a_kr, B.cnt(1, 1))
                dve.tensor_scalar(kn[:], kn[:], 1e-12, None, ALU.max).then_inc(a_kv, 1)
                dve.wait_ge(a_kv, B.cnt(2, 1))
                dve.reciprocal(kn[:], kn[:]).then_inc(a_kv, 1)
            if piece == 5:
                dve.scalar_tensor_tensor(t3[:], zz[:, 1], -1.0, B.per(PC["ka", j]), ALU.add, ALU.mult)\
                    .then_inc(a_kh, 1)
                dve.wait_ge(a_kv, B.cnt(2, 2))
                dve.tensor_tensor(kraw[:], kraw[:], kn[:], ALU.mult).then_inc(a_kk, 1)
                dve.wait_ge(a_kh, B.cnt(2, 1))
                dve.scalar_tensor_tensor(kh[:], t3[:], 1.0, B.row(rkv, KD), ALU.add, ALU.mult).then_inc(a_kh, 1)
            if piece == 6:
                dve.wait_ge(a_kh, B.cnt(2, 2))
                dve.tensor_tensor(t3[:], B.row(rkv, 0), kh[:], ALU.mult).then_inc(a_rk, 1)
                dve.wait_ge(a_ex, B.cnt(3, 2))
                dve.tensor_tensor(kst[:], kh[:], pinv[:], ALU.mult).then_inc(a_bk, 1)
                dve.wait_ge(a_rk, B.cnt(2, 1))
                dve.tensor_tensor(t3[:], t3[:], B.per(PC["rk", j]), ALU.mult).then_inc(a_rk, 1)
            if piece == 8:
                dve.wait_ge(a_bo, B.cnt(1, 1))
                dve.tensor_tensor(B.row(rkv, KD), bank(7, 256).rearrange("p (c t) -> p c t", t=CT),
                                  B.row(rkv, 2 * KD), ALU.mult).then_inc(a_bon, 1)
            if piece == 9:
                dve.wait_ge(a_co, B.cnt(4, 9 - 4 * B.last))
                dve.wait_ge(a_kk, B.cnt(1, 1))
                dve.scalar_tensor_tensor(sl["ar"][:, :, 0], kraw[:], -1.0, pprev[:], ALU.mult, ALU.mult)
                dve.wait_ge(a_bb, B.cnt(1, 1))
                dve.tensor_tensor(sl["bst"][:], bb[:], pinv[:], ALU.mult).then_inc(a_bk, 1)
                dve.wait_ge(a_ex, B.cnt(3, 3))
                dve.tensor_tensor(sl["ar"][:, :, 1], B.row(rkv, 0), sl["p"][:], ALU.mult).then_inc(a_ar, 1)
                dve.wait_ge(a_bk, B.cnt(2, 2))
                apart(dve, sl["bdb"], sl["bst"][:])
                dve.wait_ge(a_ar, B.cnt(2, 1))
                apart(dve, sl["bda"], sl["ar"][:, :, 0]).then_inc(a_ar, 1)

        def prep_act(act, B, piece):
            sl = slots[B.s]
            if piece == 1:
                act.wait_ge(a_k1, B.cnt(1, 1))
                act.activation(kn[:], kraw[:], ACT.Square).then_inc(a_k2, 1)
            if piece == 2:
                act.wait_ge(a_zz, B.cnt(1, 1))
                act.activation(zz[:], zz[:], ACT.Sigmoid).then_inc(a_sg, 1)
            if piece == 3:
                act.wait_ge(a_kn, B.cnt(1, 1))
                act.activation(flat(kn[:]), bank(7, 256), ACT.Sqrt).then_inc(a_kr, 1)
            if piece == 4:
                act.wait_ge(a_cs, B.cnt(1, 1))
                act.activation(pinv[:], csum[:], ACT.Exp, scale=DECAY).then_inc(a_ex, 1)
                act.wait_ge(a_cm, B.cnt(1, 1))
                act.activation(pprev[:], cprev[:], ACT.Exp, scale=-DECAY).then_inc(a_ex, 1)
            if piece == 9:
                act.wait_ge(a_co, B.cnt(4, 9 - 4 * B.last))
                if B.prompt:
                    act.wait_ge(a_sst, B.tile(2, B.s + 1))
                elif B.b == 0:
                    act.wait_ge(a_sst, 2 * KD * (B.j + 1) + 1)
                else:
                    act.wait_ge(a_qe, 2 * tile_no(B, 0))
                act.activation(sl["p"][:], csum[:], ACT.Exp, scale=-DECAY).then_inc(a_ex, 1)

        def prep_pool(pool, B, piece):
            sl = slots[B.s]

            def seen(s, v):
                pool.wait_ge(s, v)
                pool.sem_inc(s_seen, 1)

            if piece == 0 and B.prompt and B.s == 0:
                seen(a_z, B.cnt(1, 1))
                pool.tensor_copy(w2s[:].unsqueeze(1), lora2[:, 0:D].rearrange("p (k c) -> p k c", c=P)
                                 [:, bass.ds(B.i + B.off, 1)]).then_inc(a_w2, 1)
            if piece == 3:
                seen(a_cs, B.cnt(1, 1))
                pool.tensor_tensor(cprev[:], csum[:], zz[:, 0], ALU.subtract).then_inc(a_cm, 1)
            if piece == 5:
                seen(a_kk, B.cnt(1, 1))
                pool.tensor_tensor(bb[:], kraw[:], zz[:, 1], ALU.mult).then_inc(a_bb, 1)
            if piece == 9:
                seen(a_bk, B.cnt(2, 1))
                seen(a_co, B.cnt(4, 9 - 4 * B.last))
                apart(pool, sl["bdv"], B.row(rkv, 2 * KD))
                apart(pool, sl["bdk"], kst[:]).then_inc(a_bd, 1)

        def sq_(sl, k, p):
            return sl[k][:, p].rearrange("p a b -> p (a b)")

        INV = dict(
            d2=("m2", "m1", 0, None, "m3", ()),
            d2t=("m1", "m2", 1, None, "m4", ()),
            p4=("m4", "m5", 2, "m5", "m6", ("d2t",)),
            d4=("m4", "m3", 0, None, "m1", ("d2t",)),
            d4t=("m3", "m4", 1, "", "m2", ("d2t",)),
            p8=("m2", "m6", 2, "m6", "m5", ("d4t", "p4")),
            d8t=("m1", "m2", 0, None, "m4", ("d4t", "d4")),
            ktok=("bdk", None, 2, None, "ktok", ("p8",)),
            p16=("m4", "m5", 1, "m5", "m6", ("d8t", "p8")),
            vtok=("bdv", None, 2, None, "vtok", ("ktok",)),
            k=("et", "m6", 0, None, "m1", ("p16",)),
            t=("m6", None, 2, None, "m2", ("vtok", "p16")),
            r2=("m1", "m2", 1, "m2", "m5", ("t",)),
            vst=("bdv", "ist", 2, None, "vst", ("t",)),
            r3=("m1", "m5", 0, "m2", "m3", ("r2",)),
            btok=("bdb", None, 2, None, "btok", ("vst",)),
            r4=("m1", "m3", 1, "m2", "m5", ("r3",)),
        )
        INV_8 = {name: INV[name] for name in ("d2", "d2t", "p4", "d4t", "p8")} | dict(
            ktok=("bdk", None, 0, None, "ktok", ("d4t",)),
            t=("m5", None, 1, None, "m5", ("p8",)),
            vtok=("bdv", None, 2, None, "vtok", ("p8",)),
            btok=("bdb", None, 0, None, "btok", ("ktok",)),
            vst=("bdv", "ist", 1, None, "vst", ("t",)),
        )

        def steps_of(prompt):
            inv = INV if prompt else INV_8
            return inv, list(inv), [n for n in inv if inv[n][3] is None], [n for n in inv if inv[n][3] is not None]

        COUNTS = dict(A=(3, 3), D=(6, 6)) | {
            which: tuple(len(steps_of(prompt)[at_]) for prompt in (True, False)) for which, at_ in
            (("m", 1), ("e", 2), ("d", 3))}

        def inv_pe(pe, B, k):
            sl, b0 = slots[B.s], 3 * B.s
            if k == 0:
                pe.wait_ge(a_bd, B.cnt(1, 2))
                pe.wait_ge(a_oe, B.cnt(1, 3 - B.last))
                pe.wait_ge(a_ar, B.cnt(2, 2))
                for n, (l_, r_) in enumerate((("bda", "bst"), ("bdb", "ar"), ("bdk", "ar"))):
                    w = CT if n == 0 else P
                    for p in range(4):
                        rhs = sl["bst"][:, p] if n == 0 else sq_(sl, "ar", p)
                        mm = pe.matmul(bank(b0 + n)[:, p * w:(p + 1) * w], sq_(sl, l_, p), rhs, start=True, stop=True)
                    mm.then_inc(a_A[B.s], 1)
                return
            inv, order, copies, adds = steps_of(B.prompt)
            if k > len(order):
                return
            name = order[k - 1]
            left, right, bk, _, _, needs = inv[name]
            if name == "d2":
                pe.wait_ge(a_D[B.s], B.own("D", 2))
            if name == "d2t":
                pe.wait_ge(a_D[B.s], B.own("D", 4))
            if name == "p4":
                pe.wait_ge(a_p1, B.cnt(1, 1))
                pe.wait_ge(a_D[B.s], B.own("D", 6))
            for need in needs:
                if need in copies:
                    pe.wait_ge(a_e[B.s], B.own("e", copies.index(need) + 1))
                else:
                    pe.wait_ge(a_d[B.s], B.own("d", adds.index(need) + 1))
            for p in range(4):
                out = bank(b0 + bk)[:, p * P:(p + 1) * P]
                if right is None:
                    mm = pe.transpose(out, sq_(sl, left, p), ident)
                elif right == "ist":
                    mm = pe.matmul(bank(b0 + bk)[:, p * CT:(p + 1) * CT], sq_(sl, left, p), mview("ist"),
                                   start=True, stop=True)
                else:
                    mm = pe.matmul(out, sq_(sl, left, p), sq_(sl, right, p), start=True, stop=True)
            mm.then_inc(a_m[B.s], 1)

        def inv_act(act, B, k):
            sl, b0 = slots[B.s], 3 * B.s
            inv, order, copies, _ = steps_of(B.prompt)
            if k == 0 or k > len(order) or order[k - 1] not in copies:
                return
            name = order[k - 1]
            _, right, bk, _, to, _ = inv[name]
            act.wait_ge(a_m[B.s], B.own("m", k))
            if name == "d4":
                act.wait_ge(a_p1, B.cnt(1, 1))
            if right == "ist":
                act.activation(flat(sl[to][:]), bank(b0 + bk, 4 * CT), ACT.Copy).then_inc(a_e[B.s], 1)
            else:
                act.activation(sl[to][:].rearrange("p a b c -> p (a b c)"), bank(b0 + bk), ACT.Copy)\
                    .then_inc(a_e[B.s], 1)

        def inv_dve(dve, B, k):
            sl, b0, n = slots[B.s], 3 * B.s, 0 if B.prompt else 1
            if k == 0:
                def spread(name):
                    return mview(name, n).rearrange("p (h t) -> p h t", h=2).unsqueeze(1).to_broadcast([P, 4, 2, CT])

                def twice(src):
                    return src.unsqueeze(2).to_broadcast([P, 4, 2, CT])

                left = bank(b0, 4 * CT).rearrange("p (c t) -> p c t", t=CT)
                rb, rk_ = (bank(b0 + q).rearrange("p (c w t) -> p c w t", w=2, t=CT) for q in (1, 2))
                mr = mview("r", n).unsqueeze(1).to_broadcast([P, 4, CT])
                for need, out, src, mask in ((1, "m1", twice(left), spread("d")),
                                             (2, "m2", twice(rb[:, :, 0]), spread("dt")),
                                             (2, "et", twice(rb[:, :, 0]), spread("et")),
                                             (2, "arb", rb[:, :, 1], mr),
                                             (3, "aak", twice(rk_[:, :, 0]), spread("ak")),
                                             (3, "ark", rk_[:, :, 1], mr)):
                    dve.wait_ge(a_A[B.s], B.own("A", need))
                    dve.tensor_tensor(sl[out][:], src, mask, ALU.mult).then_inc(a_D[B.s], 1)
                return
            inv, order, _, adds = steps_of(B.prompt)
            if k <= len(order) and order[k - 1] in adds:
                _, _, bk, add, to, _ = inv[order[k - 1]]
                dve.wait_ge(a_m[B.s], B.own("m", k))
                out = sl[to][:].rearrange("p a b c -> p (a b c)")
                if add:
                    op = dve.tensor_tensor(out, bank(b0 + bk), sl[add][:].rearrange("p a b c -> p (a b c)"), ALU.add)
                else:
                    op = dve.tensor_copy(out, bank(b0 + bk))
                op.then_inc(a_d[B.s], 1)

        def inv_pool(pool, B, k):
            sl = slots[B.s]
            if k != 1:
                return
            pool.wait_ge(a_D[B.s], B.own("D", 1))
            pool.sem_inc(s_seen, 1)
            pool.tensor_tensor(sl["m5"][:].rearrange("p a b c -> p a (b c)"), sl["m1"][:].rearrange("p a b c -> p a (b c)"),
                               ident.unsqueeze(1).to_broadcast([P, 4, P]), ALU.add).then_inc(a_p1, 1)

        def state_cnt(B, g):
            return B.tile(9, g + 1)

        def chain_pe(pe, B, p, part):
            sl, g = slots[B.s], 4 * B.s + p
            cx = B.tile(8, g + 1)
            if part == 0:
                if p == 0:
                    pe.wait_ge(a_e[B.s], B.own("e", COUNTS["e"][0 if B.prompt else 1]))
                    pe.wait_ge(a_d[B.s], B.own("d", COUNTS["d"][0 if B.prompt else 1]))
                pe.wait_ge(a_s, state_cnt(B, g))
                pe.matmul(bank(6, 64), sq_(sl, "bda", p), sst[:], start=True, stop=False)
                pe.matmul(bank(6, 64), sq_(sl, "aak", p), sl["vst"][:, p], start=False, stop=True).then_inc(a_cx, 1)
            if part == 1:
                pe.wait_ge(a_xe, cx)
                pe.matmul(bank(6, 64), sq_(sl, "m5", p), xb[:], start=True, stop=True).then_inc(a_cu, 1)
            if part == 2:
                pe.wait_ge(a_ue, cx)
                pe.matmul(bank(6, 64), sq_(sl, "btok", p), ust[:], start=True, stop=False)
                pe.matmul(bank(6, 64), sq_(sl, "ktok", p), sl["vst"][:, p], start=False, stop=True)\
                    .then_inc(a_cs2, 1)
            if part == 3:
                out = bank(3 * B.s + 2)[:, p * CT:(p + 1) * CT]
                pe.wait_ge(a_sb, state_cnt(B, g))
                pe.matmul(out, sbd[:].rearrange("p a b -> p (a b)"), sl["ar"][:, p, 1], start=True, stop=False)
                pe.wait_ge(a_ub, cx)
                pe.matmul(out, ubd[:].rearrange("p a b -> p (a b)"), sl["arb"][:, p], start=False, stop=False)
                pe.matmul(out, sq_(sl, "vtok", p), sl["ark"][:, p], start=False, stop=True).then_inc(a_co, 1)

        def chain_dve(dve, B, p, part):
            sl, g = slots[B.s], 4 * B.s + p
            cx = B.tile(8, g + 1)
            if part == 0:
                if g == 0:
                    dve.wait_ge(a_co, B.cnt(4, 5))
                    dve.memset(sst[:], 0.0).then_inc(a_s, 1)
                    dve.memset(sbd[:], 0.0).then_inc(a_sb, 1)
                dve.wait_ge(a_cx, cx)
                dve.tensor_copy(xb[:], bank(6, 64)).then_inc(a_xe, 1)
            if part == 2:
                dve.wait_ge(a_cs2, cx)
                dve.wait_ge(a_sp, cx)
                dve.wait_ge(a_sb, state_cnt(B, g))
                dve.scalar_tensor_tensor(sst[:], bank(6, 64), sl["p"][:, p, CT - 1:CT], sp_[:], ALU.mult, ALU.add)\
                    .then_inc(a_s, 1)
                if p == 3:
                    dve.memset(free[:, 31:32], 0.0).then_inc(a_sst, 1)
                if g == 7:
                    dve.wait_ge(a_s, state_cnt(B, 8))
                    dve.tensor_copy(wkvo[:, bass.ds(B.i + B.off, 1)], sst[:].unsqueeze(1)).then_inc(a_ss, 1)

        def chain_act(act, B, p, part):
            sl, g = slots[B.s], 4 * B.s + p
            cx = B.tile(8, g + 1)
            if part == 0:
                act.wait_ge(a_s, state_cnt(B, g))
                act.activation(sp_[:], sst[:], ACT.Copy, scale=sl["p"][:, p, CT - 1:CT]).then_inc(a_sp, 1)
            if part == 1:
                act.wait_ge(a_cu, cx)
                act.activation(ust[:], bank(6, 64), ACT.Copy).then_inc(a_ue, 1)
            if part == 3 and p == 3:
                act.wait_ge(a_co, B.cnt(4, 9))
                act.sem_inc(s_seen, 1)
                act.activation(B.row(rkv, 0), bank(3 * B.s + 2, 256).rearrange("p (c t) -> p c t", t=CT), ACT.Copy)\
                    .then_inc(a_oe, 1)

        def chain_pool(pool, B, p, part):
            g = 4 * B.s + p
            if part == 1:
                pool.wait_ge(a_ue, B.tile(8, g + 1))
                pool.sem_inc(s_seen, 1)
                pool.tensor_tensor(ubd[:], ust[:].unsqueeze(1).to_broadcast([P, 2, 64]), two_heads, ALU.mult)\
                    .then_inc(a_ub, 1)
            if part == 3:
                pool.wait_ge(a_co, B.cnt(4, p + 6))
                pool.sem_inc(s_seen if g < 7 else a_sb, 1)
                if g < 7:
                    pool.wait_ge(a_s, state_cnt(B, g + 1))
                    pool.sem_inc(s_seen, 1)
                    pool.tensor_tensor(sbd[:], sst[:].unsqueeze(1).to_broadcast([P, 2, 64]), two_heads, ALU.mult)\
                        .then_inc(a_sb, 1)

        PREP_AT = {1: (0,), 2: (1,), 4: (2,), 5: (3,), 7: (4,), 9: (5,), 10: (6,), 11: (7,), 12: (8,), 13: (9,)}

        def half(eng, inv_step, chain_part, prep_piece, inv, chain, prep, pieces=range(PIECES)):
            for k in range(18):
                inv_step(eng, inv, k)
                if chain and 2 <= k <= 13:
                    for q in range((k - 2) * 4 // 3, (k - 1) * 4 // 3):
                        chain_part(eng, chain, q // 4, q % 4)
                if prep:
                    for piece in PREP_AT.get(k, ()):
                        if piece in pieces:
                            prep_piece(eng, prep, piece)

        def rwkv(eng, j, inv_step, chain_part, prep_piece, seq, before_samples=None):
            fns = (inv_step, chain_part, prep_piece)
            for piece in range(PIECES):
                prep_piece(eng, Bat(j, 0, 0), piece)
            half(eng, *fns, Bat(j, 0, 0), None, Bat(j, 1, 0))
            with eng.Fori(0, KD - 1) as i:
                half(eng, *fns, Bat(j, 1, i), Bat(j, 0, i), Bat(j, 0, i, 1))
                half(eng, *fns, Bat(j, 0, i, 1), Bat(j, 1, i), Bat(j, 1, i, 1))
            s0, s1 = Bat(j, 0), Bat(j, 1)
            half(eng, *fns, Bat(j, 1, KD - 1), Bat(j, 0, KD - 1), s0)
            half(eng, *fns, s0, Bat(j, 1, KD - 1), s1, range(PIECES - 1))
            if before_samples:
                before_samples()
            seq(eng, j, s0)
            prep_piece(eng, s1, PIECES - 1)
            half(eng, *fns, s1, None, None)
            seq(eng, j, s1)

        def tile_no(B, p):
            return KD * B.j + 4 * B.b + p

        def seq_pe(pe, j, B):
            sl = slots[0]
            pe.wait_ge(a_e[B.s], B.own("e", COUNTS["e"][0 if B.prompt else 1]))
            pe.wait_ge(a_d[B.s], B.own("d", COUNTS["d"][0 if B.prompt else 1]))
            pe.wait_ge(a_out, 16 * (1 + 4 * j))
            pe.wait_ge(a_oe, B.cnt(1, 2))

            def lead(p):
                n = 4 * B.b + p
                pe.matmul(bank(3), sq_(sl, "bda", p), ss[:, n].rearrange("p a b -> p (a b)"), start=True, stop=True)\
                    .then_inc(a_q, 1)
                pe.matmul(bank(5, 64), sq_(sl, "aak", p), sl["vst"][:, p], start=True, stop=True).then_inc(a_q, 1)

            lead(0)
            for p in range(4):
                t = tile_no(B, p)
                pe.wait_ge(a_qd, 3 * t + 3)
                pe.matmul(bank(6, 64), sq_(sl, "m5", p), xb[:], start=True, stop=True).then_inc(a_qu, 1)
                if p < 3:
                    lead(p + 1)
                out = bank(2)[:, p * CT:(p + 1) * CT]
                pe.wait_ge(a_qp, 2 * t + 1)
                for q in range(NS):
                    pe.matmul(out[:, q * TS:(q + 1) * TS], sb8[:, t % 2, q].rearrange("p a b -> p (a b)"),
                              sl["ar"][:, p, 1, q * TS:(q + 1) * TS], start=(q == 0), stop=False,
                              skip_group_check=True)
                pe.wait_ge(a_qp, 2 * t + 2)
                pe.matmul(out, ubd[:].rearrange("p a b -> p (a b)"), sl["arb"][:, p], start=False, stop=False,
                          skip_group_check=True)
                pe.matmul(out, sq_(sl, "vtok", p), sl["ark"][:, p], start=False, stop=True,
                          skip_group_check=True).then_inc(a_co, 1)
                pe.wait_ge(a_qv, t + 1)
                if t:
                    pe.wait_ge(a_qe, 2 * t)
                pe.matmul(bank(4), sq_(sl, "btok", p), uq[:].rearrange("p a b -> p (a b)"), start=True, stop=False)
                pe.matmul(bank(4), sq_(sl, "ktok", p), vq[:].rearrange("p a b -> p (a b)"), start=False, stop=True)\
                    .then_inc(a_qs, 1)

        def seq_dve(dve, j, B):
            sl = slots[0]
            seqm = mview("seqm").unsqueeze(2).to_broadcast([P, NS, 64])

            def lead(p):
                t = tile_no(B, p)
                dve.wait_ge(a_q, 2 * t + 1)
                dve.tensor_tensor(xq[:], bank(3).rearrange("p (q i) -> p q i", i=64), seqm, ALU.mult).then_inc(a_qd, 1)
                dve.wait_ge(a_qd, 3 * t + 1)
                dve.tensor_reduce(xb[:], xq[:].rearrange("p q i -> p i q"), AX.X, ALU.add).then_inc(a_qd, 1)
                dve.wait_ge(a_q, 2 * t + 2)
                dve.wait_ge(a_qd, 3 * t + 2)
                dve.tensor_tensor(xb[:], xb[:], bank(5, 64), ALU.add).then_inc(a_qd, 1)

            lead(0)
            for p in range(4):
                t, n = tile_no(B, p), 4 * B.b + p
                dve.wait_ge(a_qa, t + 1)
                dve.tensor_tensor(uq[:], ust[:].unsqueeze(1).to_broadcast([P, NS, 64]), seqm, ALU.mult)
                dve.tensor_tensor(vq[:], sl["vst"][:, p].unsqueeze(1).to_broadcast([P, NS, 64]), seqm, ALU.mult)\
                    .then_inc(a_qv, 1)
                if p < 3:
                    lead(p + 1)
                dve.wait_ge(a_qs, t + 1)
                dve.tensor_tensor(ss[:, n], ss[:, n], bank(4).rearrange("p (q i) -> p q i", i=64), ALU.add)\
                    .then_inc(a_qe, 1)
                dve.wait_ge(a_qe, 2 * t + 1)
                ends = sl["p"][:, p].rearrange("p (q t) -> p q t", t=TS)[:, :, TS - 1:TS].to_broadcast([P, NS, 64])
                dve.tensor_tensor(ss[:, n], ss[:, n], ends, ALU.mult).then_inc(a_qe, 1)

        def seq_act(act, j, B):
            for p in range(4):
                t = tile_no(B, p)
                act.wait_ge(a_qu, t + 1)
                act.activation(ust[:], bank(6, 64), ACT.Copy).then_inc(a_qa, 1)
            act.wait_ge(a_co, B.cnt(4, 9))
            act.activation(B.row(rkv, 0), bank(2, 256).rearrange("p (c t) -> p c t", t=CT), ACT.Copy).then_inc(a_oe, 1)

        def seq_pool(pool, j, B):
            for p in range(4):
                t, n = tile_no(B, p), 4 * B.b + p
                pool.wait_ge(a_out, 16 * (1 + 4 * j))
                if t >= 2:
                    pool.wait_ge(a_qs, t - 1)
                pool.tensor_tensor(sb8[:, t % 2], ss[:, n].unsqueeze(2).to_broadcast([P, NS, 2, 64]),
                                   two_heads.unsqueeze(1).to_broadcast([P, NS, 2, 64]), ALU.mult).then_inc(a_qp, 1)
                pool.wait_ge(a_qa, t + 1)
                pool.tensor_tensor(ubd[:], ust[:].unsqueeze(1).to_broadcast([P, 2, 64]), two_heads, ALU.mult)\
                    .then_inc(a_qp, 1)

        def over_heads(pe, out, n, src):
            h0 = CONS["hs"][0] + 14 - 2 * n
            for a_ in range(2):
                mm = pe.matmul(pst(out, a_ * HT, (a_ + 1) * HT)[0:16], con[:, h0:h0 + 16],
                               src[:, a_ * HT:(a_ + 1) * HT], start=(n == 0), stop=(n == KD - 1))
            return mm

        def to_channels(pe, out, n, src):
            for a_ in range(2):
                mm = pe.matmul(pst(out, a_ * HT, (a_ + 1) * HT),
                               spread16[0:16, 2 * n:2 * n + 2].rearrange("p h c -> p (h c)"),
                               src[0:16, a_ * HT:(a_ + 1) * HT], start=True, stop=True)
            return mm

        mean16, rstd16 = rstd, hf

        def gn_pe(pe, j):
            g = KD * j
            pe.wait_ge(a_oe, NBAT * (j + 1) + 2)
            pe.wait_ge(a_bon, NBAT * (j + 1) + 1)
            for n in range(KD):
                mm = over_heads(pe, 3, n, rkv[:, n])
            mm.then_inc(a_g, 1)
            pe.wait_ge(a_gm, 2 * j + 1)
            pe.wait_ge(a_ge, j + 1)
            for n in range(KD + 1):
                if n < KD:
                    if n >= 2:
                        pe.wait_ge(a_gc, g + n - 1)
                    to_channels(pe, n % 2, n, mean16).then_inc(a_gb, 1)
                if n:
                    pe.wait_ge(a_gs, g + n)
                    over_heads(pe, 2, n - 1, sq[:, (n - 1) % 2]).then_inc(a_gq, 1)
            pe.wait_ge(a_gi, j + 1)
            for n in range(KD):
                if n >= 2:
                    pe.wait_ge(a_gd, 3 * (g + n - 1))
                to_channels(pe, n % 2, n, rstd16)
                for a_ in range(2):
                    mm = pe.matmul(pst(2 + n % 2, a_ * HT, (a_ + 1) * HT), lora2[:, D + n * P:D + (n + 1) * P],
                                   sg[:, a_ * HT:(a_ + 1) * HT], start=True, stop=True)
                mm.then_inc(a_gr, 1)

        def gn_act(act, j):
            g = KD * j
            act.wait_ge(a_g, j + 1)
            act.activation(mean16[0:16], pst(3)[0:16], ACT.Copy, scale=1.0 / 64).then_inc(a_gm, 1)
            for n in range(KD):
                act.wait_ge(a_gc, g + n + 1)
                if n >= 2:
                    act.wait_ge(a_gq, g + n - 1)
                act.activation(sq[:, n % 2], rkv[:, n], ACT.Square).then_inc(a_gs, 1)
            act.wait_ge(a_gq, g + KD)
            act.activation(rstd16[0:16], pst(2)[0:16], ACT.Sqrt, bias=gneps[0:16], scale=1.0 / 64).then_inc(a_gm, 1)
            for n in range(KD):
                act.wait_ge(a_gd, 3 * (g + n + 1))
                act.activation(xh[:, n], rkv[:, n], ACT.Copy).then_inc(a_gx, 1)

        def gn_dve(dve, j):
            g = KD * j
            dve.wait_ge(a_g, j + 1)
            dve.tensor_copy(spread16[0:16], ident[0:16, 0:16].unsqueeze(2).to_broadcast([16, 16, 64]))\
                .then_inc(a_ge, 1)
            for n in range(KD):
                dve.wait_ge(a_gb, g + n + 1)
                dve.tensor_tensor(rkv[:, n], rkv[:, n], pst(n % 2), ALU.subtract).then_inc(a_gc, 1)
            dve.wait_ge(a_gm, 2 * (j + 1))
            dve.reciprocal(rstd16[0:16], rstd16[0:16]).then_inc(a_gi, 1)

            def lo(n):
                dve.wait_ge(a_gx, g + n + 1)
                dve.tensor_tensor(xl[:, n], rkv[:, n], xh[:, n].bitcast(F32), ALU.subtract).then_inc(a_gl, 1)

            for n in range(KD):
                lg, lb, row = PC["lg", j] + n, PC["lb", j] + n, rkv[:, n]
                dve.wait_ge(a_gc, g + n + 1)
                dve.wait_ge(a_gr, g + n + 1)
                dve.scalar_tensor_tensor(row, row, par[:, lg:lg + 1], pst(n % 2), ALU.mult, ALU.mult)\
                    .then_inc(a_gd, 1)
                dve.wait_ge(a_gd, 3 * (g + n) + 1)
                dve.scalar_tensor_tensor(row, row, par[:, lb:lb + 1], rkv[:, KD + n], ALU.add, ALU.add)\
                    .then_inc(a_gd, 1)
                dve.wait_ge(a_gd, 3 * (g + n) + 2)
                dve.tensor_tensor(row, row, pst(2 + n % 2), ALU.mult).then_inc(a_gd, 1)
                if n:
                    lo(n - 1)
            lo(KD - 1)

        def a_pe(pe, layer, j):
            for n in range(len(MIX)):
                mix_pe(pe, layer, n)
            for n in range(2):
                last = plan[layer, MIX[-1][0]].n0 - n
                pe.wait_ge(s_ev[last % 2], turns(last) + 1)
            rwkv(pe, j, inv_pe, chain_pe, prep_pe, seq_pe)
            gn_pe(pe, j)
            res_pe(pe, plan[layer, "out"], 1, xh, xl, None, row_ready=(a_gl, KD * j + 1))

        def a_act(act, layer, j):
            a_norm_act(act, layer, j)
            mixes(act, layer, j, mix_rows_act, mix_chunk_act)

            def states_in():
                act.wait_ge(a_ss, KD * (j + 1))
                act.wait_ge(a_co, 4 * (NBAT * j + 2 * KD) + 5)
                act.dma_start(ss[:], I["wkv"][j]).then_inc(a_out, 16)

            rwkv(act, j, inv_act, chain_act, prep_act, seq_act, states_in)
            act.dma_start(O["wkvp"][j], wkvo[:]).then_inc(a_out, 16)
            act.wait_ge(a_qe, 2 * KD * (j + 1))
            act.dma_start(O["wkvs"][j], ss[:]).then_inc(a_out, 16)
            act.wait_ge(a_sh, 2 * (j + 1))
            act.dma_start(O["shift"][j], sho[:]).then_inc(a_out, 16)
            gn_act(act, j)
            act.wait_ge(a_out, 64 * (j + 1))
            res_act(act, plan[layer, "out"], 1)

        def a_dve(dve, layer, j):
            a_norm_dve(dve, layer, j)
            mixes(dve, layer, j, mix_rows_dve, mix_chunk_dve)
            dve.wait_ge(s_mm, plan[layer, MIX[-1][0]].c0 + 1)
            rwkv(dve, j, inv_dve, chain_dve, prep_dve, seq_dve)
            gn_dve(dve, j)
            res_dve(dve, plan[layer, "out"], 1)

        def a_pool(pool, layer, j):
            pool.wait_ge(s_mm, plan[layer, MIX[-1][0]].c0 + 1)
            pool.wait_ge(a_ld, 64 * (j + 1))
            rwkv(pool, j, inv_pool, chain_pool, prep_pool, seq_pool)

        def store_act(act, ph, t0, n, dst, k0, func=ACT.Copy):
            with act.Fori(0, n // 4) as i:
                for j in range(4):
                    c, m = ph.c0 + t0 + j, ph.n0 + t0 + j
                    split_hi(act, c + 2, i, 4)
                    act.wait_ge(s_mm, i * 4 + c + 1)
                    act.activation(dst[:, bass.ds(i * 4 + k0 + j, 1)], one(pst(m % 2)), func)\
                        .then_inc(s_ev[m % 2], 1)

        def plain_dve(dve, ph, t0, n):
            with dve.Fori(0, n // 4) as i:
                for j in range(4):
                    split_lo(dve, ph.c0 + t0 + j + 2, i, 4)

        def qk_act(act, layer):
            ph = plan[layer, "qk"]
            for half in range(2):
                with act.Fori(0, 2) as i:
                    def root(j):
                        r = 8 * half + j
                        act.wait_ge(b_hsm, i * 4 + r + 1)
                        act.activation(rn[:, j % 2], pst(3), ACT.Sqrt, bias=eps[:], scale=1.0 / 64)\
                            .then_inc(b_hrt, 1)

                    for j in range(4):
                        r = 8 * half + j
                        c, m = ph.c0 + r, ph.n0 + r
                        split_hi(act, c + 2, i, 4)
                        act.wait_ge(s_mm, i * 4 + c + 1)
                        act.activation(qk[:, bass.ds(i * 4 + r, 1)], one(pst(m % 2)), ACT.Copy)\
                            .then_inc(s_ev[m % 2], 1)
                        act.wait_ge(b_hn, i * 4 + r + 1)
                        act.wait_ge(s_ev[m % 2], i * 2 + turns(m) + 1)
                        act.sem_inc(s_seen, 1)
                        act.activation(one(qn[:, j % 2]), qk[:, bass.ds(i * 4 + r, 1)], ACT.Square)\
                            .then_inc(b_hsq, 1)
                        if j:
                            root(j - 1)
                    root(3)

        def qk_dve(dve, layer):
            ph = plan[layer, "qk"]
            for half in range(2):
                g = qg8[:] if half == 0 else par[:, PC["kg", 0]:PC["kg", 0] + 1]
                with dve.Fori(0, 2) as i:
                    def norm(j):
                        r = 8 * half + j
                        dve.wait_ge(b_hrt, i * 4 + r + 2)
                        dve.reciprocal(rn[:, j % 2], rn[:, j % 2]).then_inc(b_hrc, 1)
                        dve.wait_ge(b_hrc, i * 4 + r + 1)
                        row = qk[:, bass.ds(i * 4 + r, 1)]
                        dve.scalar_tensor_tensor(row, row, g, one(rn[:, j % 2]), ALU.mult, ALU.mult)\
                            .then_inc(b_hn, 1)

                    for j in range(4):
                        split_lo(dve, ph.c0 + 8 * half + j + 2, i, 4)
                        if j:
                            norm(j - 1)
                    norm(3)

        def qk_pe(pe, layer, r0):
            ph = plan[layer, "qk"]
            with pe.Fori(0, 4) as i:
                def heads_sum(j):
                    pe.wait_ge(b_hsq, i * 4 + j + 1)
                    pe.wait_ge(b_hrt, i * 4 + j + 1)
                    for a in range(2):
                        mm = pe.matmul(pst(3, a * HT, (a + 1) * HT), heads, qn[:, j % 2, a * HT:(a + 1) * HT],
                                       start=True, stop=True)
                    mm.then_inc(b_hsm, 1)

                for j in range(4):
                    chunk_mm(pe, ph.c0 + j, ph.n0 + j, xh, xl, i=i, cstep=4, nstep=4,
                             row_ready=(s_xl, r0 + 1) if j == 0 else None)
                    if j:
                        heads_sum(j - 1)
                heads_sum(3)

        def forget_act(act, layer):
            ph = plan[layer, "f"]
            split_hi(act, ph.c0 + 2)
            act.wait_ge(s_mm, ph.c0 + 1)
            t = qn[0:16, 0]
            act.activation(lf[0:16], pst(ph.n0 % 2)[0:16], ACT.Identity,
                           bias=par[0:16, PC["fbias", 0]:PC["fbias", 0] + 1]).then_inc(s_ev[ph.n0 % 2], 1)
            act.wait_ge(s_ev[ph.n0 % 2], turns(ph.n0) + 1)
            act.activation(t, lf[0:16], ACT.Abs).then_inc(b_f, 1)
            act.wait_ge(b_f, 1)
            act.activation(t, t, ACT.Exp, scale=-1.0).then_inc(b_f, 1)
            act.wait_ge(b_f, 2)
            act.activation(t, t, ACT.Ln, bias=1.0).then_inc(b_f, 1)
            act.wait_ge(b_ft, 5)
            act.activation(fq[:].rearrange("p a b -> p (a b)"), ps[:, 2048:2048 + 64], ACT.Copy).then_inc(b_fe, 1)
            act.dma_start(O["logf"], lf[0:16]).then_inc(b_out, 16)
            act.dma_start(O["k"], qk[:, KD:]).then_inc(b_out, 16)
            act.dma_start(O["v"], vg[:, 0:KD]).then_inc(b_out, 16)

        def forget_dve(dve, layer):
            split_lo(dve, plan[layer, "f"].c0 + 2)
            dve.memset(rn[0:16, 0], 1.0).then_inc(b_pr, 1)
            dve.wait_ge(b_f, 3)
            dve.scalar_tensor_tensor(lf[0:16], lf[0:16], 0.0, qn[0:16, 0], ALU.min, ALU.subtract).then_inc(b_pr, 1)
            dve.wait_ge(b_pr, 2)
            dve.tensor_tensor_scan(lfc[0:16, 0:TP], rn[0:16, 0, 0:TP], lf[0:16, 0:TP], 0.0, ALU.mult, ALU.add)\
                .then_inc(b_pr, 1)
            dve.wait_ge(b_ft, 5)
            dve.tensor_copy(col[0:TSN, 32:48], ps[0:TSN, 2560:2576]).then_inc(b_fe, 1)

        def forget_pe(pe, layer):
            ph = plan[layer, "f"]
            chunk_mm(pe, ph.c0, ph.n0, xh, xl)
            pe.wait_ge(b_pr, 3)
            for n in range(4):
                pe.transpose(ps[:, 2048 + 16 * n:2048 + 16 * n + 16], lfc[0:16, n * P:(n + 1) * P],
                             ident[0:16, 0:16]).then_inc(b_ft, 1)
            pe.transpose(ps[0:TSN, 2560:2576], lf[0:16, TP:T], ident[0:16, 0:16]).then_inc(b_ft, 1)

        OFF = [0, 1, 3, 6]

        def prompt_pool(pool):
            pool.wait_ge(b_fe, 2)
            with pool.Fori(0, KD) as i:
                pool.wait_ge(b_ex, i * 8 + 4)
                pool.sem_inc(s_seen, 1)
                pool.tensor_copy(one(qs[:]), qk[:, bass.ds(i, 1), 0:TP])
                pool.tensor_copy(one(ks[:]), qk[:, bass.ds(i + KD, 1), 0:TP])
                pool.wait_ge(b_vts, i + 1)
                pool.sem_inc(s_seen, 1)
                pool.tensor_copy(one(vs[:]), vg[:, bass.ds(i, 1), 0:TP]).then_inc(b_qs, 1)

        def prompt_pe(pe):
            with pe.Fori(0, KD) as i:
                pe.wait_ge(b_qs, i + 1)
                pe.wait_ge(b_vts, i + 1)
                for n in range(4):
                    mm = pe.transpose(bank(4)[:, n * P:(n + 1) * P], vs[:, n * P:(n + 1) * P], ident)
                mm.then_inc(b_vtp, 1)
                pe.wait_ge(b_fm, i + 1)
                for h in range(2):
                    for n in range(4):
                        pe.wait_ge(b_ex, i * 8 + 4 * h + n + 1)
                        nk = (n + 1) * P
                        pe.matmul(bank(n, nk), qs[64 * h:64 * h + 64, n * P:nk],
                                  ks[64 * h:64 * h + 64, 0:nk], start=True, stop=False)
                        pe.matmul(bank(n)[:, nk - P:nk], ident, con[:, CONS["neg"][0]:CONS["neg"][0] + P],
                                  start=False, stop=False)
                        pe.matmul(bank(n, nk), ones[0:16], fm[0:16, h, 0:nk], start=False, stop=True)\
                            .then_inc(b_s, 1)
                for h in range(2):
                    for n in range(4):
                        k = 4 * h + n
                        pe.wait_ge(b_nm, i * 8 + k + 1)
                        pe.wait_ge(b_pt, i * 8 + k + 1)
                        for m in range(n + 1):
                            at = (OFF[n] + m) * P
                            mm = pe.transpose(bank(5 + 2 * (k % 2))[:, m * P:(m + 1) * P], sc[:, h, at:at + P], ident)
                        mm.then_inc(b_tp, 1)
                    pe.wait_ge(b_pt, i * 8 + 4 * h + 6)
                    pe.wait_ge(b_vts, i + 2)
                    if h == 0:
                        pe.wait_ge(b_og, i + 1)
                    for n in range(4):
                        mm = pe.matmul(bank(6)[64 * h:64 * h + 64, n * P:], vts[:, n, 64 * h:64 * h + 64],
                                       pt[:, h, n, n * P:], start=(n == 0), stop=(n == 3), skip_group_check=True)
                    mm.then_inc(b_pv, 1)

        def prompt_act(act):
            with act.Fori(0, KD) as i:
                act.wait_ge(b_vtp, i + 1)
                act.wait_ge(b_pv, i * 2 + 2)
                act.activation(vts[:].rearrange("p a b -> p (a b)"), bank(4), ACT.Copy).then_inc(b_vts, 1)

                def exp(h, n):
                    k = 4 * h + n
                    act.wait_ge(b_mx, i * 8 + k + 1)
                    act.wait_ge(b_tp, i * 8 + k + 1)
                    row = sc[:, h, OFF[n] * P:(OFF[n] + n + 1) * P]
                    act.activation(row, bank(n, (n + 1) * P), ACT.Exp, bias=col[:, 16 + k:17 + k],
                                   accum_out=col[:, 8 + k:9 + k])\
                        .then_inc(b_ex, 1)

                def turn(h, n):
                    k = 4 * h + n
                    act.wait_ge(b_tp, i * 8 + k + 9)
                    act.wait_ge(b_pv, i * 2 + h + 1)
                    act.activation(pt[:, h, 0:n + 1, n * P:(n + 1) * P],
                                   bank(5 + 2 * (k % 2), (n + 1) * P).rearrange("p (a b) -> p a b", b=P),
                                   ACT.Copy).then_inc(b_pt, 1)

                for h in range(2):
                    for n in range(4):
                        exp(h, n)
                for h in range(2):
                    for n in range(4):
                        turn(h, n)

        def prompt_dve(dve):
            def head_sums(i):
                for h in range(2):
                    op = dve.tensor_scalar(fm[0:16, h], lfc[0:16, 0:TP],
                                           con[0:16, bass.ds(i * 2 + CONS["hot"][0] + h, 1)], -1.0,
                                           ALU.mult, ALU.mult)
                op.then_inc(b_fm, 1)

            head_sums(0)
            with dve.Fori(0, KD) as i:
                for h in range(2):
                    for n in range(4):
                        k = 4 * h + n
                        dve.wait_ge(b_s, i * 8 + k + 1)
                        dve.tensor_reduce(col[:, k:k + 1], bank(n, (n + 1) * P), AX.X, ALU.max, negate=True)\
                            .then_inc(b_sc, 1)
                        dve.wait_ge(b_sc, i * 8 + k + 1)
                        f = fq[:, n, bass.ds(i * 2 + h, 1)]
                        dve.scalar_tensor_tensor(col[:, 16 + k:17 + k], col[:, k:k + 1], f, f,
                                                 ALU.subtract, ALU.add).then_inc(b_mx, 1)
                for h in range(2):
                    for n in range(4):
                        k = 4 * h + n
                        row = sc[:, h, OFF[n] * P:(OFF[n] + n + 1) * P]
                        dve.wait_ge(b_ex, i * 8 + k + 5)
                        dve.reciprocal(col[:, 8 + k:9 + k], col[:, 8 + k:9 + k]).then_inc(b_rc, 1)
                        dve.wait_ge(b_rc, i * 8 + k + 1)
                        dve.tensor_scalar(row, row, col[:, 8 + k:9 + k], None, ALU.mult).then_inc(b_nm, 1)
                head_sums(i + 1)
                dve.wait_ge(b_pv, i * 2 + 4)
                dve.tensor_tensor(qk[:, bass.ds(i, 1), 0:TP], one(bank(6)), vg[:, bass.ds(i + KD, 1), 0:TP],
                                  ALU.mult).then_inc(b_og, 1)

        def attend_sp(sp, layer):
            sp.wait_ge(s_mm, plan[layer, "f"].c0 + 1)
            sp.dma_start(pgs[0:1], I["pages"]).then_inc(b_pg, 16)
            sp.wait_ge(b_pg, 16)
            npages = I["cache_v"].shape[0]
            keys = I["cache_k"].rearrange("g p k r -> g p (k r)")

            def page_of(i, p):
                return bass.ds(sp.value_load(pgs[0:1, bass.ds(i * 8 + p, 1)], min_val=0, max_val=npages - 1), 1)

            def load(dst, src, sems, used, i, pages):
                for p in pages:
                    page = page_of(i, p)
                    sp.wait_ge(used, i * 9 + (9 + p - KR + 1 if p >= KR else 9 + p - KR))
                    sp.dma_start(dst[:, bass.ds(p % KR, 1)], src[page].rearrange("o p d -> p o d"))\
                        .then_inc(sems[p % KR], 16)

            def load_keys(i, pages):
                load(kp, keys, b_kd, b_ks, i, pages)

            def load_values(i, pages):
                load(vp, I["cache_v"], b_vd, b_vs, i, pages)

            with sp.Fori(0, NS) as i:
                for p in range(8):
                    sp.dma_start(lfp[:, bass.ds(i, 1), p], I["cache_logf"][page_of(i, p)]
                                 .rearrange("o r h -> r o h")).then_inc(b_lfp, 16)
            low, high = range(KR), range(KR, 8)
            load_keys(0, low)
            load_values(0, low)
            load_keys(0, high)
            load_keys(1, low)
            with sp.Fori(0, NS - 2) as i:
                load_keys(i + 1, high)
                load_keys(i + 2, low)
                load_values(i, high)
                load_values(i + 1, low)
            load_keys(NS - 1, high)
            load_values(NS - 2, high)
            load_values(NS - 1, low)
            load_values(NS - 1, high)

        def samples_pe(pe):
            tri, m8 = (con[:, CONS[k][0]:CONS[k][0] + CONS[k][1]] for k in ("tri", "m8"))
            pe.wait_ge(b_lfp, 16 * 64)
            pe.wait_ge(b_og, KD + 1)
            flat = lfp[:].rearrange("p a b c -> p (a b c)")
            for n in range(2):
                pe.matmul(bank(n), tri, flat[:, n * 512:(n + 1) * 512], start=True, stop=True)
            for n in range(2):
                pe.matmul(bank(2 + n), ones, flat[:, n * 512:(n + 1) * 512], start=True, stop=True)
            pe.matmul(bank(4, 16)[0:TSN], m8[0:TSN], col[0:TSN, 32:48], start=True, stop=True).then_inc(b_pre, 1)
            for n in range(KD):
                mm = pe.transpose(ps[0:TSN, 6 * 512 + n * P:6 * 512 + (n + 1) * P], vg[:, n, TP:T], ident)
            mm.then_inc(b_pre, 1)
            pe.wait_ge(b_zn, 2)
            pe.matmul(bank(5, NS), zn[0:TSN].rearrange("p a b -> p (a b)"),
                      con[0:TSN, CONS["seq"][0]:CONS["seq"][0] + NS], start=True, stop=True).then_inc(b_pre, 1)
            pe.wait_ge(b_pf, 2)
            pe.wait_ge(b_f, 4)

            def scores(s, first=False):
                pe.wait_ge(b_qb, s + 1)
                pe.wait_ge(b_sex, s + 1)
                for p in range(9):
                    if p < 8:
                        pe.wait_ge(b_kd[p % KR], s * (16 * 8 // KR) + 16 * (p // KR + 1))
                    elif not first:
                        pe.wait_ge(b_ogs, s)
                    out = bank(p // 4)[:, p % 4 * P:(p % 4 + 1) * P] if p < 8 else bank(2, TSN)
                    for n in range(KD):
                        k = kp[:, p % KR, n * P:(n + 1) * P] if p < 8 else qk[:, KD + n, TP:T]
                        pe.matmul(out, qz[:, n * P:(n + 1) * P], k, start=(n == 0), stop=False)
                    if p == 0:
                        pe.wait_ge(b_st, s + 1)
                        pe.sem_inc(s_seen, 1)
                    if p < 8:
                        mm = pe.matmul(out, nf[:, p].rearrange("p h q -> p (h q)"), ident, start=False, stop=True)
                    else:
                        mm = pe.matmul(out, nfn[0:TSN].rearrange("p h q -> p (h q)"), ident[0:TSN, 0:TSN],
                                       start=False, stop=True)
                    mm.then_inc(b_ks, 1)

            def turn(s):
                pe.wait_ge(b_sex, s + 2)
                pe.wait_ge(b_pts, s * 3 + 3)
                for p in range(9):
                    if p < 8:
                        mm = pe.transpose(bank(3 + p // 4)[:, p % 4 * P:(p % 4 + 1) * P], pm[:, p], ident)
                    else:
                        mm = pe.transpose(bank(5)[0:TSN, 0:P], pm[:, p, 0:TSN], ident)
                mm.then_inc(b_ptp, 1)

            def outputs_of(s):
                pe.wait_ge(b_pts, s * 3 + 6)
                pe.wait_ge(b_pn, s + 1)
                for p in range(9):
                    if p < 8:
                        pe.wait_ge(b_vd[p % KR], s * (16 * 8 // KR) + 16 * (p // KR + 1))
                    for n in range(2):
                        rows_, v = (P, vp[:, p % KR]) if p < 8 else (TSN, vtn[0:TSN])
                        mm = pe.matmul(bank(6 + n), pts[0:rows_, p], v[:, n * 512:(n + 1) * 512],
                                       start=(p == 0), stop=(p == 8))
                    mm.then_inc(b_vs, 1)

            def gather(s):
                pe.wait_ge(b_pn, s + 2)
                for n in range(KD):
                    mm = pe.matmul(bank(2)[:, P + n * TS:P + (n + 1) * TS],
                                   om[:, 2 * n:2 * n + 2].rearrange("p h c -> p (h c)"),
                                   con[:, CONS["qm"][0]:CONS["qm"][0] + TS], start=True, stop=True)
                mm.then_inc(b_stp, 1)

            scores(0, first=True)
            turn(0)
            with pe.Fori(0, NS - 1) as i:
                scores(i + 1)
                outputs_of(i)
                turn(i + 1)
                gather(i)
            outputs_of(NS - 1)
            gather(NS - 1)

        def samples_act(act):
            act.wait_ge(b_pre, 2)
            act.activation(vtn[0:TSN], ps[0:TSN, 6 * 512:6 * 512 + D], ACT.Copy).then_inc(b_f, 1)
            with act.Fori(0, NS) as i:
                act.wait_ge(b_nb, i + 1)
                act.activation(pm[:].rearrange("p a b -> p (a b)")[:, 0:8 * P + TSN], ps[:, 0:8 * P + TSN],
                               ACT.Exp, bias=col[:, 49:50], accum_out=col[:, 50:51]).then_inc(b_sex, 1)
                act.wait_ge(b_ptp, i + 1)
                for n in range(2):
                    act.activation(pts[:, 4 * n:4 * n + 4].rearrange("p a b -> p (a b)"), bank(3 + n), ACT.Copy)\
                        .then_inc(b_pts, 1)
                act.activation(pts[0:TSN, 8], bank(5, P)[0:TSN], ACT.Copy).then_inc(b_pts, 1)
            act.wait_ge(b_ogs, NS + 1)
            for k in range(KD):
                act.activation(xh[:, k], qk[:, k], ACT.Copy).then_inc(b_oxh, 1)

        def samples_pool(pool):
            pool.wait_ge(b_pf, 2)
            with pool.Fori(0, NS) as i:
                pool.wait_ge(b_ks, i * 9 + 9)
                pool.sem_inc(s_seen, 1)
                pool.tensor_copy(nf[:].rearrange("p a h q -> p (a h) q"),
                                 lfp[:, bass.ds(i, 1)].rearrange("p o a h -> p (o a h)")
                                 .unsqueeze(2).to_broadcast([P, 8 * 16, TS])).then_inc(b_st, 1)

        def samples_dve(dve):
            def cview(k):
                return con[:, CONS[k][0]:CONS[k][0] + CONS[k][1]]

            dve.wait_ge(b_pre, 1)
            dve.memset(tot[:, :, 0], 0.0).then_inc(b_pr, 1)
            sums = ps[:, 1024:2048].rearrange("p (s g h) -> p s g h", g=8, h=16)
            for g in range(8):
                dve.wait_ge(b_pr, 4 + g)
                dst = tot[:, :, g + 1] if g < 7 else fw8[:]
                dve.tensor_tensor(dst, tot[:, :, g], sums[:, :, g], ALU.add).then_inc(b_pr, 1)
            dve.wait_ge(b_pr, 12)
            for n in range(2):
                dve.scalar_tensor_tensor(lfp[:].rearrange("p a b c -> p (a b c)")[:, n * 512:(n + 1) * 512], bank(n),
                                         -1.0, tot[:].rearrange("p a b c -> p (a b c)")[:, n * 512:(n + 1) * 512],
                                         ALU.mult, ALU.subtract).then_inc(b_pf, 1)
            pick = pts[0:TSN, 0].rearrange("p (h s) -> p h s", s=NS)
            dve.tensor_tensor(pick, fw8[0:TSN].rearrange("p s h -> p h s"),
                              cview("seq")[0:TSN].unsqueeze(1).to_broadcast([TSN, 16, NS]), ALU.mult)\
                .then_inc(b_pr, 1)
            dve.wait_ge(b_pr, 13)
            dve.tensor_reduce(fn[0:TSN], pick, AX.X, ALU.add).then_inc(b_pr, 1)
            dve.wait_ge(b_pr, 14)
            dve.tensor_tensor(fn[0:TSN], fn[0:TSN], bank(4, 16)[0:TSN], ALU.add).then_inc(b_zn, 1)
            dve.wait_ge(b_zn, 1)
            dve.tensor_tensor(zn[0:TSN], fn[0:TSN].unsqueeze(2).to_broadcast([TSN, 16, TS]),
                              cview("qm")[0:TSN].unsqueeze(1).to_broadcast([TSN, 16, TS]), ALU.mult)\
                .then_inc(b_zn, 1)
            dve.memset(qz[:], 0.0).then_inc(b_pr, 1)
            dve.wait_ge(b_pre, 3)
            dve.tensor_copy(fqn[:], bank(5, NS)).then_inc(b_pr, 1)
            dve.wait_ge(b_pr, 16)
            dve.wait_ge(b_pf, 2)

            def queries(s):
                dve.wait_ge(b_ks, s * 9 + 9)
                for h in range(2):
                    rows_ = slice(64 * h, 64 * h + 64)
                    dve.tensor_copy(qz[rows_].rearrange("p (n c) -> p n c", c=QD)[:, :, h * TS:(h + 1) * TS],
                                    qk[rows_, 0:KD, bass.ds(s * TS + TP, TS)])
                dve.tensor_tensor(nfn[0:TSN], con[0:TSN, bass.ds(s * TS + CONS["negn"][0], TS)]
                                  .unsqueeze(1).to_broadcast([TSN, 16, TS]),
                                  fn[0:TSN].unsqueeze(2).to_broadcast([TSN, 16, TS]), ALU.subtract).then_inc(b_qb, 1)

            def maxima(s):
                dve.wait_ge(b_ks, s * 9 + 18)
                dve.tensor_reduce(col[:, 48:49], ps[:, 0:8 * P + TSN], AX.X, ALU.max, negate=True)\
                    .then_inc(b_nb1, 1)
                dve.wait_ge(b_nb1, s + 1)
                dve.tensor_tensor(col[:, 48:49], col[:, 48:49], fqn[:, bass.ds(s, 1)], ALU.subtract)\
                    .then_inc(b_src, 1)
                dve.wait_ge(b_src, s * 2 + 1)
                dve.tensor_tensor(col[:, 49:50], col[:, 48:49], fqn[:, bass.ds(s, 1)], ALU.add).then_inc(b_nb, 1)

            def sums(s):
                dve.wait_ge(b_sex, s + 2)
                dve.wait_ge(b_pn, s + 1)
                dve.reciprocal(col[:, 51:52], col[:, 50:51]).then_inc(b_src, 1)

            def normed(s):
                dve.wait_ge(b_vs, s * 9 + 18)
                dve.wait_ge(b_src, s * 2 + 2)
                dve.wait_ge(b_stp, s + 1)
                dve.scalar_tensor_tensor(om[:], ps[:, 6 * 512:8 * 512].rearrange("p (h c) -> p h c", c=64),
                                         col[:, 51:52], cview("hq").unsqueeze(2).to_broadcast([P, 16, 64]),
                                         ALU.mult, ALU.mult).then_inc(b_pn, 1)

            def gated(s):
                dve.wait_ge(b_stp, s + 2)
                dve.tensor_tensor(qk[:, 0:KD, bass.ds(s * TS + TP, TS)],
                                  bank(2)[:, P:P + KD * TS].rearrange("p (n q) -> p n q", q=TS),
                                  vg[:, KD:, bass.ds(s * TS + TP, TS)], ALU.mult).then_inc(b_ogs, 1)

            queries(0)
            maxima(0)
            queries(1)
            sums(0)
            with dve.Fori(0, NS - 2) as i:
                maxima(i + 1)
                queries(i + 2)
                normed(i)
                sums(i + 1)
                gated(i)
            maxima(NS - 1)
            normed(NS - 2)
            sums(NS - 1)
            gated(NS - 2)
            normed(NS - 1)
            gated(NS - 1)
            for k in range(KD):
                dve.wait_ge(b_oxh, k + 1)
                dve.tensor_tensor(xl[:, k], qk[:, k], xh[:, k].bitcast(F32), ALU.subtract).then_inc(b_oxl, 1)

        @block.sync
        def _(sp):
            done = 0
            for layer, (kind, idx) in enumerate(mixers):
                if kind == "b":
                    weights_in(sp, done, plan[layer, "out"].c0 + SPL + RAWS)
                    done = plan[layer, "out"].c0 + SPL + RAWS
                    attend_sp(sp, layer)
            weights_in(sp, done, NCHUNK)

        @block.tensor
        def _(pe):
            pe.wait_ge(s_const, 16 * NCONST)
            for k in range(KD):
                add_squares(pe, k % 2, k + 1, start=(k == 0), stop=(k == KD - 1))
            for layer, (kind, idx) in enumerate(mixers):
                if kind == "a":
                    a_pe(pe, layer, idx)
                if kind == "b":
                    qk_pe(pe, layer, row0[layer, "mix"])
                    rows_pe(pe, plan[layer, "vg"], row0[layer, "mix"], 4)
                    forget_pe(pe, layer)
                    prompt_pe(pe)
                    samples_pe(pe)
                    res_pe(pe, plan[layer, "out"], 1, xh, xl, None, row_ready=(b_oxl, 1))
                if kind == "c":
                    rows_pe(pe, plan[layer, "in"], row0[layer, "mix"], 12)
                    res_pe(pe, plan[layer, "out"], 1, hh, hl,
                           (s_hl, conv0[layer, "in"] + KD))
                rows_pe(pe, plan[layer, "up"], row0[layer, "ffn"], 4)
                res_pe(pe, plan[layer, "down"], len(down_chunks()), hh, hl,
                       (s_hl, conv0[layer, "up"] + KF))

        def history_in(act, layer, name, src):
            if conv0[layer, name]:
                act.wait_ge(s_pad, conv0[layer, name])
            act.dma_start(cs[:, 0:src.shape[1]], src).then_inc(s_cs, 16)

        def history_out(act, layer, name, dst):
            act.wait_ge(s_cap, conv0[layer, name] + dst.shape[1])
            act.dma_start(dst, co[:, 0:dst.shape[1]]).then_inc(s_co, 16)

        @block.scalar
        def _(act):
            act.dma_start(con[:], I["consts"]).then_inc(s_const, 16)
            act.dma_start(par[:], I["params"]).then_inc(s_const, 16)
            act.dma_start(x[:], I["x"]).then_inc(s_xin, 16)
            act.wait_ge(s_xin, 16)
            split_hi(act, 0)
            split_hi(act, 1)
            for k in range(KD):
                square(act, k, k - 1)
            act.wait_ge(s_ev[0], 1)
            act.wait_ge(s_const, 16 * NCONST)
            for layer, (kind, idx) in enumerate(mixers):
                if kind in "ab" and hist_done(layer):
                    act.wait_ge(s_co, 16 * hist_done(layer))
                if kind == "a":
                    a_act(act, layer, idx)
                if kind == "b":
                    norm_act(act, n_norm[layer, "mix"], row0[layer, "mix"])
                    qk_act(act, layer)
                    store_act(act, plan[layer, "vg"], 0, 8, vg, 0)
                    store_act(act, plan[layer, "vg"], 8, 8, vg, 8, ACT.Sigmoid)
                    forget_act(act, layer)
                    prompt_act(act)
                    samples_act(act)
                    res_act(act, plan[layer, "out"], 1)
                if kind == "c":
                    history_in(act, layer, "in", I["conv_mix"])
                    norm_act(act, n_norm[layer, "mix"], row0[layer, "mix"])
                    convmix_act(act, layer)
                    history_out(act, layer, "in", O["conv_mix"])
                    res_act(act, plan[layer, "out"], 1)
                history_in(act, layer, "up", I["conv_ffn"][layer])
                norm_act(act, n_norm[layer, "ffn"], row0[layer, "ffn"])
                up_act(act, layer)
                history_out(act, layer, "up", O["conv_ffn"][layer])
                res_act(act, plan[layer, "down"], len(down_chunks()))
            last = plan[depth - 1, "down"]
            for n in range(last.n0 + KD - 2, last.n0 + KD):
                act.wait_ge(s_ev[n % 2], turns(n) + 1)
            act.dma_start(O["x"], x[:]).then_inc(s_out, 16)
            act.wait_ge(s_out, 16)
            act.wait_ge(s_co, 16 * len(hist_of))
            if ("b", 0) in mixers:
                act.wait_ge(b_out, 48)

        @block.vector
        def _(dve):
            dve.memset(gneps[:], GN_EPS)
            dve.memset(eps[:], RMS_EPS)
            for b in range(2):
                dve.memset(free[:, 2 * b:2 * b + 1], 0.0).then_inc(s_ev[b], 1)
                dve.memset(free[:, 2 * b + 1:2 * b + 2], 0.0).then_inc(s_cv, 1)
            for n, (s, by) in enumerate(((b_hn, 2), (b_hrt, 1), (b_ex, 4), (b_vts, 1), (b_tp, 8), (b_pt, 2),
                                         (b_pv, 2), (b_og, 1), (b_ks, 9), (b_pts, 3), (b_sex, 1), (b_vs, 9),
                                         (b_ogs, 1), (b_pn, 1), (b_stp, 1), (a_bon, 1), (a_bd, 1), (a_co, 5),
                                         (a_oe, 2), (a_z, 1), (a_sst, 2))):
                dve.memset(free[:, 4 + n:5 + n], 0.0).then_inc(s, by)
            dve.wait_ge(s_const, 16 * NCONST)
            dve.tensor_scalar(qg8[:], par[:, PC["qg", 0]:PC["qg", 0] + 1], 64.0 ** -0.5, None, ALU.mult)
            split_lo(dve, 0)
            split_lo(dve, 1)
            for layer, (kind, idx) in enumerate(mixers):
                if kind == "a":
                    a_dve(dve, layer, idx)
                if kind == "b":
                    norm_dve(dve, n_norm[layer, "mix"], row0[layer, "mix"], PC["gm", layer])
                    qk_dve(dve, layer)
                    plain_dve(dve, plan[layer, "vg"], 0, 16)
                    forget_dve(dve, layer)
                    prompt_dve(dve)
                    samples_dve(dve)
                    res_dve(dve, plan[layer, "out"], 1)
                if kind == "c":
                    norm_dve(dve, n_norm[layer, "mix"], row0[layer, "mix"], PC["gm", layer])
                    convmix_dve(dve, layer)
                    res_dve(dve, plan[layer, "out"], 1)
                norm_dve(dve, n_norm[layer, "ffn"], row0[layer, "ffn"], PC["gf", layer])
                up_dve(dve, layer)
                res_dve(dve, plan[layer, "down"], len(down_chunks()))

        @block.gpsimd
        def _(pool):
            for layer, (kind, idx) in enumerate(mixers):
                if kind == "a":
                    a_pool(pool, layer, idx)
                if kind == "b":
                    prompt_pool(pool)
                    samples_pool(pool)
                if kind == "c":
                    conv_pool(pool, layer, "in", row0[layer, "mix"])
                conv_pool(pool, layer, "up", row0[layer, "ffn"])


def rows(a):
    a = np.asarray(a)
    return np.ascontiguousarray(a.T.reshape(-1, P, a.shape[0]).transpose(1, 0, 2))


def unrows(a):
    return np.ascontiguousarray(a.transpose(1, 0, 2).reshape(-1, a.shape[2]).T)


def cols(v):
    return np.asarray(v).reshape(-1, P).T


def tiles(w):
    k, m = w.shape
    return np.asarray(w).reshape(k // P, P, m // P, P).transpose(2, 1, 0, 3)


def pack(a):
    w = np.zeros((sum(KINDS[k] + FFN_CHUNKS for k, _ in MIXERS), P, CH, P), np.float32)
    at = 0

    def put(*chunks):
        nonlocal at
        for c in chunks:
            w[at, :, 0:c.shape[1]] = c
            at += 1

    for layer, (kind, j) in enumerate(MIXERS):
        if kind == "a":
            for n in range(3):
                put(*tiles(a["a_w_rkv"][j, n]))
            put(*tiles(a["a_g1"][j]))
            lora = tiles(np.concatenate([a["a_w1"][j], a["a_a1"][j]], 1))
            put(*lora, *lora)
            put(*tiles(a["a_w_out"][j]))
        elif kind == "b":
            put(*tiles(a["b_w_in"][j, :, 0:4 * D]))
            put(*tiles(np.concatenate([a["b_w_in"][j, :, 4 * D:], np.zeros((D, P - 16), np.float32)], 1)))
            put(*tiles(a["b_w_out"][j]))
        else:
            t = tiles(a["c_w_in"][j])
            for n in range(KD):
                put(t[KD + n], t[2 * KD + n], t[n])
            put(*tiles(a["c_w_out"][j]))
        t = tiles(a["f_w_up"][layer])
        for n in range(KF):
            put(t[n], t[KF + n])
        t = tiles(a["f_w_down"][layer])
        for n in range(KD):
            put(*[t[n][:, k:k + nk] for k, nk in down_chunks()])
    where, npar = params()
    par = np.zeros((P, npar), np.float32)

    def put_par(name, n, v):
        v = cols(v)
        par[:, where[name, n]:where[name, n] + v.shape[1]] = v

    for layer in range(DEPTH):
        put_par("gm", layer, a["norm_mix_g"][layer])
        put_par("gf", layer, a["norm_ffn_g"][layer])
        put_par("fw", layer, a["f_conv_w"][layer])
        put_par("fb", layer, a["f_conv_b"][layer])
    for j in range(2):
        for name, v in (("mu", "a_mu"), ("w0", "a_w0"), ("a0", "a_a0"), ("kk", "a_k_k"), ("ka", "a_k_a"),
                        ("rk", "a_r_k"), ("lg", "a_lnx_g"), ("lb", "a_lnx_b")):
            put_par(name, j, a[v][j])
    put_par("cw", 0, a["c_conv_w"][0])
    for name, v in (("qg", "b_q_norm_g"), ("kg", "b_k_norm_g")):
        put_par(name, 0, np.tile(a[v][0], 2))
    par[0:16, where["fbias", 0]] = np.asarray(a["b_f_bias"][0])
    x = np.concatenate([a["x_prompt"].reshape(TP, D), a["x_sample"].reshape(TSN, D)])
    return dict(
        masks=masks(),
        lora2=np.stack([np.concatenate([np.concatenate([a["a_w2"][j], a["a_a2"][j]]), a["a_g2"][j]], 1)
                        for j in range(2)]),
        shift=np.stack([rows(v) for v in np.asarray(a["state_shift"])]),
        wkv=np.ascontiguousarray(np.asarray(a["state_wkv"]).reshape(2, NS, KD, 2, 64, 64)
                                 .transpose(0, 3, 5, 2, 1, 4).reshape(2, P, KD, NS, 64)),
        pages=np.asarray(a["page_table"]).reshape(1, -1),
        cache_k=np.ascontiguousarray(np.asarray(a["cache_k"][0]).reshape(-1, P, KD, P).transpose(0, 3, 2, 1)),
        cache_v=np.asarray(a["cache_v"][0]).reshape(-1, P, D), cache_logf=np.asarray(a["cache_logf"][0]),
        x=rows(x), w=w.reshape(-1, P, CH * P), params=par, consts=constants(),
        conv_ffn=np.stack([rows(c.reshape(2 * NS, FF)) for c in np.asarray(a["state_conv_ffn"])]),
        conv_mix=rows(np.asarray(a["state_conv_mix"]).reshape(2 * NS, D)),
    )


def constants():
    c = np.zeros((P, NCON), np.float32)
    p, f = np.arange(P)[:, None], np.arange(P)[None, :]
    tok, tok2, q = np.arange(P)[:, None], np.arange(TSN)[None, :], np.arange(TS)[None, :]
    values = dict(
        ones=np.ones((P, P)), ident=p == f,
        heads=p // 64 == f // 64,
        tri=p <= f,
        neg=np.where(f > p, NEG, 0),
        hot=p == f[:, 0:18],
        m8=(p // TS == tok2 // TS) & (p <= tok2),
        seq=p // TS == f[:, 0:NS],
        negn=np.where((p // TS == tok2 // TS) & (p % TS <= tok2 % TS), 0, NEG),
        qm=p % TS == q,
        hq=p // TS == f[:, 0:16],
        hs=p // 64 == f[:, 0:30] - 14,
    )
    for name, v in values.items():
        at, w = CONS[name]
        c[:, at:at + w] = v
    return c


def masks():
    c = np.zeros((P, NMASK), np.float32)
    h, t = np.divmod(np.arange(P), CT)
    same, before = h[:, None] == h[None, :], t[:, None] > t[None, :]
    u = np.arange(CT)[None, :]
    values = dict(ist=t[:, None] == u, seqm=t[:, None] // TS == np.arange(NS)[None, :])
    for n, block, chunk in ((0, SB, CT), (1, TS, TS)):
        near = t[:, None] // block == t[None, :] // block
        within = t[:, None] // chunk == t[None, :] // chunk
        d = same & before & near
        low = same & before & within
        values |= {f"d{n}": d, f"dt{n}": d.T, f"et{n}": (low & ~near).T, f"ak{n}": low.T,
                   f"r{n}": (t[:, None] <= u) & (t[:, None] // chunk == u // chunk),
                   f"scan{n}": np.broadcast_to(np.tile(np.arange(CT) % chunk != 0, 4), (P, 4 * CT))}
    for name, v in values.items():
        at, w = MASKS[name]
        c[:, at:at + w] = v
    return c


def outputs():
    return dict(x=((P, KD, T), "float32"), conv_ffn=((DEPTH, P, KF, 2 + 2 * NS), "float32"),
                conv_mix=((P, KD, 2 + 2 * NS), "float32"), k=((P, KD, T), "float32"), v=((P, KD, T), "float32"),
                logf=((16, T), "float32"), shift=((2, P, KD, 1 + NS), "float32"), wkvp=((2, P, KD, 64), "float32"),
                wkvs=((2, P, KD, NS, 64), "float32"))


def split_groups(a):
    return a[None, 0:TP], a[TP:T].reshape(NS, TS, -1)


def split_history(a):
    h = unrows(a)
    return h[None, 0:2], h[2:].reshape(NS, 2, -1)


def kernel(**inputs):
    import concourse.bacc as bacc
    from concourse.bass_utils import run_bass_kernel_spmd

    nc = bacc.Bacc("TRN2", target_bir_lowering=False, num_devices=1, dynamic_dma_scratch_size=1024)
    arrays = pack({k: np.asarray(v) for k, v in inputs.items()})
    ins = {k: nc.dram_tensor(f"in_{k}", a.shape, mybir.dt.from_np(a.dtype), kind="ExternalInput").ap()
           for k, a in arrays.items()}
    outs = {k: nc.dram_tensor(f"out_{k}", shape, mybir.dt.from_np(np.dtype(dt)), kind="ExternalOutput").ap()
            for k, (shape, dt) in outputs().items()}
    build_program(nc, ins, outs)
    results = run_bass_kernel_spmd(nc, [{f"in_{k}": a for k, a in arrays.items()}], core_ids=[0]).results[0]
    r = {k: results[f"out_{k}"] for k in outs}
    xp, xs = split_groups(unrows(r["x"]))
    kp, ks = split_groups(unrows(r["k"]))
    vp, vs = split_groups(unrows(r["v"]))
    fp, fs = split_groups(r["logf"].T)
    mp, ms = split_history(r["conv_mix"])
    cp, cs = zip(*(split_history(c) for c in r["conv_ffn"]))
    shift = np.stack([unrows(s) for s in r["shift"]])
    wkvp = r["wkvp"].reshape(2, 2, 64, KD, 64).transpose(0, 3, 1, 4, 2).reshape(2, 1, 2 * KD, 64, 64)
    wkvs = r["wkvs"].reshape(2, 2, 64, KD, NS, 64).transpose(0, 4, 3, 1, 5, 2).reshape(2, NS, 2 * KD, 64, 64)

    def heads(a):
        return np.ascontiguousarray(a.reshape(a.shape[:-1] + (16, 64))[None])

    return tuple(np.ascontiguousarray(o) for o in (
        xp, xs, wkvp, shift[:, 0:1], wkvs, shift[:, 1:], heads(kp), heads(vp), fp[None], heads(ks), heads(vs),
        fs[None], mp[None], ms[None], np.stack(cp), np.stack(cs)))
```
